# Optimizing a Trainium2 kernel written in Bass

```python
import jax, jax.numpy as jnp
from jax import lax
import numpy as np
import math

D_MODEL = 1024
BATCH = 1
SEQ = 256
DEPTH = 2

CHUNK = 64
N_MIXERS = 2
N_ATTN_LAYERS = (DEPTH + 1) // 2
N_REC_LAYERS = DEPTH // 2

N_HEADS = 16
HEAD_DIM = D_MODEL // N_HEADS
LEFT_CHUNKS = 8
BAND_CHUNKS = LEFT_CHUNKS + 1
BAND = BAND_CHUNKS * CHUNK
MAX_REL_DIST = 128
N_REL = 2 * MAX_REL_DIST + 1
NEG_INF = -1e30

D_RNN = D_MODEL
N_RG_BLOCKS = 8
RG_BLOCK = D_RNN // N_RG_BLOCKS
CONV_WIDTH = 4
RG_C = 8.0

D_FF = 4 * D_MODEL
RMS_EPS = 1e-6


def rmsnorm(x, g):
    xf = x.astype(jnp.float32)
    y = xf * lax.rsqrt(jnp.mean(xf * xf, axis=-1, keepdims=True) + RMS_EPS)
    return (y * g.astype(jnp.float32)).astype(x.dtype)

def chunked_band_attention(h, w_qkv, w_o, rel_table):
    B, S, _ = h.shape
    n_chunks = S // CHUNK
    qkv = jnp.einsum('bsd,de->bse', h, w_qkv).reshape(B, S, 3, N_HEADS, HEAD_DIM)
    q, k, v = qkv[:, :, 0], qkv[:, :, 1], qkv[:, :, 2]
    pad = LEFT_CHUNKS * CHUNK
    k_pad = jnp.pad(k, ((0, 0), (pad, 0), (0, 0), (0, 0)))
    v_pad = jnp.pad(v, ((0, 0), (pad, 0), (0, 0), (0, 0)))
    q_chunks = q.reshape(B, n_chunks, CHUNK, N_HEADS, HEAD_DIM).transpose(1, 0, 2, 3, 4)
    qi = jnp.arange(CHUNK)[:, None]
    kj = jnp.arange(BAND)[None, :]
    rel = qi + pad - kj
    idx = jnp.clip(rel, -MAX_REL_DIST, MAX_REL_DIST) + MAX_REL_DIST
    bias = rel_table[:, idx].astype(jnp.float32)
    scale = HEAD_DIM ** -0.5
    band_offsets = jnp.arange(BAND)

    def one_chunk(args):
        c, q_c = args
        start = c * CHUNK
        k_band = lax.dynamic_slice_in_dim(k_pad, start, BAND, axis=1)
        v_band = lax.dynamic_slice_in_dim(v_pad, start, BAND, axis=1)
        s = jnp.einsum('bqhd,bkhd->bhqk', q_c, k_band).astype(jnp.float32) * scale + bias
        key_pos = start - pad + band_offsets
        s = jnp.where(key_pos[None, None, None, :] >= 0, s, NEG_INF)
        p = jax.nn.softmax(s, axis=-1).astype(v_band.dtype)
        return jnp.einsum('bhqk,bkhd->bqhd', p, v_band)

    o = lax.map(one_chunk, (jnp.arange(n_chunks), q_chunks))
    o = o.transpose(1, 0, 2, 3, 4).reshape(B, S, D_MODEL)
    return jnp.einsum('bsd,de->bse', o, w_o)

def rglru_block(h, w_in, b_in, conv_w, conv_b, w_ga, b_ga, w_gx, b_gx, a_param, w_o, b_o):
    B, S, _ = h.shape
    u = jnp.einsum('bsd,de->bse', h, w_in) + b_in
    x_br = u[..., :D_RNN]
    y_br = jax.nn.gelu(u[..., D_RNN:], approximate=True)
    xp = jnp.pad(x_br, ((0, 0), (CONV_WIDTH - 1, 0), (0, 0)))
    xc = conv_b + xp[:, 0:S] * conv_w[0]
    for tap in range(1, CONV_WIDTH):
        xc = xc + xp[:, tap:tap + S] * conv_w[tap]
    xb = xc.reshape(B, S, N_RG_BLOCKS, RG_BLOCK)
    r = jax.nn.sigmoid(jnp.einsum('bsnc,nce->bsne', xb, w_ga) + b_ga).reshape(B, S, D_RNN)
    ig = jax.nn.sigmoid(jnp.einsum('bsnc,nce->bsne', xb, w_gx) + b_gx).reshape(B, S, D_RNN)
    log_a = -RG_C * r.astype(jnp.float32) * jax.nn.softplus(-a_param.astype(jnp.float32))
    a = jnp.exp(log_a)
    mult = jnp.sqrt(-jnp.expm1(2.0 * log_a))
    b_seq = mult * (ig * xc).astype(jnp.float32)

    def combine(left, right):
        a1, b1 = left
        a2, b2 = right
        return a1 * a2, a2 * b1 + b2

    _, hs = lax.associative_scan(combine, (a, b_seq), axis=1)
    out = hs.astype(h.dtype) * y_br
    return jnp.einsum('bse,ed->bsd', out, w_o) + b_o

def sq_relu_mlp(h, w1, w2):
    z = jax.nn.relu(jnp.einsum('bsd,df->bsf', h, w1))
    return jnp.einsum('bsf,fd->bsd', z * z, w2)

def first_inputs(seed: int = 0) -> dict:
    key = jax.random.key(seed)
    ks = jax.random.split(key, 20)
    nrm = lambda k, shape, s: jax.random.normal(k, shape, jnp.float32) * s
    x = jax.random.normal(ks[0], (BATCH, SEQ, D_MODEL), jnp.float32)
    norm_mix = 1.0 + nrm(ks[1], (DEPTH, D_MODEL), 0.05)
    norm_mlp = 1.0 + nrm(ks[2], (DEPTH, D_MODEL), 0.05)
    attn_w_qkv = nrm(ks[3], (N_ATTN_LAYERS, D_MODEL, 3 * D_MODEL), D_MODEL ** -0.5)
    attn_w_o = nrm(ks[4], (N_ATTN_LAYERS, D_MODEL, D_MODEL), D_MODEL ** -0.5)
    attn_rel_bias = nrm(ks[5], (N_ATTN_LAYERS, N_HEADS, N_REL), 0.2)
    rec_w_in = nrm(ks[6], (N_REC_LAYERS, D_MODEL, 2 * D_RNN), D_MODEL ** -0.5)
    rec_b_in = nrm(ks[7], (N_REC_LAYERS, 2 * D_RNN), 0.02)
    rec_conv_w = nrm(ks[8], (N_REC_LAYERS, CONV_WIDTH, D_RNN), CONV_WIDTH ** -0.5)
    rec_conv_b = nrm(ks[9], (N_REC_LAYERS, D_RNN), 0.02)
    rec_w_ga = nrm(ks[10], (N_REC_LAYERS, N_RG_BLOCKS, RG_BLOCK, RG_BLOCK), RG_BLOCK ** -0.5)
    rec_b_ga = nrm(ks[11], (N_REC_LAYERS, N_RG_BLOCKS, RG_BLOCK), 0.02)
    rec_w_gx = nrm(ks[12], (N_REC_LAYERS, N_RG_BLOCKS, RG_BLOCK, RG_BLOCK), RG_BLOCK ** -0.5)
    rec_b_gx = nrm(ks[13], (N_REC_LAYERS, N_RG_BLOCKS, RG_BLOCK), 0.02)
    a0 = jax.random.uniform(ks[14], (N_REC_LAYERS, D_RNN), jnp.float32, 0.81, 0.998)
    s0 = a0 ** (1.0 / RG_C)
    rec_a_param = jnp.log(s0) - jnp.log1p(-s0)
    rec_w_o = nrm(ks[15], (N_REC_LAYERS, D_RNN, D_MODEL), D_RNN ** -0.5)
    rec_b_o = nrm(ks[16], (N_REC_LAYERS, D_MODEL), 0.02)
    mlp_w1 = nrm(ks[17], (DEPTH, D_MODEL, D_FF), D_MODEL ** -0.5)
    mlp_w2 = nrm(ks[18], (DEPTH, D_FF, D_MODEL), D_FF ** -0.5)
    norm_final = 1.0 + nrm(ks[19], (D_MODEL,), 0.05)
    return {"x": x, "norm_mix": norm_mix, "norm_mlp": norm_mlp,
            "attn_w_qkv": attn_w_qkv, "attn_w_o": attn_w_o, "attn_rel_bias": attn_rel_bias,
            "rec_w_in": rec_w_in, "rec_b_in": rec_b_in, "rec_conv_w": rec_conv_w,
            "rec_conv_b": rec_conv_b, "rec_w_ga": rec_w_ga, "rec_b_ga": rec_b_ga,
            "rec_w_gx": rec_w_gx, "rec_b_gx": rec_b_gx, "rec_a_param": rec_a_param,
            "rec_w_o": rec_w_o, "rec_b_o": rec_b_o,
            "mlp_w1": mlp_w1, "mlp_w2": mlp_w2, "norm_final": norm_final}

def first_block(x, norm_mix, norm_mlp, attn_w_qkv, attn_w_o, attn_rel_bias,
              rec_w_in, rec_b_in, rec_conv_w, rec_conv_b, rec_w_ga, rec_b_ga,
              rec_w_gx, rec_b_gx, rec_a_param, rec_w_o, rec_b_o,
              mlp_w1, mlp_w2, norm_final):
    h = x
    for layer in range(DEPTH):
        hn = rmsnorm(h, norm_mix[layer])
        j = layer // N_MIXERS
        if layer % N_MIXERS == 0:
            mix = chunked_band_attention(hn, attn_w_qkv[j], attn_w_o[j], attn_rel_bias[j])
        else:
            mix = rglru_block(hn, rec_w_in[j], rec_b_in[j], rec_conv_w[j], rec_conv_b[j],
                              rec_w_ga[j], rec_b_ga[j], rec_w_gx[j], rec_b_gx[j],
                              rec_a_param[j], rec_w_o[j], rec_b_o[j])
        h = h + mix
        h = h + sq_relu_mlp(rmsnorm(h, norm_mlp[layer]), mlp_w1[layer], mlp_w2[layer])
    return rmsnorm(h, norm_final)


DEPTH_2 = 1

N_MEM = 256
EPS = 1e-6
GLA_HEADS = 4
GLA_DK = D_MODEL // (2 * GLA_HEADS)
GLA_DV = D_MODEL // GLA_HEADS
GLA_RANK = 16
GLA_GATE_NORM = 16.0
GLA_CHUNK = 64
DSA_HEADS = 8
DSA_KV_HEADS = 2
DSA_HD = D_MODEL // DSA_HEADS
IDX_HEADS = 8
IDX_DIM = 64
TOPK_MAX = 256
Q_BLOCK = 128
REL_BUCKETS = 32
REL_MAX_DIST = 128
X_HEADS = 4
X_HD = D_MODEL // X_HEADS
N_BRANCH = 3

SPLIT_SIZES = (
    GLA_HEADS * GLA_DK,
    GLA_HEADS * GLA_DK,
    GLA_HEADS * GLA_DV,
    GLA_RANK,
    GLA_HEADS * GLA_DV,
    DSA_HEADS * DSA_HD,
    DSA_KV_HEADS * DSA_HD,
    DSA_KV_HEADS * DSA_HD,
    IDX_HEADS * IDX_DIM,
    IDX_DIM,
    IDX_HEADS,
    DSA_HEADS * DSA_HD,
    X_HEADS * X_HD,
    X_HEADS * X_HD,
    N_BRANCH * D_MODEL,
)
W_IN_COLS = 11352


def rmsnorm_2(x, g):
    xf = x.astype(jnp.float32)
    y = xf * lax.rsqrt(jnp.mean(xf * xf, axis=-1, keepdims=True) + EPS)
    return (y * g.astype(jnp.float32)).astype(x.dtype)

def split_cols(u):
    offsets = np.cumsum(np.array(SPLIT_SIZES))[:-1].tolist()
    return jnp.split(u, offsets, axis=-1)

def t5_bucket(dist):
    max_exact = REL_BUCKETS // 2
    d = jnp.maximum(dist, 1).astype(jnp.float32)
    large = max_exact + (jnp.log(d / max_exact) / math.log(REL_MAX_DIST / max_exact)
                         * (REL_BUCKETS - max_exact)).astype(jnp.int32)
    large = jnp.minimum(large, REL_BUCKETS - 1)
    return jnp.where(dist < max_exact, dist, large)

def gla_mixer(q, k, v, a_low, z, w_a_up, b_a, g_head):
    B, L, _ = q.shape
    H, dk, dv, C = GLA_HEADS, GLA_DK, GLA_DV, GLA_CHUNK
    nc = L // C
    q = q.reshape(B, nc, C, H, dk) * (dk ** -0.5)
    k = k.reshape(B, nc, C, H, dk)
    v = v.reshape(B, nc, C, H, dv)
    log_a = jax.nn.log_sigmoid((a_low @ w_a_up + b_a).astype(jnp.float32)) / GLA_GATE_NORM
    b = jnp.cumsum(log_a.reshape(B, nc, C, H, dk), axis=2)
    b_last = b[:, :, -1:]
    q_d = q * jnp.exp(b).astype(q.dtype)
    k_d = k * jnp.exp(-b).astype(k.dtype)
    k_t = k * jnp.exp(b_last - b).astype(k.dtype)
    decay = jnp.exp(b_last[:, :, 0]).astype(q.dtype)
    causal = jnp.tril(jnp.ones((C, C), dtype=bool))
    att = jnp.einsum('bnthd,bnshd->bnhts', q_d, k_d)
    att = jnp.where(causal, att, jnp.zeros_like(att))
    o_intra = jnp.einsum('bnhts,bnshv->bnthv', att, v)

    def step(state, inp):
        qc, kc, vc, dc = inp
        o = jnp.einsum('bthd,bhdv->bthv', qc, state)
        state = dc[..., None] * state + jnp.einsum('bthd,bthv->bhdv', kc, vc)
        return state, o

    s0 = jnp.zeros((B, H, dk, dv), q.dtype)
    xs = (q_d.transpose(1, 0, 2, 3, 4), k_t.transpose(1, 0, 2, 3, 4),
          v.transpose(1, 0, 2, 3, 4), decay.transpose(1, 0, 2, 3))
    _, o_inter = lax.scan(step, s0, xs)
    o = o_intra + o_inter.transpose(1, 0, 2, 3, 4)
    o = rmsnorm_2(o.reshape(B, L, H, dv), g_head)
    return o.reshape(B, L, H * dv) * jax.nn.silu(z)

def dsa_mixer(q, k, v, iq, ik, iw, z, rel_bias):
    B, L, _ = q.shape
    topk = min(TOPK_MAX, L // 4)
    nb = L // Q_BLOCK
    KV = DSA_KV_HEADS
    G = DSA_HEADS // KV
    q = q.reshape(B, nb, Q_BLOCK, KV, G, DSA_HD) * (DSA_HD ** -0.5)
    k = k.reshape(B, L, KV, DSA_HD)
    v = v.reshape(B, L, KV, DSA_HD)
    iq = iq.reshape(B, nb, Q_BLOCK, IDX_HEADS, IDX_DIM)
    iw = iw.reshape(B, nb, Q_BLOCK, IDX_HEADS) * (IDX_HEADS ** -0.5) * (IDX_DIM ** -0.5)
    ik_f = ik.astype(jnp.float32)
    key_pos = jnp.arange(L, dtype=jnp.int32)

    def block(inp):
        qb, iqb, iwb, start = inp
        q_pos = start + jnp.arange(Q_BLOCK, dtype=jnp.int32)
        s = jax.nn.relu(jnp.einsum('bqhd,bsd->bqhs', iqb.astype(jnp.float32), ik_f))
        score = jnp.einsum('bqhs,bqh->bqs', s, iwb.astype(jnp.float32))
        visible = key_pos[None, :] <= q_pos[:, None]
        score = jnp.where(visible[None], score, -jnp.inf)
        _, idx = lax.top_k(score, topk)
        valid = idx <= q_pos[None, :, None]
        k_sel = jax.vmap(lambda kb, ib: kb[ib])(k, idx)
        v_sel = jax.vmap(lambda vb, ib: vb[ib])(v, idx)
        logits = jnp.einsum('bqcgd,bqncd->bqcgn', qb, k_sel).astype(jnp.float32)
        bucket = t5_bucket(jnp.maximum(q_pos[None, :, None] - idx, 0))
        bias = rel_bias[bucket].reshape(B, Q_BLOCK, topk, KV, G).transpose(0, 1, 3, 4, 2)
        logits = logits + bias.astype(jnp.float32)
        logits = jnp.where(valid[:, :, None, None, :], logits, -1e30)
        p = jax.nn.softmax(logits, axis=-1).astype(v.dtype)
        o = jnp.einsum('bqcgn,bqncd->bqcgd', p, v_sel)
        return o.reshape(B, Q_BLOCK, DSA_HEADS * DSA_HD)

    starts = jnp.arange(nb, dtype=jnp.int32) * Q_BLOCK
    xs = (q.transpose(1, 0, 2, 3, 4, 5), iq.transpose(1, 0, 2, 3, 4),
          iw.transpose(1, 0, 2, 3), starts)
    o = lax.map(block, xs)
    o = o.transpose(1, 0, 2, 3).reshape(B, L, DSA_HEADS * DSA_HD)
    return o * jax.nn.silu(z)

def cross_mixer(q, z, mem_n, w_mem_kv):
    B, L, _ = q.shape
    M = mem_n.shape[1]
    mk, mv = jnp.split(mem_n @ w_mem_kv, 2, axis=-1)
    mk = mk.reshape(B, M, X_HEADS, X_HD)
    mv = mv.reshape(B, M, X_HEADS, X_HD)
    q = q.reshape(B, L, X_HEADS, X_HD) * (X_HD ** -0.5)
    logits = jnp.einsum('bthd,bmhd->bhtm', q, mk).astype(jnp.float32)
    p = jax.nn.softmax(logits, axis=-1).astype(mv.dtype)
    o = jnp.einsum('bhtm,bmhd->bthd', p, mv).reshape(B, L, X_HEADS * X_HD)
    return o * jax.nn.silu(z)

def second_inputs(seed: int = 0) -> dict:
    key = jax.random.key(seed)
    ks = jax.random.split(key, 16)
    D = D_MODEL

    def w(k, shape, fan_in):
        return jax.random.normal(k, shape, jnp.float32) * (fan_in ** -0.5)

    def gain(k, shape):
        return 1.0 + 0.05 * jax.random.normal(k, shape, jnp.float32)

    return {
        "x": jax.random.normal(ks[0], (BATCH, SEQ, D), jnp.float32),
        "mem": jax.random.normal(ks[1], (BATCH, N_MEM, D), jnp.float32),
        "g_pre": gain(ks[2], (DEPTH_2, D)),
        "g_post": gain(ks[3], (DEPTH_2, D)),
        "g_mem": gain(ks[4], (DEPTH_2, D)),
        "w_in": w(ks[5], (DEPTH_2, D, W_IN_COLS), D),
        "w_gla_a_up": w(ks[6], (DEPTH_2, GLA_RANK, GLA_HEADS * GLA_DK), GLA_RANK),
        "b_gla_a": 0.1 * jax.random.normal(ks[7], (DEPTH_2, GLA_HEADS * GLA_DK), jnp.float32),
        "g_gla": gain(ks[8], (DEPTH_2, GLA_DV)),
        "rel_bias": 0.5 * jax.random.normal(ks[9], (REL_BUCKETS, DSA_HEADS), jnp.float32),
        "w_mem_kv": w(ks[10], (DEPTH_2, D, 2 * X_HEADS * X_HD), D),
        "w_gla_out": w(ks[11], (DEPTH_2, GLA_HEADS * GLA_DV, D), GLA_HEADS * GLA_DV),
        "w_dsa_out": w(ks[12], (DEPTH_2, DSA_HEADS * DSA_HD, D), DSA_HEADS * DSA_HD),
        "w_x_out": w(ks[13], (DEPTH_2, X_HEADS * X_HD, D), X_HEADS * X_HD),
        "w_o": w(ks[14], (DEPTH_2, D, D), D),
    }

def second_block(x, mem, g_pre, g_post, g_mem, w_in, w_gla_a_up, b_gla_a, g_gla,
              rel_bias, w_mem_kv, w_gla_out, w_dsa_out, w_x_out, w_o):
    for i in range(DEPTH_2):
        h = rmsnorm_2(x, g_pre[i])
        (gq, gk, gv, ga, gz, dq, dk, dv, iq, ik, iw, dz, xq, xz, gates) = split_cols(h @ w_in[i])
        y_gla = gla_mixer(gq, gk, gv, ga, gz, w_gla_a_up[i], b_gla_a[i], g_gla[i])
        y_dsa = dsa_mixer(dq, dk, dv, iq, ik, iw, dz, rel_bias)
        y_mem = cross_mixer(xq, xz, rmsnorm_2(mem, g_mem[i]), w_mem_kv[i])
        s_gla, s_dsa, s_mem = jnp.split(jax.nn.sigmoid(gates), N_BRANCH, axis=-1)
        merged = (s_gla * (y_gla @ w_gla_out[i]) + s_dsa * (y_dsa @ w_dsa_out[i])
                  + s_mem * (y_mem @ w_x_out[i]))
        x = x + rmsnorm_2(merged @ w_o[i], g_post[i])
    return x


def setup_inputs(seed=0):
    out = dict(first_inputs(seed))
    for name, value in second_inputs(seed + 1).items():
        if name != "x":
            out[name + "_2"] = value
    return out


def reference(
    x, norm_mix, norm_mlp, attn_w_qkv, attn_w_o, attn_rel_bias, rec_w_in, rec_b_in, rec_conv_w,
    rec_conv_b, rec_w_ga, rec_b_ga, rec_w_gx, rec_b_gx, rec_a_param, rec_w_o, rec_b_o, mlp_w1,
    mlp_w2, norm_final, mem_2, g_pre_2, g_post_2, g_mem_2, w_in_2, w_gla_a_up_2, b_gla_a_2,
    g_gla_2, rel_bias_2, w_mem_kv_2, w_gla_out_2, w_dsa_out_2, w_x_out_2, w_o_2,
):
    x = first_block(
        x, norm_mix, norm_mlp, attn_w_qkv, attn_w_o, attn_rel_bias, rec_w_in, rec_b_in,
        rec_conv_w, rec_conv_b, rec_w_ga, rec_b_ga, rec_w_gx, rec_b_gx, rec_a_param, rec_w_o,
        rec_b_o, mlp_w1, mlp_w2, norm_final,
    )
    return second_block(
        x, mem_2, g_pre_2, g_post_2, g_mem_2, w_in_2, w_gla_a_up_2, b_gla_a_2, g_gla_2,
        rel_bias_2, w_mem_kv_2, w_gla_out_2, w_dsa_out_2, w_x_out_2, w_o_2,
    )


_drawn_inputs = setup_inputs


def setup_inputs(seed=0):
    import zlib

    import numpy as np

    out = dict(_drawn_inputs(seed))
    spreads = {}
    factors = {'rec_b_ga': 21.372,
     'rec_b_gx': 5.686,
     'g_mem_2': 8.0,
     'b_gla_a_2': 8.0,
     'g_gla_2': 8.0,
     'rel_bias_2': 6.223}
    for name, (base, spread) in spreads.items():
        noise = np.random.default_rng([zlib.crc32(name.encode()), seed]).standard_normal(out[name].shape)
        drawn = base * np.exp(spread * noise) if base else spread * noise
        out[name] = __import__('jax').numpy.asarray(drawn.astype(out[name].dtype))
    for name, factor in factors.items():
        out[name] = (out[name] * factor).astype(out[name].dtype)
    return out
```

```python
from contextlib import ExitStack
from math import log

import numpy as np

import concourse.bass as bass
from concourse import mybir

P = 128
S = 256
D = 1024
NC = D // P
F32 = mybir.dt.float32
F32R = mybir.dt.float32r
ALU = mybir.AluOpType
ACT = mybir.ActivationFunctionType
AX = mybir.AxisListType.X

RAW, HIS = 5, 3
TILE = 2048
NEG = -1e30
GONE = -3e38
TAKEN = -3.4e38

VEC = [("norm_mix", 16), ("norm_mlp", 16), ("norm_final", 8), ("rec_b_in", 16), ("rec_conv_w", 32),
       ("rec_conv_b", 8), ("rec_b_ga", 8), ("rec_b_gx", 8), ("rec_a_param", 8), ("rec_b_o", 8),
       ("g_pre_2", 8), ("g_post_2", 8), ("g_mem_2", 8), ("b_gla_a_2", 4), ("g_gla_2", 2)]
VCOL = {}
for _name, _n in VEC:
    VCOL[_name] = sum(n for _, n in VEC[:len(VCOL)])
NV = sum(n for _, n in VEC)



def mlp_plan(n):
    out = [(f"w1_{n}", 0)]
    for i in range(1, 16):
        out += [(f"w1_{n}", i), (f"w2_{n}", i - 1)]
    return out + [(f"w2_{n}", 15)]


def plan():
    out = [("wv", i) for i in range(4)] + [("wk", i) for i in range(4)] + [("wq", 0)]
    for i in range(4):
        out += ([("wq", i + 1)] if i < 3 else []) + ([("wo", i - 1)] if i > 0 else [])
    out += [("wo", 3)]
    out += mlp_plan(0)
    out += [("rin", i) for i in range(8)] + [("rout", i) for i in range(4)]
    out += mlp_plan(1)
    out += [("misc", 0), ("iq", 0), ("iq", 1), ("dk", 0), ("dv", 0)] + [("dq", i) for i in range(4)]
    out += [("gq", 0), ("gq", 1), ("gk", 0), ("gk", 1)] + [("gv", i) for i in range(4)]
    out += [("dz", i) for i in range(4)]
    for i in range(4):
        out += [("ta", i), ("wd", i)]
    out += [("xq", i) for i in range(4)] + [("gz", i) for i in range(4)]
    for i in range(4):
        out += [("tg", i), ("wg", i)]
    out += [("mk", i) for i in range(4)] + [("mv", i) for i in range(4)] + [("xz", i) for i in range(4)]
    for i in range(4):
        out += [("tx", i), ("wx", i)]
    out += [("wf", i) for i in range(4)]
    return out


PLAN = plan()


class Count:

    def __init__(self, sem):
        self.sem, self.n = sem, 0


def build(nc, A, out):
    ctx = ExitStack()
    PE, ACTE, DVE, POOL, SP = nc.tensor, nc.scalar, nc.vector, nc.gpsimd, nc.sync

    def sem(name):
        return Count(ctx.enter_context(nc.semaphore(name)))

    c_hi, c_lo, c_w = sem("hi"), sem("lo"), sem("wdone")
    c_pe, c_act, c_dve, c_pool = sem("pe"), sem("act"), sem("dve"), sem("pool")
    c_raw = [sem(f"raw{i}") for i in range(RAW)]
    c_in = sem("inputs")
    c_tab, c_toep, c_out = sem("tab"), sem("toep"), sem("out")
    c_gw, c_dup = sem("gatew"), sem("dup")

    waited = {}

    def wait(eng, *toks):
        for tok in toks:
            if tok is None:
                continue
            c, n = tok
            if waited.get((id(eng), id(c)), 0) < n:
                waited[(id(eng), id(c))] = n
                eng.wait_ge(c.sem, n)

    def inc(ins, c, k=1):
        c.n += k
        ins.then_inc(c.sem, k)
        return (c, c.n)

    def act(o, i, f, after=(), **k):
        wait(ACTE, *after)
        return inc(ACTE.activation(o, i, f, **k), c_act)

    def dve(op, *a, after=(), **k):
        wait(DVE, *after)
        return inc(op(*a, **k), c_dve)

    def pool(op, *a, after=(), **k):
        wait(POOL, *after)
        return inc(op(*a, **k), c_pool)

    def last_pe(ins):
        return inc(ins, c_pe)

    base = (nc.sbuf_base + 63) // 64 * 64
    top = [base]

    def region(n):
        at = top[0]
        top[0] += n
        assert top[0] <= nc.sbuf_usable_end, top[0]
        return at

    def place(name, off, free, dt=F32):
        return nc.alloc_sbuf_tensor_at(name, [P] + list(free), dt, offset=off)

    o_raw = region(RAW * 4 * TILE)
    o_hi = region(HIS * 4 * TILE)
    o_slot = [region(8192) for _ in range(15)]
    raw = [place(f"raw_{i}", o_raw + i * 8192, [TILE]) for i in range(RAW)]
    lo = [place(f"lo_{i}", o_raw + i * 8192, [TILE], F32R) for i in range(RAW)]
    hi = [place(f"hi_{i}", o_hi + i * 8192, [TILE], F32R) for i in range(HIS)]

    def slot(name, i, free=(NC, S), dt=F32, off=0):
        return place(name, o_slot[i] + off, free, dt)

    def small(name, free, dt=F32):
        n = 4
        for f in free:
            n *= f
        return place(name, region((n + 31) // 32 * 32), free, dt)

    vec = small("vec", [NV])
    ones = small("ones", [P])
    ident = small("ident", [P])
    flip = small("flip", [P])
    gmask = small("gmask", [P])
    reset = small("reset", [S])
    sq = [small(f"sq{i}", [S]) for i in range(3)]
    rms_t = small("rms_t", [S])
    rstd = small("rstd", [S])
    L = [small(f"L{i}", [512]) for i in range(2)]
    PT = [small(f"PT{i}", [512]) for i in range(2)]
    stat = small("stat", [16, 8])
    o_tmp = region(5 * 1024)
    tmp = [place(f"tmp{i}", o_tmp + 1024 * i, [S]) for i in range(5)]
    epsc = small("epsc", [1])

    bank = [ctx.enter_context(nc.psum_tensor(f"bank{i}", [P, 512], F32)) for i in range(8)]

    def gain(name, j):
        return vec[:, VCOL[name] + j:VCOL[name] + j + 1]

    issued, cut, used = [0], [0], [0]
    hi_tok, lo_tok, raw_tok, w_tok = {}, {}, {}, {}

    def issue_dma(u):
        name, i = PLAN[u]
        if u >= RAW:
            wait(SP, w_tok[u - RAW])
        raw_tok[u] = inc(SP.dma_start(raw[u % RAW][:, :], A[name][i]), c_raw[u % RAW], 16)

    def split(u):
        if u >= HIS:
            wait(ACTE, w_tok[u - HIS])
        wait(ACTE, raw_tok[u])
        r, h, l = raw[u % RAW], hi[u % HIS], lo[u % RAW]
        hi_tok[u] = inc(ACTE.activation(h[:, :], r[:, :], ACT.Copy), c_hi)
        wait(DVE, hi_tok[u])
        lo_tok[u] = inc(DVE.tensor_tensor(l[:, :], r[:, :], h[:, :].bitcast(F32), ALU.subtract), c_lo)

    def advance():
        t = used[0]
        while cut[0] < min(t + HIS, len(PLAN)):
            split(cut[0])
            cut[0] += 1
        while issued[0] < min(t + RAW, len(PLAN)):
            issue_dma(issued[0])
            issued[0] += 1

    def take(name, i):
        t = used[0]
        assert PLAN[t] == (name, i), (PLAN[t], name, i)
        advance()
        wait(PE, lo_tok[t])
        return hi[t % HIS], lo[t % RAW]

    def give(ins):
        w_tok[used[0]] = inc(ins, c_w)
        used[0] += 1
        return w_tok[used[0] - 1]

    def mm3(o, ah, al, bh, bl, start, stop, skip=False):
        PE.matmul(o, ah, bh, start=start, stop=False, skip_group_check=skip)
        PE.matmul(o, ah, bl, start=False, stop=False, skip_group_check=skip)
        return PE.matmul(o, al, bh, start=False, stop=stop, skip_group_check=skip)

    free = [None] * 8

    def cols(name, i, x, banks, evac):
        wh, wl = take(name, i)
        xh, xl = x
        for j in range(2):
            b = banks[j]
            wait(PE, free[b])
            for k in range(NC):
                c = k * 256 + j * 128
                m = mm3(bank[b][:, 0:S], wh[:, c:c + P], wl[:, c:c + P], xh[:, k, :], xl[:, k, :], k == 0, k == NC - 1)
            if j == 0:
                t = last_pe(m)
            else:
                t = give(m)
            free[b] = evac(2 * i + j, bank[b][:, 0:S], t)

    def toks(name, i, x, banks, evac):
        wh, wl = take(name, i)
        xh, xl = x
        for j in range(2):
            b = banks[j]
            wait(PE, free[b])
            for k in range(NC):
                m = mm3(bank[b][:, 0:S], xh[:, k, j * P:(j + 1) * P], xl[:, k, j * P:(j + 1) * P],
                        wh[:, k * 256:(k + 1) * 256], wl[:, k * 256:(k + 1) * 256], k == 0, k == NC - 1)
            t = last_pe(m) if j == 0 else give(m)
            free[b] = evac(i, j, bank[b][:, 0:S], t)

    def rows(name, i, n, xh, xl):
        wh, wl = take(name, i)
        done = []
        for j in range(NC):
            b = j // 2
            if i == 0:
                wait(PE, free[b])
            for k in range(2):
                c = k * 1024 + j * 128
                m = mm3(bank[b][:, (j % 2) * S:(j % 2 + 1) * S], wh[:, c:c + P], wl[:, c:c + P], xh[:, k, :], xl[:, k, :],
                        i == 0 and k == 0 and j % 2 == 0, i == n - 1 and k == 1, skip=True)
            if i == n - 1 and j % 2:
                done.append(last_pe(m) if j < NC - 1 else give(m))
        if i < n - 1:
            give(m)
        return done

    def load(dst, src):
        return inc(SP.dma_start(dst, src), c_in, 16)

    h = slot("h", 0)
    t_eps = dve(DVE.memset, epsc[:, :], 1e-6)
    t_h = inc(SP.dma_start(h[:, :, :], A["xT"]), c_gw, 16)
    issue_dma(0)
    issued[0] = 1
    load(vec[:, :], A["vec"])
    load(ones[:, :], A["ones"])
    load(ident[:, :], A["ident"])
    load(flip[:, :], A["flip"])
    relT = slot("relT", 12, [2, 16])
    selA = slot("selA", 12, [2, 384], off=256)
    selB = slot("selB", 13, [384])
    relB = slot("relB", 13, [8], off=2048)
    load(relT[:, :, :], A["relT"])
    load(selA[:, :, :], A["selA"])
    load(selB[0:32, :], A["selB"])
    load(relB[0:32, :], A["rel_bias_2"])
    load(gmask[:, :], A["gmask"])
    t_in = load(reset[:, :], A["reset"])
    while issued[0] < RAW - 1:
        issue_dma(issued[0])
        issued[0] += 1

    def pick(j):
        return sq[j % 3]

    sq_free = [None] * 3

    def norm(src, names, x, add=None, after=(), eps_after=None):
        t_src = []
        for j in range(NC):
            t = None
            if add is not None:
                done, bias = add
                i1 = bank[j // 2][:, (j % 2) * S:(j % 2 + 1) * S]
                if bias is None:
                    t = dve(DVE.tensor_tensor, src[:, j, :], i1, src[:, j, :], ALU.add, after=[done[j // 2]])
                else:
                    t = dve(DVE.scalar_tensor_tensor, out=src[:, j, :], in0=i1, scalar=gain(bias, j),
                            in1=src[:, j, :], op0=ALU.add, op1=ALU.add, after=[done[j // 2]])
                free[j // 2] = t
            t_src.append(t)
            s = pick(j)
            t = act(s[:, :], src[:, j, :], ACT.Square, after=[t, sq_free[j % 3], *after])
            wait(PE, t, free[6])
            sq_free[j % 3] = last_pe(PE.matmul(bank[6][:, 0:S], ones[:, :], s[:, :], start=j == 0, stop=j == NC - 1))
        t = act(rms_t[:, :], bank[6][:, 0:S], ACT.Ln, scale=1.0 / D, bias=epsc[:, 0:1], after=[sq_free[(NC - 1) % 3], t_eps])
        free[6] = t
        t_r = act(rstd[:, :], rms_t[:, :], ACT.Exp, scale=-0.5, after=[t])
        return t_r, t_src

    def spread(src, name, g0, x, t_r, used_by):
        xh, xl = x
        t_x = None
        f = [None, None, None]
        for j in range(NC):
            v = tmp[j % 3]
            t = dve(DVE.scalar_tensor_tensor, out=v[:, :], in0=src[:, j, :], scalar=gain(name, g0 + j), in1=rstd[:, :],
                    op0=ALU.mult, op1=ALU.mult, after=[t_r, f[j % 3]])
            t1 = act(xh[:, j, :], v[:, :], ACT.Copy, after=[t, *used_by])
            t_x = dve(DVE.tensor_tensor, xl[:, j, :], v[:, :], xh[:, j, :].bitcast(F32), ALU.subtract, after=[t, t1, *used_by])
            f[j % 3] = t1
        return t_x

    x = (slot("xh", 1, dt=F32R), slot("xl", 2, dt=F32R))

    tabs = tmp[0]
    tab_dram = A["scratch"]
    wait(PE, t_in)
    PE.matmul(bank[7][0:16, 0:384], relT[:, 0, :], selA[:, 0, :], start=True, stop=False)
    t = last_pe(PE.matmul(bank[7][0:16, 0:384], relT[:, 1, :], selA[:, 1, :], start=False, stop=True))
    tabA = slot("tabA", 14, [384])
    tabB = slot("tabB", 14, [384], off=2048)
    t1 = dve(DVE.tensor_copy, tabA[0:16, :], bank[7][0:16, 0:384], after=[t])
    t = last_pe(PE.matmul(bank[6][0:8, 0:384], relB[0:32, :], selB[0:32, :], start=True, stop=True))
    t2 = dve(DVE.tensor_copy, tabB[0:8, :], bank[6][0:8, 0:384], after=[t])
    free[7], free[6] = t1, t2
    wait(ACTE, t2)
    inc(ACTE.dma_start(tab_dram[0:16, :], tabA[0:16, :]), c_tab, 16)
    t_tab = inc(ACTE.dma_start(tab_dram[16:24, :], tabB[0:8, :]), c_tab, 16)

    def toeplitz(dst, g, row, n):
        wait(ACTE, t_tab)
        t = inc(ACTE.dma_start(g, bass.AP(tab_dram.tensor, row * 384, [[1, P], [384, n], [1, 256]])), c_toep, 16)
        g2, d2 = g.rearrange("p n j -> p (n j)"), dst.rearrange("p n j -> p (n j)")
        for i in range(n // 2):
            b = 6 + i % 2
            wait(PE, t, free[b])
            t1 = last_pe(PE.matmul(bank[b][:, :], flip[:, :], g2[:, i * 512:(i + 1) * 512], start=True, stop=True))
            free[b] = dve(DVE.tensor_copy, d2[:, i * 512:(i + 1) * 512], bank[b][:, :], after=[t1])
        return free[b]

    T = place("T", o_slot[8], [16, 256])
    GT = place("GT", o_slot[10], [16, 256])
    t = toeplitz(T[:, :, :], GT[:, :, :], 0, 16)
    wait(POOL, t)
    t_T = inc(POOL.memset(T[0:64, :, 192:256], NEG), c_pool)

    wait(ACTE, t_h, t_in)
    wait(DVE, t_h, t_in)
    t_r, _ = norm(h, None, x)
    t_x = spread(h, "norm_mix", 0, x, t_r, [])
    wait(PE, t_x)

    def softmax_tail(Lb, tiles, mx, t_max, src_neg, st):
        t = t_max
        for n, (a, b) in enumerate(tiles):
            t = act(Lb[:, a:b], Lb[:, a:b], ACT.Exp, scale=-1.0, bias=st[:, n:n + 1], accum_out=st[:, 2 + n:3 + n],
                    after=[t_max])
        t = dve(DVE.reciprocal, st[:, 4:6], st[:, 2:4], after=[t])
        for n, (a, b) in enumerate(tiles):
            t2 = dve(DVE.tensor_scalar, Lb[:, a:b], Lb[:, a:b], st[:, 4 + n:5 + n], None, ALU.mult, after=[t])
        return t2

    TT = [(0, 256), (256, 384)]
    head_n = [0]
    L_free, PT_free = [None, None], [None, None]

    def scores(qT, kT, sb_):
        wait(PE, free[sb_])
        PE.matmul(bank[sb_][:, 0:256], qT[:, P:S], kT, start=True, stop=True)
        return last_pe(PE.matmul(bank[sb_][:, 256:384], qT[:, 0:P], kT[:, 0:P], start=True, stop=True, skip_group_check=True))

    def soft(t_s, sb_, bias, mask, t_b):
        n = head_n[0]
        head_n[0] += 1
        Lb, st = L[n % 2], stat[:, n % 16, :]
        if mask is None:
            for a, (o, e, c) in enumerate([(0, 256, 0), (256, 384, 128)]):
                t = dve(DVE.tensor_tensor_reduce, out=Lb[:, o:e], in0=bank[sb_][:, o:e], in1=bias[:, c:256], scale=-1.0,
                        scalar=3.4e38, op0=ALU.add, op1=ALU.min, accum_out=st[:, a:a + 1], after=[t_s, t_b, L_free[n % 2]])
            free[sb_] = t
        else:
            for a, (o, e, c) in enumerate([(0, 256, 0), (256, 384, 128)]):
                t = dve(DVE.tensor_tensor, Lb[:, o:e], bank[sb_][:, o:e], bias[:, c:256], ALU.add,
                        after=[t_s, t_b, L_free[n % 2]])
            free[sb_] = t
            for a, (o, e) in enumerate(TT):
                t = dve(DVE.tensor_tensor_reduce, out=Lb[:, o:e], in0=Lb[:, o:e], in1=mask[:, o:e], scale=-1.0,
                        scalar=3.4e38, op0=ALU.add, op1=ALU.min, accum_out=st[:, a:a + 1], after=[t])
        return n, softmax_tail(Lb, TT, None, t, None, st)

    def turn(n, t_p, pb, blocks, width):
        wait(PE, t_p, free[pb])
        for src, dst in blocks:
            m = PE.transpose(bank[pb][:, dst:dst + P], L[n % 2][:, src:src + P], ident[:, :])
        t = last_pe(m)
        L_free[n % 2] = t
        t2 = act(PT[n % 2][:, 0:width], bank[pb][:, 0:width], ACT.Copy, after=[t, PT_free[n % 2]])
        free[pb] = t2
        return t2

    CAUSAL = [(256, 0), (0, 128), (128, 256)]

    def weigh(n, t_t, o, V, lo_, hi_):
        wait(PE, t_t)
        PE.matmul(o, V[:, 0, lo_:hi_], PT[n % 2][:, 0:256], start=True, stop=False)
        t = last_pe(PE.matmul(o[:, P:S], V[:, 1, lo_:hi_], PT[n % 2][:, 256:384], start=False, stop=True))
        PT_free[n % 2] = t
        return t

    q, k = slot("q", 5), slot("k", 6)
    v = slot("v", 7, [2, D])
    oh, ol = slot("oh", 10, dt=F32R), slot("ol", 11, dt=F32R)

    def to_v(i, j, ps, t):
        return dve(DVE.tensor_copy, v[:, j, i * 256:(i + 1) * 256], ps, after=[t])

    def to_k(n, ps, t):
        return act(k[:, n, :], ps, ACT.Copy, after=[t])

    q_tok = {}

    def to_q(n, ps, t):
        q_tok[n] = act(q[:, n, :], ps, ACT.Copy, scale=0.125, after=[t])
        return q_tok[n]

    for i in range(4):
        toks("wv", i, x, (4, 5), to_v)
    for i in range(4):
        cols("wk", i, x, (4, 5), to_k)
    cols("wq", 0, x, (4, 5), to_q)
    wait(PE, free[4], free[5], (c_dve, c_dve.n))

    def pipeline(n_heads, start, middle, end, fills):
        st1, st2 = {}, {}
        for i in range(n_heads + 2):
            if i < n_heads:
                st1[i] = start(i)
            if i in fills:
                fills[i]()
            if 1 <= i <= n_heads:
                st2[i - 1] = middle(i - 1, st1[i - 1])
            if 2 <= i:
                end(i - 2, st2[i - 2])

    o_tok = {}

    def a_start(i):
        j, r = i // 2, (i % 2) * 64
        wait(PE, q_tok[j])
        t = scores(q[r:r + 64, j, :], k[r:r + 64, j, :], 4)
        return soft(t, 4, T[:, i, :], None, t_T)

    def a_middle(i, s):
        return s[0], turn(s[0], s[1], 5, CAUSAL, 384)

    def a_end(i, s):
        r = (i % 2) * 64
        if i % 2 == 0:
            wait(PE, free[7])
        t = weigh(s[0], s[1], bank[7][r:r + 64, 0:S], v, i * 64, i * 64 + 64)
        if i % 2:
            j = i // 2
            t1 = act(oh[:, j, :], bank[7][:, 0:S], ACT.Copy, after=[t])
            o_tok[j] = dve(DVE.tensor_tensor, ol[:, j, :], bank[7][:, 0:S], oh[:, j, :].bitcast(F32), ALU.subtract, after=[t1])
            free[7] = o_tok[j]

    def wo_part(i):
        wait(PE, o_tok[2 * i], o_tok[2 * i + 1])
        return rows("wo", i, 4, oh[:, 2 * i:2 * i + 2, :], ol[:, 2 * i:2 * i + 2, :])

    fills = {}
    for i in range(3):
        fills[4 * i + 1] = lambda i=i: cols("wq", i + 1, x, (6, 6), to_q)
        fills[4 * i + 7] = lambda i=i: wo_part(i)
    pipeline(16, a_start, a_middle, a_end, fills)
    done = wo_part(3)

    zf = [slot(f"zf{i}", 5, [S], off=1024 * i) for i in range(4)]
    zr = [slot(f"zr{i}", 6, [S], off=1024 * i) for i in range(4)]
    zh = [slot(f"zh{i}", 7, [2, S], F32R, off=2048 * i) for i in range(3)]
    zl = [slot(f"zl{i}", 10, [2, S], F32R, off=2048 * i) for i in range(3)]

    def mlp(layer, done, bias):
        t_r, _ = norm(h, None, x, add=(done, bias))
        t_x = spread(h, "norm_mlp", 8 * layer, x, t_r, [])
        wait(PE, t_x)
        z_tok, z_free = {}, {}

        def to_z(n, ps, t):
            i, j = n // 2, n % 2
            t1 = act(zr[n % 4][:, :], ps, ACT.Relu, after=[t, z_tok.get(i - 2)])
            t2 = act(zh[i % 3][:, j, :], zr[n % 4][:, :], ACT.Square, after=[t1, z_free.get(i - 3)])
            t3 = dve(DVE.tensor_tensor, zf[n % 4][:, :], zr[n % 4][:, :], zr[n % 4][:, :], ALU.mult, after=[t1])
            z_tok[i] = dve(DVE.tensor_tensor, zl[i % 3][:, j, :], zf[n % 4][:, :], zh[i % 3][:, j, :].bitcast(F32),
                           ALU.subtract, after=[t2, t3, z_free.get(i - 3)])
            return t1

        def down(i):
            wait(PE, z_tok[i])
            d = rows(f"w2_{layer}", i, 16, zh[i % 3], zl[i % 3])
            z_free[i] = w_tok[used[0] - 1]
            return d

        for i in range(17):
            if i < 16:
                cols(f"w1_{layer}", i, x, (4, 5), to_z)
            if i > 0:
                d = down(i - 1)
        return d

    done = mlp(0, done, None)

    t_r, _ = norm(h, None, x, add=(done, None))
    t_x = spread(h, "norm_mix", 8, x, t_r, [])
    wait(PE, t_x)
    XW = S + 3
    xbr = place("xbr", o_slot[5], [NC, XW])
    xc, rg, ig, tt, yb = slot("xc", 7), slot("rg", 8), slot("ig", 9), slot("tt", 10), slot("yb", 11)
    gw = slot("gw", 14, [2, NC, P])
    wait(ACTE, t_x)
    t_gw = inc(ACTE.dma_start(gw[:, :, :, :], A["gatew"]), c_gw, 16)
    gh, gl = slot("gh", 5, dt=F32R), slot("gl", 12, dt=F32R)
    sp_ = stat[:, 0:2, :].rearrange("p a b -> p (a b)")
    ap_ = vec[:, VCOL["rec_a_param"]:VCOL["rec_a_param"] + 8]
    z8 = tmp[3]
    t = act(z8[:, 0:8], ap_, ACT.Abs, after=[t_x])
    t1 = dve(DVE.tensor_scalar, z8[:, 8:16], ap_, -1.0, 0.0, ALU.mult, ALU.max, after=[t_x])
    t = act(z8[:, 16:24], z8[:, 0:8], ACT.Exp, scale=-1.0, after=[t])
    t = act(z8[:, 24:32], z8[:, 16:24], ACT.Ln, bias=1.0, after=[t])
    t = dve(DVE.tensor_tensor, z8[:, 32:40], z8[:, 8:16], z8[:, 24:32], ALU.add, after=[t, t1])
    t = dve(DVE.tensor_scalar, sp_[:, 0:8], z8[:, 32:40], 8.0, None, ALU.mult, after=[t])
    t_sp = dve(DVE.tensor_scalar, sp_[:, 8:16], z8[:, 32:40], -8.0, None, ALU.mult)
    t_pad = dve(DVE.memset, xbr[:, :, 0:3], 0.0)
    xc_tok = {}
    g_tok = {}

    def to_x(n, ps, t):
        t1 = act(xbr[:, n, 3:XW], ps, ACT.Identity, bias=gain("rec_b_in", n), after=[t])
        t = dve(DVE.tensor_scalar, xc[:, n, :], xbr[:, n, 0:S], gain("rec_conv_w", n), gain("rec_conv_b", n),
                ALU.mult, ALU.add, after=[t1, t_pad])
        for w in range(1, 4):
            t = dve(DVE.scalar_tensor_tensor, out=xc[:, n, :], in0=xbr[:, n, w:w + S], scalar=gain("rec_conv_w", 8 * w + n),
                    in1=xc[:, n, :], op0=ALU.mult, op1=ALU.add, after=[t])
        xc_tok[n] = t
        return t1

    def gates(n):
        wait(PE, xc_tok[n], t_gw)
        for m, (dst, name, b) in enumerate([(rg, "rec_b_ga", 6), (ig, "rec_b_gx", 7)]):
            wait(PE, free[b])
            t = last_pe(PE.matmul(bank[b][:, 0:S], gw[:, m, n, :], xc[:, n, :], start=True, stop=True))
            free[b] = act(dst[:, n, :], bank[b][:, 0:S], ACT.Sigmoid, bias=gain(name, n), after=[t])
            g_tok[n, m] = free[b]

    def to_y(n, ps, t):
        return act(yb[:, n - 8, :], ps, ACT.Gelu_apprx_tanh, bias=gain("rec_b_in", n), after=[t])

    for i in range(4):
        cols("rin", i, x, (4, 5), to_x)
        if i:
            gates(2 * i - 2)
            gates(2 * i - 1)
    for i in range(4, 8):
        cols("rin", i, x, (4, 5), to_y)
        if i == 4:
            gates(6)
            gates(7)
    t_y = free[5]
    t_a, t_t = {}, {}
    for n in range(NC):
        t_t[n] = act(tt[:, n, :], rg[:, n, :], ACT.Tanh, scale=sp_[:, n:n + 1], after=[t_sp, g_tok[n, 0]])
        t_a[n] = act(rg[:, n, :], rg[:, n, :], ACT.Exp, scale=sp_[:, 8 + n:9 + n], after=[t_t[n]])
    t_m = {}
    t_gi = {}
    for n in range(NC):
        s = tmp[n % 3]
        t = dve(DVE.tensor_tensor, s[:, :], rg[:, n, :], rg[:, n, :], ALU.mult, after=[t_a[n]])
        t_m[n] = dve(DVE.scalar_tensor_tensor, out=tt[:, n, :], in0=s[:, :], scalar=1.0, in1=tt[:, n, :], op0=ALU.add,
                     op1=ALU.mult, after=[t])
        t_gi[n] = dve(DVE.tensor_tensor, ig[:, n, :], ig[:, n, :], xc[:, n, :], ALU.mult, after=[g_tok[n, 1]])
    t_s = {}
    for n in range(NC):
        t_s[n] = act(tt[:, n, :], tt[:, n, :], ACT.Sqrt, after=[t_m[n]])
    gh_tok = {}
    for n in range(NC):
        t = dve(DVE.tensor_tensor, ig[:, n, :], tt[:, n, :], ig[:, n, :], ALU.mult, after=[t_s[n]])
        t = dve(DVE.tensor_tensor_scan, tt[:, n, :], rg[:, n, :], ig[:, n, :], 0.0, ALU.mult, ALU.add, after=[t])
        t = dve(DVE.tensor_tensor, tt[:, n, :], tt[:, n, :], yb[:, n, :], ALU.mult, after=[t, t_y])
        t1 = act(gh[:, n, :], tt[:, n, :], ACT.Copy, after=[t])
        gh_tok[n] = dve(DVE.tensor_tensor, gl[:, n, :], tt[:, n, :], gh[:, n, :].bitcast(F32), ALU.subtract, after=[t1])
    for i in range(4):
        wait(PE, gh_tok[2 * i + 1])
        done = rows("rout", i, 4, gh[:, 2 * i:2 * i + 2, :], gl[:, 2 * i:2 * i + 2, :])

    done = mlp(1, done, "rec_b_o")

    t_r, _ = norm(h, None, x, add=(done, None))
    for j in range(NC):
        t_res = dve(DVE.scalar_tensor_tensor, out=h[:, j, :], in0=h[:, j, :], scalar=gain("norm_final", j), in1=rstd[:, :],
                    op0=ALU.mult, op1=ALU.mult, after=[t_r])
    t_r, _ = norm(h, None, x, after=[t_res])
    t_x = spread(h, "g_pre_2", 0, x, t_r, [])
    wait(PE, t_x)

    merged = slot("merged", 5)
    dq = slot("dq", 6)
    iq = slot("iq", 7, [4, S])
    dk = slot("dk", 7, [2, S], off=4096)
    dv = slot("dv", 7, [2, S], off=6144)
    sz = slot("sz", 8)
    T2 = slot("T2", 9, [8, 256])
    yh, yl = slot("yh", 10, dt=F32R), slot("yl", 11, dt=F32R)
    gq, gk = slot("gq", 12, [4, S]), slot("gk", 12, [4, S], off=4096)
    gv = slot("gv", 13, [2, D])
    gb, kd = slot("gb", 14, [4, S]), slot("kd", 14, [4, S], off=4096)
    ik = slot("ik", 3, [S])
    low = slot("low", 3, [S], off=1024)
    sc = slot("sc", 3, [384], off=2048)
    wk_ = slot("wk_", 3, [384], off=3584)
    cm = slot("cm", 3, [384], off=5120)
    rl = [slot(f"rl{i}", 4, [384], off=1536 * i) for i in range(2)]
    iw = slot("iw", 4, [2, 32], off=3072)
    mx8 = slot("mx8", 4, [2, 8], off=3328)
    up = slot("up", 4, [512], off=4096)
    dec = slot("dec", 4, [4, 4], off=6144)

    wait(ACTE, t_x)
    t_T2 = toeplitz(T2[:, :, :], slot("GT2", 10, [8, 256])[:, :, :], 16, 8)
    t_cm = inc(ACTE.dma_start(cm[:, :], A["cm"]), c_dup, 16)
    t_cm = inc(ACTE.dma_start(up[0:16, :], A["w_gla_a_up_2"][0]), c_dup, 16)

    misc_tok = {}

    def to_misc(n, ps, t):
        if n == 0:
            misc_tok[0] = act(ik[:, :], ps, ACT.Copy, after=[t])
        else:
            misc_tok[1] = act(low[:, :], ps, ACT.Copy, after=[t])
        return misc_tok[n]

    iq_tok = {}

    def to_iq(n, ps, t):
        iq_tok[n] = act(iq[:, n, :], ps, ACT.Copy, after=[t])
        return iq_tok[n]

    cols("misc", 0, x, (4, 5), to_misc)
    for i in range(2):
        cols("iq", i, x, (4, 5), to_iq)
    wait(PE, misc_tok[1], free[6])
    for j in range(2):
        m = PE.transpose(bank[6][:, 32 * j:32 * j + 32], low[0:32, j * P:(j + 1) * P], ident[0:32, 0:32])
    t = last_pe(m)
    t_iw = dve(DVE.tensor_scalar, iw[:, :, :].rearrange("p a b -> p (a b)"), bank[6][:, 0:64], 8 ** -0.5, 64 ** -0.5,
               ALU.mult, ALU.mult, after=[t])
    free[6] = t_iw

    def dk_(n, ps, t):
        dk_tok[n] = act(dk[:, n, :], ps, ACT.Copy, after=[t])
        return dk_tok[n]

    dk_tok, dv_tok, dq_tok = {}, {}, {}

    def dv_(i, j, ps, t):
        dv_tok[j] = dve(DVE.tensor_copy, dv[:, j, :], ps, after=[t])
        return dv_tok[j]

    def dq_(n, ps, t):
        dq_tok[n] = act(dq[:, n, :], ps, ACT.Copy, scale=128 ** -0.5, after=[t])
        return dq_tok[n]

    t_sc = None
    rl_free = [None, None]
    for i in range(8):
        r = (i % 2) * 64
        b = 6 + i % 2
        wait(PE, iq_tok[i // 2], misc_tok[0], free[b])
        PE.matmul(bank[b][:, 0:256], iq[r:r + 64, i // 2, P:S], ik[r:r + 64, :], start=True, stop=True)
        t = last_pe(PE.matmul(bank[b][:, 256:384], iq[r:r + 64, i // 2, 0:P], ik[r:r + 64, 0:P], start=True, stop=True,
                              skip_group_check=True))
        t = act(rl[i % 2][:, :], bank[b][:, 0:384], ACT.Relu, after=[t, rl_free[i % 2]])
        free[b] = t
        for j, (a, e) in ((1, TT[0]), (0, TT[1])):
            w = iw[:, j, 16 + i:17 + i]
            if i == 0:
                t_sc = dve(DVE.tensor_scalar, sc[:, a:e], rl[0][:, a:e], w, None, ALU.mult, after=[t, t_iw])
            else:
                t_sc = dve(DVE.scalar_tensor_tensor, out=sc[:, a:e], in0=rl[i % 2][:, a:e], scalar=w, in1=sc[:, a:e],
                           op0=ALU.mult, op1=ALU.add, after=[t, t_sc])
        rl_free[i % 2] = t_sc
    t = dve(DVE.tensor_tensor, sc[:, :], sc[:, :], cm[:, :], ALU.add, after=[t_sc, t_cm])
    src = sc
    top_state = [t]

    def top8(r):
        t = top_state[0]
        src = sc if r == 0 else wk_
        ts = []
        for j, (a, e) in enumerate(TT):
            ts.append(dve(DVE.max, mx8[:, j, :], src[:, a:e], after=[t]))
        for j, (a, e) in enumerate(TT):
            t = dve(DVE.match_replace, wk_[:, a:e], mx8[:, j, :], src[:, a:e], TAKEN, after=[ts[j]])
        top_state[0] = t

    cols("dk", 0, x, (4, 5), dk_)
    top8(0)
    toks("dv", 0, x, (4, 5), dv_)
    top8(1)
    for i in range(4):
        cols("dq", i, x, (4, 5), dq_)
        top8(2 + i)

    gq_tok, gk_tok, gv_tok, gl_t = {}, {}, {}, {}

    def gq_(n, ps, t):
        gq_tok[n] = act(gq[:, n, :], ps, ACT.Copy, after=[t])
        return gq_tok[n]

    def gk_(n, ps, t):
        gk_tok[n] = act(gk[:, n, :], ps, ACT.Copy, after=[t])
        return gk_tok[n]

    def gv_(i, j, ps, t):
        gv_tok[i] = act(gv[:, j, i * 256:(i + 1) * 256], ps, ACT.Copy, after=[t])
        return gv_tok[i]

    for i in range(2):
        cols("gq", i, x, (4, 5), gq_)
        top8(6 + i)
    mask = sc
    t = dve(DVE.tensor_scalar, sc[:, :], wk_[:, :], -3.2e38, NEG, ALU.is_gt, ALU.mult, after=[top_state[0]])
    t_mask = dve(DVE.tensor_tensor, sc[:, :], sc[:, :], cm[:, :], ALU.min, after=[t])
    for i in range(2):
        cols("gk", i, x, (4, 5), gk_)
    for i in range(4):
        toks("gv", i, x, (4, 5), gv_)

    wait(PE, t_cm)
    for n in range(4):
        b = 6 + n % 2
        u, w = tmp[n % 2], tmp[2 + n % 2]
        wait(PE, free[b])
        t = last_pe(PE.matmul(bank[b][:, 0:S], up[0:16, n * P:(n + 1) * P], low[0:16, :], start=True, stop=True))
        t = act(u[:, :], bank[b][:, 0:S], ACT.Identity, bias=gain("b_gla_a_2", n), after=[t, gl_t.get(n - 2)])
        free[b] = t
        t = act(w[:, :], u[:, :], ACT.Abs, after=[t])
        t = act(w[:, :], w[:, :], ACT.Exp, scale=-1.0, after=[t])
        t = act(w[:, :], w[:, :], ACT.Ln, bias=1.0, after=[t])
        t = dve(DVE.scalar_tensor_tensor, out=u[:, :], in0=u[:, :], scalar=0.0, in1=w[:, :], op0=ALU.min, op1=ALU.subtract,
                after=[t])
        t = dve(DVE.tensor_tensor_scan, gb[:, n, :], reset[:, :], u[:, :], 0.0, ALU.mult, ALU.add, after=[t])
        gl_t[n] = t
    e_t = {}
    for n in range(4):
        ep, en = tmp[n % 2], tmp[2 + n % 2]
        t = act(ep[:, :], gb[:, n, :], ACT.Exp, scale=1.0 / 16, after=[gl_t[n], gl_t[3], e_t.get(n - 2)])
        t1 = act(en[:, :], gb[:, n, :], ACT.Exp, scale=-1.0 / 16)
        t2 = dve(DVE.tensor_copy, dec[:, n, :], ep[:, 63:S:64], after=[t])
        dve(DVE.scalar_tensor_tensor, out=gq[:, n, :], in0=gq[:, n, :], scalar=128 ** -0.5, in1=ep[:, :], op0=ALU.mult,
            op1=ALU.mult, after=[gq_tok[n]])
        t = dve(DVE.tensor_tensor, kd[:, n, :], gk[:, n, :], en[:, :], ALU.mult, after=[t1, gk_tok[n]])
        e_t[n] = dve(DVE.tensor_tensor, gk[:, n, :].rearrange("p (c t) -> p c t", c=4),
                     kd[:, n, :].rearrange("p (c t) -> p c t", c=4), dec[:, n, :].unsqueeze(2).to_broadcast([P, 4, 64]),
                     ALU.mult, after=[t, t2])

    def to_sz(n, ps, t):
        sz_tok[n] = act(sz[:, n, :], ps, ACT.Silu, after=[t, *sz_after])
        return sz_tok[n]

    sz_tok, sz_after = {}, []
    for i in range(4):
        cols("dz", i, x, (4, 5), to_sz)

    y_tok = {}

    def d_start(i):
        wait(PE, dq_tok[i], dk_tok[i // 4])
        return soft(scores(dq[:, i, :], dk[:, i // 4, :], 4), 4, T2[:, i, :], mask, t_T2)

    wait(DVE, t_mask)

    def d_end(i, s):
        wait(PE, free[7])
        c = (i // 4) * 128
        t = weigh(s[0], s[1], bank[7][:, 0:S], dv, c, c + 128)
        o = tmp[i % 2]
        t = dve(DVE.tensor_tensor, o[:, :], bank[7][:, 0:S], sz[:, i, :], ALU.mult, after=[t, sz_tok[i], y_tok.get(i - 2)])
        free[7] = t
        t1 = act(yh[:, i, :], o[:, :], ACT.Copy, after=[t])
        y_tok[i] = dve(DVE.tensor_tensor, yl[:, i, :], o[:, :], yh[:, i, :].bitcast(F32), ALU.subtract, after=[t1])

    wait(PE, dv_tok[0], dv_tok[1])
    pipeline(8, d_start, a_middle, d_end, {})
    m_tok = {}

    def branch(gname, wname, first):
        wait(PE, y_tok[7])
        g_t = {}

        def to_g(n, ps, t):
            g_t[n] = act(tmp[3 + n % 2][:, :], ps, ACT.Sigmoid, after=[t, m_tok.get(n - 2), m_tok.get(n + 6)])
            return g_t[n]

        def to_m(n, ps, t):
            if first:
                m_tok[n] = dve(DVE.tensor_tensor, merged[:, n, :], ps, tmp[3 + n % 2][:, :], ALU.mult, after=[t, g_t[n]])
                return m_tok[n]
            t = dve(DVE.tensor_tensor, tmp[n % 2][:, :], ps, tmp[3 + n % 2][:, :], ALU.mult, after=[t, g_t[n]])
            m_tok[n] = dve(DVE.tensor_tensor, merged[:, n, :], merged[:, n, :], tmp[n % 2][:, :], ALU.add, after=[t])
            return t

        for i in range(4):
            cols(gname, i, x, (4, 5), to_g)
            cols(wname, i, (yh, yl), (6, 7), to_m)

    branch("ta", "wd", True)
    dsa_done = w_tok[used[0] - 1]

    xq = slot("xq", 7)
    xq_tok = {}

    def to_xq(n, ps, t):
        xq_tok[n] = act(xq[:, n, :], ps, ACT.Copy, scale=1.0 / 16, after=[t])
        return xq_tok[n]

    for i in range(4):
        cols("xq", i, x, (4, 5), to_xq)
    sz_tok.clear()
    sz_after.append(y_tok[7])
    for i in range(4):
        cols("gz", i, x, (4, 5), to_sz)
    og = slot("og", 6)
    at = [slot(f"at{i}", 9, [2, P], off=1024 * i) for i in range(2)]
    ktT = [slot(f"ktT{i}", 9, [2, P], off=2048 + 1024 * i) for i in range(2)]
    st = [slot(f"st{i}", 9, [256], off=4096 + 1024 * i) for i in range(3)]
    wait(PE, e_t[3], gv_tok[3], (c_dve, c_dve.n))
    gdone = {}
    y_tok.clear()
    for n in range(4):
        A_, K_ = at[n % 2], ktT[n % 2]
        wait(PE, free[0])
        for j in range(2):
            m = PE.matmul(bank[0][:, j * P:(j + 1) * P], kd[:, n, j * P:(j + 1) * P], gq[:, n, j * P:(j + 1) * P],
                          start=True, stop=True, skip_group_check=True)
        t = last_pe(m)
        t_at = dve(DVE.tensor_tensor, A_[:, :, :], bank[0][:, 0:S].rearrange("p (a b) -> p a b", a=2),
                   gmask[:, :].unsqueeze(1).to_broadcast([P, 2, P]), ALU.mult, after=[t, gdone.get(n - 2)])
        free[0] = t_at
        wait(PE, free[1])
        for j in range(2):
            m = PE.transpose(bank[1][:, j * P:(j + 1) * P], gk[:, n, j * P:(j + 1) * P], ident[:, :])
        t = last_pe(m)
        t_k = act(K_[:, :, :], bank[1][:, 0:S].rearrange("p (a b) -> p a b", a=2), ACT.Copy, after=[t, gdone.get(n - 2)])
        free[1] = t_k
        wait(PE, t_k, free[2])
        wait(PE, free[3])
        for c in range(3):
            r, j = (c % 2) * 64, c // 2
            m = PE.matmul(bank[2 + c % 2][:, j * 256:j * 256 + 256], K_[r:r + 64, j, :],
                          gv[r:r + 64, j, n * 256:(n + 1) * 256], start=True, stop=True, skip_group_check=True)
        t_u = last_pe(m)
        t = dve(DVE.tensor_copy, st[0][:, :], bank[2][:, 0:256], after=[t_u, gdone.get(n - 1)])
        t = dve(DVE.scalar_tensor_tensor, out=st[1][:, :], in0=st[0][:, :], scalar=dec[:, n, 1:2], in1=bank[3][:, 0:256],
                op0=ALU.mult, op1=ALU.add, after=[t])
        free[3] = t
        t = dve(DVE.scalar_tensor_tensor, out=st[2][:, :], in0=st[1][:, :], scalar=dec[:, n, 2:3], in1=bank[2][:, 256:512],
                op0=ALU.mult, op1=ALU.add, after=[t])
        free[2] = t
        t_st = t
        wait(PE, t_at)
        for m_ in range(2):
            b = 6 + m_
            wait(PE, free[b])
            for j in range(2):
                o = bank[b][:, j * P:(j + 1) * P]
                c0 = n * 256 + m_ * P
                PE.matmul(o, gv[:, j, c0:c0 + P], A_[:, j, :], start=j == 0, stop=False, skip_group_check=True)
            wait(PE, t_st)
            for c in range(1, 4):
                m = PE.matmul(bank[b][:, c * 64:c * 64 + 64], st[c - 1][:, m_ * P:(m_ + 1) * P], gq[:, n, c * 64:c * 64 + 64],
                              start=False, stop=True, skip_group_check=True)
            t = last_pe(m)
            gdone[n] = t
            free[b] = act(og[:, 2 * n + m_, :], bank[b][:, 0:S], ACT.Copy, after=[t])
            s = sq[m_]
            t = act(s[:, :], og[:, 2 * n + m_, :], ACT.Square, after=[free[b], sq_free[m_]])
            wait(PE, t, free[4])
            sq_free[m_] = last_pe(PE.matmul(bank[4][:, 0:S], ones[:, :], s[:, :], start=m_ == 0, stop=m_ == 1))
        t = act(rms_t[:, :], bank[4][:, 0:S], ACT.Ln, scale=1.0 / 256, bias=epsc[:, 0:1], after=[sq_free[1]])
        free[4] = t
        t_r = act(rstd[:, :], rms_t[:, :], ACT.Exp, scale=-0.5, after=[t, y_tok.get(2 * n - 1)])
        for m_ in range(2):
            i = 2 * n + m_
            w = tmp[m_]
            t = dve(DVE.scalar_tensor_tensor, out=w[:, :], in0=og[:, i, :], scalar=gain("g_gla_2", m_), in1=rstd[:, :],
                    op0=ALU.mult, op1=ALU.mult, after=[t_r])
            t = dve(DVE.tensor_tensor, w[:, :], w[:, :], sz[:, i, :], ALU.mult, after=[t, sz_tok[i]])
            t1 = act(yh[:, i, :], w[:, :], ACT.Copy, after=[t, dsa_done])
            y_tok[i] = dve(DVE.tensor_tensor, yl[:, i, :], w[:, :], yh[:, i, :].bitcast(F32), ALU.subtract,
                           after=[t1, dsa_done])
    branch("tg", "wg", False)
    gla_done = w_tok[used[0] - 1]

    mem = slot("mem", 6)
    mh, ml = slot("mh", 12, dt=F32R), slot("ml", 13, dt=F32R)
    mk, mv = slot("mk", 3), slot("mv", 4, [2, D])
    wait(ACTE, y_tok[7], gla_done)
    t_mem = inc(ACTE.dma_start(mem[:, :, :], A["memT"]), c_dup, 16)
    t_r, _ = norm(mem, None, None, after=[t_mem])
    t_x = spread(mem, "g_mem_2", 0, (mh, ml), t_r, [t_mem])
    wait(PE, t_x)
    mk_tok, mv_tok = {}, {}

    def to_mk(n, ps, t):
        mk_tok[n] = act(mk[:, n, :], ps, ACT.Copy, after=[t, t_x])
        return mk_tok[n]

    def to_mv(i, j, ps, t):
        mv_tok[i] = dve(DVE.tensor_copy, mv[:, j, i * 256:(i + 1) * 256], ps, after=[t, t_x])
        return mv_tok[i]

    for i in range(4):
        cols("mk", i, (mh, ml), (4, 5), to_mk)
    for i in range(4):
        toks("mv", i, (mh, ml), (4, 5), to_mv)
    sz_tok.clear()
    sz_after[:] = [y_tok[7]]
    for i in range(4):
        cols("xz", i, x, (4, 5), to_sz)
    y_tok.clear()
    wait(PE, mk_tok[7], mv_tok[3])

    def x_start(i):
        wait(PE, free[4], xq_tok[7])
        for j, c in ((1, 0), (0, 256)):
            for k_ in range(2):
                m = PE.matmul(bank[4][:, c:c + 256], xq[:, 2 * i + k_, j * P:(j + 1) * P], mk[:, 2 * i + k_, :],
                              start=k_ == 0, stop=k_ == 1, skip_group_check=True)
        t = last_pe(m)
        n = head_n[0]
        head_n[0] += 1
        Lb, s_ = L[n % 2], stat[:, n % 16, :]
        t = dve(DVE.tensor_scalar, Lb[:, :], bank[4][:, :], -1.0, None, ALU.mult, after=[t, L_free[n % 2]])
        free[4] = t
        t = dve(DVE.tensor_reduce, s_[:, 0:2], Lb[:, :].rearrange("p (a b) -> p a b", a=2), AX, ALU.min, after=[t])
        return n, softmax_tail(Lb, [(0, 256), (256, 512)], None, t, None, s_)

    def x_middle(i, s):
        return s[0], turn(s[0], s[1], 5, [(256, 0), (0, 128), (384, 256), (128, 384)], 512)

    def x_end(i, s):
        n, t_t = s
        wait(PE, t_t)
        for m_ in range(2):
            b = 6 + m_
            wait(PE, free[b])
            c = i * 256 + m_ * P
            PE.matmul(bank[b][:, 0:S], mv[:, 0, c:c + P], PT[n % 2][:, 0:256], start=True, stop=False)
            t = last_pe(PE.matmul(bank[b][:, 0:S], mv[:, 1, c:c + P], PT[n % 2][:, 256:512], start=False, stop=True))
            PT_free[n % 2] = t
            j = 2 * i + m_
            o = tmp[m_]
            t = dve(DVE.tensor_tensor, o[:, :], bank[b][:, 0:S], sz[:, j, :], ALU.mult, after=[t, sz_tok[j], y_tok.get(j - 2)])
            free[b] = t
            t1 = act(yh[:, j, :], o[:, :], ACT.Copy, after=[t, gla_done])
            y_tok[j] = dve(DVE.tensor_tensor, yl[:, j, :], o[:, :], yh[:, j, :].bitcast(F32), ALU.subtract,
                           after=[t1, gla_done])

    pipeline(4, x_start, x_middle, x_end, {})
    branch("tx", "wx", False)

    fh, fl = slot("fh", 6, dt=F32R), slot("fl", 7, dt=F32R)
    res = slot("res", 9)
    for j in range(NC):
        t1 = act(fh[:, j, :], merged[:, j, :], ACT.Copy, after=[m_tok[j]])
        t = dve(DVE.tensor_tensor, fl[:, j, :], merged[:, j, :], fh[:, j, :].bitcast(F32), ALU.subtract, after=[t1])
    wait(PE, t)
    for i in range(4):
        done = rows("wf", i, 4, fh[:, 2 * i:2 * i + 2, :], fl[:, 2 * i:2 * i + 2, :])
    for j in range(NC):
        t = act(res[:, j, :], bank[j // 2][:, (j % 2) * S:(j % 2 + 1) * S], ACT.Copy, after=[done[j // 2]])
    t_r, _ = norm(res, None, None, after=[t])
    outT = out.rearrange("(j p) s -> p j s", p=P)
    for j in range(NC):
        t = dve(DVE.scalar_tensor_tensor, out=res[:, j, :], in0=res[:, j, :], scalar=gain("g_post_2", j), in1=rstd[:, :],
                op0=ALU.mult, op1=ALU.mult, after=[t_r])
        t = dve(DVE.tensor_tensor, res[:, j, :], res[:, j, :], h[:, j, :], ALU.add, after=[t])
        wait(SP, t)
        t_out = inc(SP.dma_start(outT[:, j, :], res[:, j, :]), c_out, 16)
    assert used[0] == len(PLAN)
    wait(SP, t_out)
    ctx.close()


def bucket(d):
    if d < 16:
        return d
    return min(31, 16 + int(log(d / 16) / log(8) * 16))


def constants():
    f = np.float32
    selA = np.zeros((P, 2, 384), f)
    selB = np.zeros((32, 384), f)
    for i in range(383):
        n = min(max(255 - i, -128), 128) + 128 - 1
        selA[n % P, n // P, i] = 1
        selB[bucket(max(255 - i, 0)), i] = 1
    p, c = np.arange(P)[:, None], np.arange(384)[None, :]
    key = np.where(c < 256, c, c - 256)
    query = np.where(c < 256, p + P, p)
    s, t = np.arange(P)[:, None], np.arange(P)[None, :]
    return {
        "selA": selA, "selB": selB, "ones": np.ones((P, P), f), "ident": np.eye(P, dtype=f), "flip": np.eye(P, dtype=f)[::-1].copy(),
        "gmask": ((s <= t) & (s // 64 == t // 64)).astype(f),
        "reset": np.tile((np.arange(S) % 64 != 0).astype(f), (P, 1)),
        "cm": np.where(key > query, f(GONE), f(0)).astype(f),
    }


def by_cols(w):
    return np.ascontiguousarray(w.reshape(NC, P, -1, 256).transpose(2, 1, 0, 3)).reshape(-1, P, TILE)


def by_rows(w):
    return np.ascontiguousarray(w.reshape(-1, 2, P, D).transpose(0, 2, 1, 3)).reshape(-1, P, TILE)


def feature(x):
    return np.ascontiguousarray(x.T.reshape(NC, P, S).transpose(1, 0, 2))


def kernel(**inputs):
    import concourse.bacc as _bacc
    from concourse.bass_utils import run_bass_kernel_spmd as _run

    a = {k: np.asarray(v) for k, v in inputs.items()}
    qkv, win, w1, w2 = a["attn_w_qkv"][0], a["w_in_2"][0], a["mlp_w1"], a["mlp_w2"]
    cuts = np.cumsum([0, 512, 512, 1024, 16, 1024, 1024, 256, 256, 512, 64, 8, 1024, 1024, 1024, 1024, 1024, 1024])
    gq, gk, gv, ga, gz, dq, dk, dv, iq, ik, iw, dz, xq, xz, ta, tg, tx = [win[:, cuts[i]:cuts[i + 1]] for i in range(17)]
    misc = np.concatenate([ik, ik, ga, iw, np.zeros((D, 104), win.dtype)], axis=1)
    arrays = {
        "wv": by_cols(qkv[:, 2 * D:]), "wk": by_cols(qkv[:, D:2 * D]), "wq": by_cols(qkv[:, :D]),
        "wo": by_rows(a["attn_w_o"][0]), "w1_0": by_cols(w1[0]), "w2_0": by_rows(w2[0]), "w1_1": by_cols(w1[1]),
        "w2_1": by_rows(w2[1]), "rin": by_cols(a["rec_w_in"][0]), "rout": by_rows(a["rec_w_o"][0]),
        "misc": by_cols(misc), "iq": by_cols(iq), "dk": by_cols(dk), "dv": by_cols(dv), "dq": by_cols(dq),
        "gq": by_cols(gq), "gk": by_cols(gk), "gv": by_cols(gv), "dz": by_cols(dz), "ta": by_cols(tg), "wd": by_cols(a["w_dsa_out_2"][0]),
        "xq": by_cols(xq), "gz": by_cols(gz), "tg": by_cols(ta), "wg": by_cols(a["w_gla_out_2"][0]),
        "mk": by_cols(a["w_mem_kv_2"][0][:, :D]), "mv": by_cols(a["w_mem_kv_2"][0][:, D:]), "xz": by_cols(xz),
        "tx": by_cols(tx), "wx": by_cols(a["w_x_out_2"][0]), "wf": by_rows(a["w_o_2"][0]),
        "xT": feature(a["x"][0]), "memT": feature(a["mem_2"][0]),
        "gatew": np.ascontiguousarray(np.stack([a["rec_w_ga"][0], a["rec_w_gx"][0]]).transpose(2, 0, 1, 3)),
        "vec": np.ascontiguousarray(np.concatenate([a[n].reshape(-1, P) for n, _ in VEC]).T),
        "relT": np.ascontiguousarray(a["attn_rel_bias"][0][:, 1:].T.reshape(2, P, 16).transpose(1, 0, 2)),
        "rel_bias_2": a["rel_bias_2"], "w_gla_a_up_2": a["w_gla_a_up_2"], **constants(),
    }
    nc = _bacc.Bacc("TRN2", target_bir_lowering=False, num_devices=1)
    A = {n: nc.dram_tensor(f"in_{n}", v.shape, F32, kind="ExternalInput").ap() for n, v in arrays.items()}
    A["scratch"] = nc.dram_tensor("scratch", (24, 384), F32).ap()
    out = nc.dram_tensor("out_0", (D, S), F32, kind="ExternalOutput").ap()
    build(nc, A, out)
    r = _run(nc, [{f"in_{n}": v for n, v in arrays.items()}], core_ids=[0])
    return np.ascontiguousarray(r.results[0]["out_0"].T).reshape(1, S, D)
```

```python
from contextlib import ExitStack
from math import log

import numpy as np

import concourse.bass as bass
from concourse import mybir

P = 128
S = 256
D = 1024
NC = D // P
F32 = mybir.dt.float32
F32R = mybir.dt.float32r
ALU = mybir.AluOpType
ACT = mybir.ActivationFunctionType
AX = mybir.AxisListType.X

RAW, HIS = 5, 3
TILE = 2048
NEG = -1e30
GONE = -3e38
TAKEN = -3.4e38

VEC = [("norm_mix", 16), ("norm_mlp", 16), ("norm_final", 8), ("rec_b_in", 16), ("rec_conv_w", 32),
       ("rec_conv_b", 8), ("rec_b_ga", 8), ("rec_b_gx", 8), ("rec_a_param", 8), ("rec_b_o", 8),
       ("g_pre_2", 8), ("g_post_2", 8), ("g_mem_2", 8), ("b_gla_a_2", 4), ("g_gla_2", 2)]
VCOL = {}
for _name, _n in VEC:
    VCOL[_name] = sum(n for _, n in VEC[:len(VCOL)])
NV = sum(n for _, n in VEC)



def mlp_plan(n):
    out = [(f"w1_{n}", 0)]
    for i in range(1, 16):
        out += [(f"w1_{n}", i), (f"w2_{n}", i - 1)]
    return out + [(f"w2_{n}", 15)]


def plan():
    out = [("wv", i) for i in range(4)] + [("wk", i) for i in range(4)] + [("wq", 0)]
    for i in range(4):
        out += ([("wq", i + 1)] if i < 3 else []) + ([("wo", i - 1)] if i > 0 else [])
    out += [("wo", 3), ("mk", 0)] + mlp_plan(0) + [("mk", 1)]
    out += [("rin", i) for i in (4, 5, 6, 7, 0, 1, 2, 3)] + [("mk", 2)] + [("rout", i) for i in range(4)]
    out += [("mk", 3)] + mlp_plan(1) + [("mv", 0), ("mv", 1)]
    out += [("misc", 0), ("iq", 0), ("iq", 1), ("dk", 0), ("dv", 0)] + [("dq", i) for i in range(4)] + [("mv", 2), ("mv", 3)]
    out += [("gq", 0), ("gq", 1), ("gk", 0), ("gk", 1)] + [("gv", i) for i in range(4)]
    out += [("dz", i) for i in range(4)] + [("xq", i) for i in range(4)] + [("gz", i) for i in range(4)]
    for i in range(4):
        out += [("ta", i), ("wd", i)]
    out += [("xz", i) for i in range(4)]
    for i in range(4):
        out += [("tg", i), ("wg", i)]
    out += [("tx", 0), ("wx", 0)]
    for i in range(1, 4):
        out += [("tx", i), ("wf", i - 1), ("wx", i)]
    return out + [("wf", 3)]


PLAN = plan()


class Count:

    def __init__(self, sem):
        self.sem, self.n = sem, 0


def build(nc, A, out):
    ctx = ExitStack()
    PE, ACTE, DVE, POOL, SP = nc.tensor, nc.scalar, nc.vector, nc.gpsimd, nc.sync

    def sem(name):
        return Count(ctx.enter_context(nc.semaphore(name)))

    c_hi, c_lo, c_w = sem("hi"), sem("lo"), sem("wdone")
    c_pe, c_act, c_dve, c_pool = sem("pe"), sem("act"), sem("dve"), sem("pool")
    c_raw = [sem(f"raw{i}") for i in range(RAW)]
    c_in = sem("inputs")
    c_tab, c_toep, c_out = sem("tab"), sem("toep"), sem("out")
    c_gw, c_late, c_mem, c_one, c_vec = sem("gatew"), sem("late"), sem("mem"), sem("one"), sem("vec")
    c_x0, c_x1, c_x2, c_x3 = sem("x0"), sem("x1"), sem("x2"), sem("x3")

    waited = {}

    def wait(eng, *toks):
        for tok in toks:
            if tok is None:
                continue
            c, n = tok
            if waited.get((id(eng), id(c)), 0) < n:
                waited[(id(eng), id(c))] = n
                eng.wait_ge(c.sem, n)

    def inc(ins, c, k=1):
        c.n += k
        ins.then_inc(c.sem, k)
        return (c, c.n)

    def act(o, i, f, after=(), **k):
        wait(ACTE, *after)
        return inc(ACTE.activation(o, i, f, **k), c_act)

    def dve(op, *a, after=(), **k):
        wait(DVE, *after)
        return inc(op(*a, **k), c_dve)

    def pool(op, *a, after=(), **k):
        wait(POOL, *after)
        return inc(op(*a, **k), c_pool)

    def last_pe(ins):
        return inc(ins, c_pe)

    base = (nc.sbuf_base + 63) // 64 * 64
    top = [base]

    def region(n):
        at = top[0]
        top[0] += n
        assert top[0] <= nc.sbuf_usable_end, top[0]
        return at

    def place(name, off, free, dt=F32):
        return nc.alloc_sbuf_tensor_at(name, [P] + list(free), dt, offset=off)

    o_raw = region(RAW * 4 * TILE)
    o_hi = region(HIS * 4 * TILE)
    o_slot = [region(8192) for _ in range(15)]
    raw = [place(f"raw_{i}", o_raw + i * 8192, [TILE]) for i in range(RAW)]
    lo = [place(f"lo_{i}", o_raw + i * 8192, [TILE], F32R) for i in range(RAW)]
    hi = [place(f"hi_{i}", o_hi + i * 8192, [TILE], F32R) for i in range(HIS)]

    def slot(name, i, free=(NC, S), dt=F32, off=0):
        return place(name, o_slot[i] + off, free, dt)

    def small(name, free, dt=F32):
        n = 4
        for f in free:
            n *= f
        return place(name, region((n + 31) // 32 * 32), free, dt)

    vec = small("vec", [NV])
    ones = small("ones", [P])
    ident = small("ident", [P])
    flip = small("flip", [P])
    gmask = small("gmask", [P])
    reset = small("reset", [S])
    sq = [small(f"sq{i}", [S]) for i in range(4)]
    rms_t = small("rms_t", [S])
    rstd = small("rstd", [S])
    L = [small(f"L{i}", [512]) for i in range(2)]
    PT = [small(f"PT{i}", [512]) for i in range(2)]
    stat = small("stat", [16, 8])
    o_tmp = region(5 * 1024)
    tmp = [place(f"tmp{i}", o_tmp + 1024 * i, [S]) for i in range(5)]
    epsc = small("epsc", [1])
    dec = small("dec", [4, 4])

    bank = [ctx.enter_context(nc.psum_tensor(f"bank{i}", [P, 512], F32)) for i in range(8)]

    def gain(name, j):
        return vec[:, VCOL[name] + j:VCOL[name] + j + 1]

    issued, cut, used = [0], [0], [0]
    hi_tok, lo_tok, raw_tok, w_tok = {}, {}, {}, {}

    def issue_dma(u):
        name, i = PLAN[u]
        if u >= RAW:
            wait(SP, w_tok[u - RAW])
        raw_tok[u] = inc(SP.dma_start(raw[u % RAW][:, :], A[name][i]), c_raw[u % RAW], 16)

    def split(u):
        if u >= HIS:
            wait(ACTE, w_tok[u - HIS])
        wait(ACTE, raw_tok[u])
        r, h, l = raw[u % RAW], hi[u % HIS], lo[u % RAW]
        hi_tok[u] = inc(ACTE.activation(h[:, :], r[:, :], ACT.Copy), c_hi)
        wait(DVE, hi_tok[u])
        lo_tok[u] = inc(DVE.tensor_tensor(l[:, :], r[:, :], h[:, :].bitcast(F32), ALU.subtract), c_lo)

    def advance():
        t = used[0]
        while issued[0] < min(t + RAW, len(PLAN)):
            issue_dma(issued[0])
            issued[0] += 1
        while cut[0] < min(t + HIS, len(PLAN)):
            split(cut[0])
            cut[0] += 1

    def take(name, i, ahead=True):
        t = used[0]
        assert PLAN[t] == (name, i), (PLAN[t], name, i)
        if ahead:
            advance()
        wait(PE, lo_tok[t])
        return hi[t % HIS], lo[t % RAW]

    def give(ins):
        w_tok[used[0]] = inc(ins, c_w)
        used[0] += 1
        return w_tok[used[0] - 1]

    def mm3(o, ah, al, bh, bl, start, stop, skip=False):
        PE.matmul(o, ah, bh, start=start, stop=False, skip_group_check=skip)
        PE.matmul(o, ah, bl, start=False, stop=False, skip_group_check=skip)
        return PE.matmul(o, al, bh, start=False, stop=stop, skip_group_check=skip)

    free = [None] * 8

    def block(tile, x, j, b, by_tokens, k):
        wh, wl = tile
        xh, xl = x
        o = bank[b][:, 0:S]
        if by_tokens:
            r = slice(j * P, (j + 1) * P)
            return mm3(o, xh[:, k, r], xl[:, k, r], wh[:, k * 256:(k + 1) * 256], wl[:, k * 256:(k + 1) * 256],
                       k == 0, k == NC - 1)
        c = k * 256 + j * 128
        return mm3(o, wh[:, c:c + P], wl[:, c:c + P], xh[:, k, :], xl[:, k, :], k == 0, k == NC - 1)

    def halves(name, i, x, banks, by_tokens):
        tile = []

        def half(j):
            if j == 0:
                tile.append(take(name, i, False))
            wait(PE, free[banks[j]])
            for k in range(NC):
                m = block(tile[0], x, j, banks[j], by_tokens, k)
            return last_pe(m) if j == 0 else give(m)

        return half

    def both(name, i, x, banks, evac, by_tokens, ready):
        tile = take(name, i)
        t = [None, None]
        if ready is None:
            for j in range(2):
                b = banks[j]
                wait(PE, free[b])
                for k in range(NC):
                    m = block(tile, x, j, b, by_tokens, k)
                t = last_pe(m) if j == 0 else give(m)
                free[b] = evac(j, bank[b][:, 0:S], t)
        else:
            wait(PE, free[banks[0]], free[banks[1]])
            for k in range(NC):
                wait(PE, ready[k])
                for j in range(2):
                    m = block(tile, x, j, banks[j], by_tokens, k)
                    if j == 0 and k == NC - 1:
                        t0 = last_pe(m)
            t1 = give(m)
            free[banks[0]] = evac(0, bank[banks[0]][:, 0:S], t0)
            free[banks[1]] = evac(1, bank[banks[1]][:, 0:S], t1)

    def cols(name, i, x, banks, evac, ready=None):
        both(name, i, x, banks, lambda j, ps, t: evac(2 * i + j, ps, t), False, ready)

    def toks(name, i, x, banks, evac, ready=None):
        both(name, i, x, banks, lambda j, ps, t: evac(i, j, ps, t), True, ready)

    def rows(name, i, n, xh, xl):
        wh, wl = take(name, i)
        done = []
        for j in range(NC):
            b = j // 2
            if i == 0:
                wait(PE, free[b])
            for k in range(2):
                c = k * 1024 + j * 128
                m = mm3(bank[b][:, (j % 2) * S:(j % 2 + 1) * S], wh[:, c:c + P], wl[:, c:c + P], xh[:, k, :], xl[:, k, :],
                        i == 0 and k == 0 and j % 2 == 0, i == n - 1 and k == 1, skip=True)
            if i == n - 1 and j % 2:
                done.append(last_pe(m) if j < NC - 1 else give(m))
        if i < n - 1:
            give(m)
        return done

    def load(dst, src):
        return inc(SP.dma_start(dst, src), c_in, 16)

    h = slot("h", 0)
    t_eps = dve(DVE.memset, epsc[:, :], 1e-6)
    t_h = [inc(SP.dma_start(h[:, 2 * j:2 * j + 2, :], A["xT"][:, 2 * j:2 * j + 2, :]), c, 16)
           for j, c in enumerate([c_x0, c_x1, c_x2, c_x3])]
    t_one = inc(SP.dma_start(ones[:, :], A["ones"]), c_one, 16)
    t_vec = inc(SP.dma_start(vec[:, :], A["vec"]), c_vec, 16)
    issue_dma(0)
    issued[0] = 1
    load(ident[:, :], A["ident"])
    load(flip[:, :], A["flip"])
    relT = slot("relT", 14, [2, 16])
    selA = slot("selA", 14, [2, 384], off=256)
    selB = slot("selB", 14, [384], off=3584)
    relB = slot("relB", 14, [8], off=5120)
    load(relT[:, :, :], A["relT"])
    load(selA[:, :, :], A["selA"])
    load(selB[0:32, :], A["selB"])
    load(relB[0:32, :], A["rel_bias_2"])
    load(gmask[:, :], A["gmask"])
    t_in = load(reset[:, :], A["reset"])
    mem = slot("mem", 6)
    mh, ml = slot("mh", 12, dt=F32R), slot("ml", 13, dt=F32R)
    issue_dma(1)
    issued[0] = 2
    t_mem = inc(SP.dma_start(mem[:, :, :], A["memT"]), c_mem, 16)
    while issued[0] < RAW - 1:
        issue_dma(issued[0])
        issued[0] += 1

    sq_read = [None] * 4

    def logs():
        ACTE.preload_act_table_set("natural_log_exp_and_others")

    def mean_square(src, add=None, ready=None, after=()):
        logs()
        acc, t_acc, t_src = None, None, []
        for j in range(NC):
            t = ready[j] if ready else None
            if add is not None:
                done, bias = add
                i1 = bank[j // 2][:, (j % 2) * S:(j % 2 + 1) * S]
                if bias is None:
                    t = dve(DVE.tensor_tensor, src[:, j, :], i1, src[:, j, :], ALU.add, after=[done[j // 2]])
                else:
                    t = dve(DVE.scalar_tensor_tensor, out=src[:, j, :], in0=i1, scalar=gain(bias, j),
                            in1=src[:, j, :], op0=ALU.add, op1=ALU.add, after=[done[j // 2]])
                free[j // 2] = t
            t_src.append(t)
            if j == 0:
                acc = sq[3]
                t_acc = act(acc[:, :], src[:, j, :], ACT.Square, after=[t, sq_read[3], *after])
                continue
            s = sq[j % 3]
            t = act(s[:, :], src[:, j, :], ACT.Square, after=[t, sq_read[j % 3], *after])
            if j < 6:
                t_acc = pool(POOL.tensor_tensor, acc[:, :], acc[:, :], s[:, :], ALU.add, after=[t, t_acc])
                sq_read[j % 3] = t_acc
            else:
                if j == 6:
                    wait(PE, t_acc, free[6])
                    sq_read[3] = last_pe(PE.matmul(bank[6][:, 0:S], ones[:, :], acc[:, :], start=True, stop=False))
                wait(PE, t)
                t_ms = last_pe(PE.matmul(bank[6][:, 0:S], ones[:, :], s[:, :], start=False, stop=j == NC - 1))
                sq_read[j % 3] = t_ms
        t = act(rms_t[:, :], bank[6][:, 0:S], ACT.Ln, scale=1.0 / D, bias=epsc[:, 0:1], after=[t_ms, t_eps])
        free[6] = t
        t_r = act(rstd[:, :], rms_t[:, :], ACT.Exp, scale=-0.5, after=[t])
        return t_r, t_src

    def gained(src, name, g0, dst, t_src, after=()):
        return [dve(DVE.tensor_scalar, dst[:, j, :], src[:, j, :], gain(name, g0 + j), None, ALU.mult,
                    after=[t_src[j], *after]) for j in range(NC)]

    GROUPS = [(0, 1), (1, 2), (2, 4), (4, 6), (6, 8)]

    def spread(hg, t_g, x, t_r, after=()):
        xh, xl = x
        ready, t_m = {}, {}

        def product(g):
            a, b = GROUPS[g]
            t_m[g] = dve(DVE.tensor_tensor, hg[:, a:b, :], hg[:, a:b, :], rstd[:, :].unsqueeze(1).to_broadcast([P, b - a, S]),
                         ALU.mult, after=[t_r, *t_g[a:b]])

        product(0)
        for g, (a, b) in enumerate(GROUPS):
            t = act(xh[:, a:b, :], hg[:, a:b, :], ACT.Copy, after=[t_m[g], *after])
            if g + 1 < len(GROUPS):
                product(g + 1)
            t = dve(DVE.tensor_tensor, xl[:, a:b, :], hg[:, a:b, :], xh[:, a:b, :].bitcast(F32), ALU.subtract, after=[t])
            for j in range(a, b):
                ready[j] = t
        return ready

    def norm(src, name, g0, x, hg, add=None, ready=None, fill=None, after=()):
        if fill:
            half, banks, evac = fill
            f0 = half(0)
        t_r, t_src = mean_square(src, add, ready, after)
        if fill:
            f1 = half(1)
        t_g = gained(src, name, g0, hg, t_src, after)
        out = spread(hg, t_g, x, t_r, after)
        if fill:
            free[banks[0]] = evac(0, bank[banks[0]][:, 0:S], f0)
            free[banks[1]] = evac(1, bank[banks[1]][:, 0:S], f1)
        return out

    x = (slot("xh", 1, dt=F32R), slot("xl", 2, dt=F32R))
    hg = slot("hg", 2)

    wait(PE, t_one)
    wait(DVE, t_vec)
    ready = norm(h, "norm_mix", 0, x, hg, ready=[t_h[j // 2] for j in range(NC)])

    def softmax_tail(Lb, tiles, mx, t_max, src_neg, st):
        t = t_max
        for n, (a, b) in enumerate(tiles):
            t = act(Lb[:, a:b], Lb[:, a:b], ACT.Exp, scale=-1.0, bias=st[:, n:n + 1], accum_out=st[:, 2 + n:3 + n],
                    after=[t_max])
        t = dve(DVE.reciprocal, st[:, 4:6], st[:, 2:4], after=[t])
        for n, (a, b) in enumerate(tiles):
            t2 = dve(DVE.tensor_scalar, Lb[:, a:b], Lb[:, a:b], st[:, 4 + n:5 + n], None, ALU.mult, after=[t])
        return t2

    TT = [(0, 256), (256, 384)]
    head_n = [0]
    L_free, PT_free = [None, None], [None, None]

    def scores(qT, kT, sb_):
        wait(PE, free[sb_])
        PE.matmul(bank[sb_][:, 0:256], qT[:, P:S], kT, start=True, stop=True)
        return last_pe(PE.matmul(bank[sb_][:, 256:384], qT[:, 0:P], kT[:, 0:P], start=True, stop=True, skip_group_check=True))

    def soft(t_s, sb_, bias, mask, t_b):
        n = head_n[0]
        head_n[0] += 1
        Lb, st = L[n % 2], stat[:, n % 16, :]
        if mask is None:
            for a, (o, e, c) in enumerate([(0, 256, 0), (256, 384, 128)]):
                t = dve(DVE.tensor_tensor_reduce, out=Lb[:, o:e], in0=bank[sb_][:, o:e], in1=bias[:, c:256], scale=-1.0,
                        scalar=3.4e38, op0=ALU.add, op1=ALU.min, accum_out=st[:, a:a + 1], after=[t_s, t_b, L_free[n % 2]])
            free[sb_] = t
        else:
            for a, (o, e, c) in enumerate([(0, 256, 0), (256, 384, 128)]):
                t = dve(DVE.tensor_tensor, Lb[:, o:e], bank[sb_][:, o:e], bias[:, c:256], ALU.add,
                        after=[t_s, t_b, L_free[n % 2]])
            free[sb_] = t
            for a, (o, e) in enumerate(TT):
                t = dve(DVE.tensor_tensor_reduce, out=Lb[:, o:e], in0=Lb[:, o:e], in1=mask[:, o:e], scale=-1.0,
                        scalar=3.4e38, op0=ALU.add, op1=ALU.min, accum_out=st[:, a:a + 1], after=[t])
        return n, softmax_tail(Lb, TT, None, t, None, st)

    def turn(n, t_p, pb, blocks, width):
        wait(PE, t_p, free[pb])
        for src, dst in blocks:
            m = PE.transpose(bank[pb][:, dst:dst + P], L[n % 2][:, src:src + P], ident[:, :])
        t = last_pe(m)
        L_free[n % 2] = t
        t2 = act(PT[n % 2][:, 0:width], bank[pb][:, 0:width], ACT.Copy, after=[t, PT_free[n % 2]])
        free[pb] = t2
        return t2

    CAUSAL = [(256, 0), (0, 128), (128, 256)]

    def weigh(n, t_t, o, V, lo_, hi_):
        wait(PE, t_t)
        PE.matmul(o, V[:, 0, lo_:hi_], PT[n % 2][:, 0:256], start=True, stop=False)
        t = last_pe(PE.matmul(o[:, P:S], V[:, 1, lo_:hi_], PT[n % 2][:, 256:384], start=False, stop=True))
        PT_free[n % 2] = t
        return t

    q, k = slot("q", 5), slot("k", 6)
    v = slot("v", 7, [2, D])
    oh, ol = slot("oh", 10, dt=F32R), slot("ol", 11, dt=F32R)

    def to_v(i, j, ps, t):
        return dve(DVE.tensor_copy, v[:, j, i * 256:(i + 1) * 256], ps, after=[t])

    def to_k(n, ps, t):
        return act(k[:, n, :], ps, ACT.Copy, after=[t])

    q_tok = {}

    def to_q(n, ps, t):
        q_tok[n] = act(q[:, n, :], ps, ACT.Copy, scale=0.125, after=[t])
        return q_tok[n]

    toks("wv", 0, x, (4, 5), to_v, ready)
    tab_dram = A["scratch"]
    wait(PE, t_in)
    PE.matmul(bank[7][0:16, 0:384], relT[:, 0, :], selA[:, 0, :], start=True, stop=False)
    t = last_pe(PE.matmul(bank[7][0:16, 0:384], relT[:, 1, :], selA[:, 1, :], start=False, stop=True))
    tabA = slot("tabA", 5, [384])
    tabB = slot("tabB", 5, [384], off=2048)
    t1 = dve(DVE.tensor_copy, tabA[0:16, :], bank[7][0:16, 0:384], after=[t])
    t = last_pe(PE.matmul(bank[6][0:8, 0:384], relB[0:32, :], selB[0:32, :], start=True, stop=True))
    t2 = dve(DVE.tensor_copy, tabB[0:8, :], bank[6][0:8, 0:384], after=[t])
    free[7], free[6] = t1, t2
    wait(ACTE, t2)
    inc(ACTE.dma_start(tab_dram[0:16, :], tabA[0:16, :]), c_tab, 16)
    t_tab = inc(ACTE.dma_start(tab_dram[16:24, :], tabB[0:8, :]), c_tab, 16)

    def toeplitz(dst, g, row, n):
        wait(ACTE, t_tab)
        t = inc(ACTE.dma_start(g, bass.AP(tab_dram.tensor, row * 384, [[1, P], [384, n], [1, 256]])), c_toep, 16)
        g2, d2 = g.rearrange("p n j -> p (n j)"), dst.rearrange("p n j -> p (n j)")
        for i in range(n // 2):
            b = 6 + i % 2
            wait(PE, t, free[b])
            t1 = last_pe(PE.matmul(bank[b][:, :], flip[:, :], g2[:, i * 512:(i + 1) * 512], start=True, stop=True))
            free[b] = dve(DVE.tensor_copy, d2[:, i * 512:(i + 1) * 512], bank[b][:, :], after=[t1])
        return free[b]

    toks("wv", 1, x, (4, 5), to_v)
    mg = place("mg", o_slot[13], [NC, S])
    m_ready = norm(mem, "g_mem_2", 0, (mh, ml), mg, ready=[t_mem] * NC)
    toks("wv", 2, x, (4, 5), to_v)
    toks("wv", 3, x, (4, 5), to_v)
    cols("wk", 0, x, (4, 5), to_k)
    T = place("T", o_slot[8], [16, 256])
    GT = place("GT", o_slot[10], [16, 256])
    t = toeplitz(T[:, :, :], GT[:, :, :], 0, 16)
    wait(POOL, t)
    t_T = inc(POOL.memset(T[0:64, :, 192:256], NEG), c_pool)

    for i in range(1, 4):
        cols("wk", i, x, (4, 5), to_k)
    cols("wq", 0, x, (4, 5), to_q)
    wait(PE, free[4], free[5], (c_dve, c_dve.n))

    def pipeline(n_heads, start, middle, end, fills):
        st1, st2 = {}, {}
        for i in range(n_heads + 2):
            if i < n_heads:
                st1[i] = start(i)
            if i in fills:
                fills[i]()
            if 1 <= i <= n_heads:
                st2[i - 1] = middle(i - 1, st1[i - 1])
            if 2 <= i:
                end(i - 2, st2[i - 2])

    o_tok = {}

    def a_start(i):
        j, r = i // 2, (i % 2) * 64
        wait(PE, q_tok[j])
        t = scores(q[r:r + 64, j, :], k[r:r + 64, j, :], 4)
        return soft(t, 4, T[:, i, :], None, t_T)

    def a_middle(i, s):
        return s[0], turn(s[0], s[1], 5, CAUSAL, 384)

    def a_end(i, s):
        r = (i % 2) * 64
        if i % 2 == 0:
            wait(PE, free[7])
        t = weigh(s[0], s[1], bank[7][r:r + 64, 0:S], v, i * 64, i * 64 + 64)
        if i % 2:
            j = i // 2
            t1 = act(oh[:, j, :], bank[7][:, 0:S], ACT.Copy, after=[t])
            o_tok[j] = dve(DVE.tensor_tensor, ol[:, j, :], bank[7][:, 0:S], oh[:, j, :].bitcast(F32), ALU.subtract, after=[t1])
            free[7] = o_tok[j]

    def wo_part(i):
        wait(PE, o_tok[2 * i], o_tok[2 * i + 1])
        return rows("wo", i, 4, oh[:, 2 * i:2 * i + 2, :], ol[:, 2 * i:2 * i + 2, :])

    fills = {}
    for i in range(3):
        fills[4 * i + 1] = lambda i=i: cols("wq", i + 1, x, (6, 6), to_q)
        fills[4 * i + 7] = lambda i=i: wo_part(i)
    pipeline(16, a_start, a_middle, a_end, fills)
    done = wo_part(3)

    mk, mv = slot("mk", 3), slot("mv", 4, [2, D])
    mk_tok, mv_tok = {}, {}
    wait(PE, m_ready[7])

    def mem_fill(name, i, banks=(7, 0)):
        def evac(j, ps, t):
            if name == "mk":
                mk_tok[i] = act(mk[:, 2 * i + j, :], ps, ACT.Copy, after=[t])
                return mk_tok[i]
            mv_tok[i] = act(mv[:, j, i * 256:(i + 1) * 256], ps, ACT.Copy, after=[t])
            return mv_tok[i]

        return halves(name, i, (mh, ml), banks, name == "mv"), banks, evac

    zf = [slot(f"zf{i}", 5, [S], off=1024 * i) for i in range(4)]
    zr = [slot(f"zr{i}", 6, [S], off=1024 * i) for i in range(4)]
    zh = [slot(f"zh{i}", 7, [2, S], F32R, off=2048 * i) for i in range(3)]
    zl = [slot(f"zl{i}", 10, [2, S], F32R, off=2048 * i) for i in range(3)]

    def mlp(layer, done, bias, fill):
        ready = norm(h, "norm_mlp", 8 * layer, x, hg, add=(done, bias), fill=fill)
        z_tok, z_free = {}, {}

        def to_z(n, ps, t):
            i, j = n // 2, n % 2
            t1 = act(zr[n % 4][:, :], ps, ACT.Relu, after=[t, z_tok.get(i - 2)])
            t2 = act(zh[i % 3][:, j, :], zr[n % 4][:, :], ACT.Square, after=[t1, z_free.get(i - 3)])
            t3 = dve(DVE.tensor_tensor, zf[n % 4][:, :], zr[n % 4][:, :], zr[n % 4][:, :], ALU.mult, after=[t1])
            z_tok[i] = dve(DVE.tensor_tensor, zl[i % 3][:, j, :], zf[n % 4][:, :], zh[i % 3][:, j, :].bitcast(F32),
                           ALU.subtract, after=[t2, t3, z_free.get(i - 3)])
            return t1

        def down(i):
            wait(PE, z_tok[i])
            d = rows(f"w2_{layer}", i, 16, zh[i % 3], zl[i % 3])
            z_free[i] = w_tok[used[0] - 1]
            return d

        for i in range(17):
            if i < 16:
                cols(f"w1_{layer}", i, x, (4, 5), to_z, ready if i == 0 else None)
            if i > 0:
                d = down(i - 1)
        return d

    done = mlp(0, done, None, mem_fill("mk", 0))

    ready = norm(h, "norm_mix", 8, x, hg, add=(done, None), fill=mem_fill("mk", 1))
    XW = S + 3
    xbr = place("xbr", o_slot[5], [NC, XW])
    xc, rg, ig, tt, yb = slot("xc", 7), slot("rg", 8), slot("ig", 9), slot("tt", 10), slot("yb", 11)
    gw = slot("gw", 14, [2, NC, P])
    wait(ACTE, ready[0])
    t_gw = inc(ACTE.dma_start(gw[:, :, :, :], A["gatew"]), c_gw, 16)
    gh, gl = slot("gh", 5, dt=F32R), slot("gl", 8, dt=F32R)
    sp_ = stat[:, 0:2, :].rearrange("p a b -> p (a b)")
    ap_ = vec[:, VCOL["rec_a_param"]:VCOL["rec_a_param"] + 8]
    z8 = tmp[3]
    t = act(z8[:, 0:8], ap_, ACT.Abs)
    t1 = dve(DVE.tensor_scalar, z8[:, 8:16], ap_, -1.0, 0.0, ALU.mult, ALU.max)
    t = act(z8[:, 16:24], z8[:, 0:8], ACT.Exp, scale=-1.0, after=[t])
    t = act(z8[:, 24:32], z8[:, 16:24], ACT.Ln, bias=1.0, after=[t])
    t = dve(DVE.tensor_tensor, z8[:, 32:40], z8[:, 8:16], z8[:, 24:32], ALU.add, after=[t, t1])
    t = dve(DVE.tensor_scalar, sp_[:, 0:8], z8[:, 32:40], 8.0, None, ALU.mult, after=[t])
    t_sp = dve(DVE.tensor_scalar, sp_[:, 8:16], z8[:, 32:40], -8.0, None, ALU.mult)
    t_pad = dve(DVE.memset, xbr[:, :, 0:3], 0.0)
    xc_tok = {}
    g_tok = {}
    t_t, t_a, t_m, t_gi, t_s, gh_tok = {}, {}, {}, {}, {}, {}

    def to_y(n, ps, t):
        return act(yb[:, n - 8, :], ps, ACT.Gelu_apprx_tanh, bias=gain("rec_b_in", n), after=[t])

    def to_x(n, ps, t):
        t1 = act(xbr[:, n, 3:XW], ps, ACT.Identity, bias=gain("rec_b_in", n), after=[t])
        t = dve(DVE.tensor_scalar, xc[:, n, :], xbr[:, n, 0:S], gain("rec_conv_w", n), gain("rec_conv_b", n),
                ALU.mult, ALU.add, after=[t1, t_pad])
        for w in range(1, 4):
            t = dve(DVE.scalar_tensor_tensor, out=xc[:, n, :], in0=xbr[:, n, w:w + S], scalar=gain("rec_conv_w", 8 * w + n),
                    in1=xc[:, n, :], op0=ALU.mult, op1=ALU.add, after=[t])
        xc_tok[n] = t
        return t1

    def gates(n):
        wait(PE, xc_tok[n], t_gw)
        for m, (dst, name, b) in enumerate([(rg, "rec_b_ga", 6), (ig, "rec_b_gx", 7)]):
            wait(PE, free[b])
            t = last_pe(PE.matmul(bank[b][:, 0:S], gw[:, m, n, :], xc[:, n, :], start=True, stop=True))
            free[b] = act(dst[:, n, :], bank[b][:, 0:S], ACT.Sigmoid, bias=gain(name, n), after=[t])
            g_tok[n, m] = free[b]
        t_t[n] = act(tt[:, n, :], rg[:, n, :], ACT.Tanh, scale=sp_[:, n:n + 1], after=[t_sp, g_tok[n, 0]])
        t_gi[n] = pool(POOL.tensor_tensor, ig[:, n, :], ig[:, n, :], xc[:, n, :], ALU.mult, after=[g_tok[n, 1], xc_tok[n]])

    def decays(n0):
        for n in range(n0, n0 + 4):
            t_a[n] = act(rg[:, n, :], rg[:, n, :], ACT.Exp, scale=sp_[:, 8 + n:9 + n], after=[t_t[n]])
            s = tmp[n % 3]
            t = dve(DVE.tensor_tensor, s[:, :], rg[:, n, :], rg[:, n, :], ALU.mult, after=[t_a[n]])
            t_m[n] = dve(DVE.scalar_tensor_tensor, out=tt[:, n, :], in0=s[:, :], scalar=1.0, in1=tt[:, n, :], op0=ALU.add,
                         op1=ALU.mult, after=[t])
        for n in range(n0, n0 + 4, 2):
            t_s[n] = t_s[n + 1] = act(tt[:, n:n + 2, :], tt[:, n:n + 2, :], ACT.Sqrt, after=[t_m[n + 1]])

    def recur(n):
        t = dve(DVE.tensor_tensor, ig[:, n, :], tt[:, n, :], ig[:, n, :], ALU.mult, after=[t_s[n], t_gi[n]])
        t = dve(DVE.tensor_tensor_scan, tt[:, n, :], rg[:, n, :], ig[:, n, :], 0.0, ALU.mult, ALU.add, after=[t])
        t = dve(DVE.tensor_tensor, tt[:, n, :], tt[:, n, :], yb[:, n, :], ALU.mult, after=[t, t_y])
        t1 = act(gh[:, n, :], tt[:, n, :], ACT.Copy, after=[t])
        gh_tok[n] = dve(DVE.tensor_tensor, gl[:, n, :], tt[:, n, :], gh[:, n, :].bitcast(F32), ALU.subtract, after=[t1])

    for i in range(4, 8):
        cols("rin", i, x, (4, 5), to_y, ready if i == 4 else None)
    t_y = free[5]
    for i in range(4):
        cols("rin", i, x, (4, 5), to_x)
        if i:
            gates(2 * i - 2)
            gates(2 * i - 1)
        if i == 3:
            decays(0)
    fill, banks, evac = mem_fill("mk", 2, (0, 1))
    f0 = fill(0)
    gates(6)
    gates(7)
    f1 = fill(1)
    for n in range(4):
        recur(n)
    decays(4)
    free[0] = evac(0, bank[0][:, 0:S], f0)
    free[1] = evac(1, bank[1][:, 0:S], f1)
    for n in range(4, 8):
        recur(n)
    for i in range(4):
        wait(PE, gh_tok[2 * i + 1])
        done = rows("rout", i, 4, gh[:, 2 * i:2 * i + 2, :], gl[:, 2 * i:2 * i + 2, :])

    done = mlp(1, done, "rec_b_o", mem_fill("mk", 3))

    half, (b0, b1), evac = mem_fill("mv", 0)
    f0 = half(0)
    t_r, t_src = mean_square(h, (done, None))
    t_g = gained(h, "norm_final", 0, hg, t_src)
    f1 = half(1)
    t_res = {}
    for a, b in GROUPS:
        t = dve(DVE.tensor_tensor, h[:, a:b, :], hg[:, a:b, :], rstd[:, :].unsqueeze(1).to_broadcast([P, b - a, S]), ALU.mult,
                after=[t_r, *t_g[a:b]])
        for j in range(a, b):
            t_res[j] = t
    free[b0] = evac(0, bank[b0][:, 0:S], f0)
    free[b1] = evac(1, bank[b1][:, 0:S], f1)
    ready = norm(h, "g_pre_2", 0, x, hg, ready=t_res, fill=mem_fill("mv", 1))

    merged = slot("merged", 5)
    ik, low = slot("ik", 5, [S]), slot("low", 5, [S], off=1024)
    sc, wk_, cm = [slot(f"sc{n}", 5, [384], off=2048 + 1536 * n) for n in range(3)]
    rl = [slot(f"rl{n}", 10, [384], off=1536 * n) for n in range(2)]
    iw, mx8 = slot("iw", 10, [2, 32], off=3072), slot("mx8", 10, [2, 8], off=3328)
    up = slot("up", 10, [512], off=4096)
    dq = slot("dq", 6)
    iq = slot("iq", 7, [4, S])
    dk = slot("dk", 7, [2, S], off=4096)
    dv = slot("dv", 7, [2, S], off=6144)
    sz = slot("sz", 8)
    T2 = slot("T2", 9, [8, 256])
    yh, yl = slot("yh", 10, dt=F32R), slot("yl", 11, dt=F32R)
    gq, gk = slot("gq", 12, [4, S]), slot("gk", 12, [4, S], off=4096)
    gv = slot("gv", 13, [2, D])
    gb, kd = slot("gb", 14, [4, S]), slot("kd", 14, [4, S], off=4096)

    wait(ACTE, ready[0])
    t_late = inc(ACTE.dma_start(cm[:, :], A["cm"]), c_late, 16)
    t_late = inc(ACTE.dma_start(up[0:16, :], A["w_gla_a_up_2"][0]), c_late, 16)

    tok = {}

    def keep(name, dst, scale=1.0, base=0):
        def evac(n, ps, t):
            tok[name, n] = act(dst[:, n - base, :], ps, ACT.Copy, scale=scale, after=[t])
            return tok[name, n]
        return evac

    def keep_tokens(name, dst):
        def evac(i, j, ps, t):
            tok[name, i, j] = act(dst[:, j, i * 256:(i + 1) * 256], ps, ACT.Copy, after=[t])
            return tok[name, i, j]
        return evac

    def to_misc(n, ps, t):
        tok["misc", n] = act((ik, low)[n][:, :], ps, ACT.Copy, after=[t])
        return tok["misc", n]

    cols("misc", 0, x, (4, 5), to_misc, ready)
    t_T2 = toeplitz(T2[:, :, :], slot("GT2", 11, [8, 256])[:, :, :], 16, 8)
    for i in range(2):
        cols("iq", i, x, (4, 5), keep("iq", iq))
    wait(PE, tok["misc", 1], free[6])
    for j in range(2):
        m = PE.transpose(bank[6][:, 32 * j:32 * j + 32], low[0:32, j * P:(j + 1) * P], ident[0:32, 0:32])
    t = last_pe(m)
    t_iw = dve(DVE.tensor_scalar, iw[:, :, :].rearrange("p a b -> p (a b)"), bank[6][:, 0:64], 8 ** -0.5, 64 ** -0.5,
               ALU.mult, ALU.mult, after=[t])
    free[6] = t_iw

    score = {"t": None}
    rl_free = [None, None]

    def index_head(i):
        r = (i % 2) * 64
        b = 6 + i % 2
        wait(PE, tok["iq", i // 2], tok["misc", 0], free[b])
        PE.matmul(bank[b][:, 0:256], iq[r:r + 64, i // 2, P:S], ik[r:r + 64, :], start=True, stop=True)
        t = last_pe(PE.matmul(bank[b][:, 256:384], iq[r:r + 64, i // 2, 0:P], ik[r:r + 64, 0:P], start=True, stop=True,
                              skip_group_check=True))
        t = act(rl[i % 2][:, :], bank[b][:, 0:384], ACT.Relu, after=[t, rl_free[i % 2]])
        free[b] = t
        ts = []
        for j, (a, e) in ((1, TT[0]), (0, TT[1])):
            w = iw[:, j, 16 + i:17 + i]
            if i == 0:
                ts.append(dve(DVE.tensor_scalar, sc[:, a:e], rl[0][:, a:e], w, None, ALU.mult, after=[t, t_iw]))
            else:
                ts.append(dve(DVE.scalar_tensor_tensor, out=sc[:, a:e], in0=rl[i % 2][:, a:e], scalar=w, in1=sc[:, a:e],
                              op0=ALU.mult, op1=ALU.add, after=[t, score["t"]]))
        score["t"] = rl_free[i % 2] = ts[-1]

    def top8(r):
        t = score["t"]
        src = sc if r == 0 else wk_
        ts = [dve(DVE.max, mx8[:, j, :], src[:, a:e], after=[t]) for j, (a, e) in enumerate(TT)]
        for j, (a, e) in enumerate(TT):
            t = dve(DVE.match_replace, wk_[:, a:e], mx8[:, j, :], src[:, a:e], TAKEN, after=[ts[j]])
        score["t"] = t

    for i in range(4):
        index_head(i)
    cols("dk", 0, x, (4, 5), keep("dk", dk))
    for i in range(4, 8):
        index_head(i)
    score["t"] = dve(DVE.tensor_tensor, sc[:, :], sc[:, :], cm[:, :], ALU.add, after=[score["t"], t_late])
    toks("dv", 0, x, (4, 5), keep_tokens("dv", dv))
    top8(0)
    for i in range(4):
        cols("dq", i, x, (4, 5), keep("dq", dq, scale=128 ** -0.5))
        top8(1 + i)
    for i in (2, 3):
        m2 = mem_fill("mv", i)
        toks("mv", i, (mh, ml), (4, 5), lambda i_, j, ps, t: m2[2](j, ps, t))
        top8(3 + i)
    for i in range(2):
        cols("gq", i, x, (4, 5), keep("gq", gq))
        if i == 0:
            top8(7)
    mask = sc
    t = dve(DVE.tensor_scalar, sc[:, :], wk_[:, :], -3.2e38, NEG, ALU.is_gt, ALU.mult, after=[score["t"]])
    t_mask = dve(DVE.tensor_tensor, sc[:, :], sc[:, :], cm[:, :], ALU.min, after=[t])
    for i in range(2):
        cols("gk", i, x, (4, 5), keep("gk", gk))

    wait(PE, t_late)
    g_t, e_t = {}, {}

    def decay_sum(n):
        b = 6 + n % 2
        u, w = tmp[n % 2], tmp[2 + n % 2]
        wait(PE, free[b])
        t = last_pe(PE.matmul(bank[b][:, 0:S], up[0:16, n * P:(n + 1) * P], low[0:16, :], start=True, stop=True))
        t = act(u[:, :], bank[b][:, 0:S], ACT.Identity, bias=gain("b_gla_a_2", n), after=[t, g_t.get(n - 2)])
        free[b] = t
        t = act(w[:, :], u[:, :], ACT.Abs, after=[t])
        t = act(w[:, :], w[:, :], ACT.Exp, scale=-1.0, after=[t])
        t = act(w[:, :], w[:, :], ACT.Ln, bias=1.0, after=[t])
        t = dve(DVE.scalar_tensor_tensor, out=u[:, :], in0=u[:, :], scalar=0.0, in1=w[:, :], op0=ALU.min, op1=ALU.subtract,
                after=[t])
        g_t[n] = dve(DVE.tensor_tensor_scan, gb[:, n, :], reset[:, :], u[:, :], 0.0, ALU.mult, ALU.add, after=[t])

    def decayed(n):
        ep, en = tmp[n % 2], tmp[2 + n % 2]
        t = act(ep[:, :], gb[:, n, :], ACT.Exp, scale=1.0 / 16, after=[g_t[n], g_t[3], e_t.get(n - 2)])
        t1 = act(en[:, :], gb[:, n, :], ACT.Exp, scale=-1.0 / 16)
        t2 = dve(DVE.tensor_copy, dec[:, n, :], ep[:, 63:S:64], after=[t])
        dve(DVE.scalar_tensor_tensor, out=gq[:, n, :], in0=gq[:, n, :], scalar=128 ** -0.5, in1=ep[:, :], op0=ALU.mult,
            op1=ALU.mult, after=[tok["gq", n]])
        t = dve(DVE.tensor_tensor, kd[:, n, :], gk[:, n, :], en[:, :], ALU.mult, after=[t1, tok["gk", n]])
        e_t[n] = dve(DVE.tensor_tensor, gk[:, n, :].rearrange("p (c t) -> p c t", c=4),
                     kd[:, n, :].rearrange("p (c t) -> p c t", c=4), dec[:, n, :].unsqueeze(2).to_broadcast([P, 4, 64]),
                     ALU.mult, after=[t, t2])

    logs()
    for i in range(4):
        toks("gv", i, x, (4, 5), keep_tokens("gv", gv))
        decay_sum(i)

    def to_sz(name):
        def evac(n, ps, t):
            tok[name, n] = act(sz[:, n, :], ps, ACT.Silu, after=[t, tok.get(("sz free", n))])
            return tok[name, n]
        return evac

    for i in range(4):
        decayed(i)
    for i in range(4):
        cols("dz", i, x, (4, 5), to_sz("dz"))

    xq = slot("xq", 6)

    def d_start(i):
        wait(PE, tok["dq", i], tok["dk", i // 4])
        return soft(scores(dq[:, i, :], dk[:, i // 4, :], 4), 4, T2[:, i, :], mask, t_T2)

    y = {}

    def d_end(i, s):
        wait(PE, free[7])
        c = (i // 4) * 128
        t = weigh(s[0], s[1], bank[7][:, 0:S], dv, c, c + 128)
        o = tmp[i % 2]
        t = dve(DVE.tensor_tensor, o[:, :], bank[7][:, 0:S], sz[:, i, :], ALU.mult, after=[t, tok["dz", i], y.get(("d", i - 2))])
        free[7] = tok["sz free", i] = t
        t1 = act(yh[:, i, :], o[:, :], ACT.Copy, after=[t])
        y["d", i] = dve(DVE.tensor_tensor, yl[:, i, :], o[:, :], yh[:, i, :].bitcast(F32), ALU.subtract, after=[t1])

    wait(DVE, t_mask)
    wait(PE, tok["dv", 0, 0], tok["dv", 0, 1])
    logs()
    pipeline(8, d_start, a_middle, d_end,
             {2 * i + 2: lambda i=i: cols("xq", i, x, (6, 3), keep("xq", xq, scale=1.0 / 16)) for i in range(4)})
    for i in range(4):
        cols("gz", i, x, (4, 5), to_sz("gz"))

    og = slot("og", 7)
    at = [slot(f"at{i}", 9, [2, P], off=1024 * i) for i in range(2)]
    ktT = [slot(f"ktT{i}", 9, [2, P], off=2048 + 1024 * i) for i in range(2)]
    st = [slot(f"st{i}", 9, [256], off=4096 + 1024 * i) for i in range(3)]
    gms = slot("gms", 14, [4, S])
    gdone, g_head, ms_t = {}, {}, {}

    def g_first(n):
        A_, K_ = at[n % 2], ktT[n % 2]
        wait(PE, e_t[n], free[0])
        for j in range(2):
            m = PE.matmul(bank[0][:, j * P:(j + 1) * P], kd[:, n, j * P:(j + 1) * P], gq[:, n, j * P:(j + 1) * P],
                          start=True, stop=True, skip_group_check=True)
        t = last_pe(m)
        t_at = dve(DVE.tensor_tensor, A_[:, :, :], bank[0][:, 0:S].rearrange("p (a b) -> p a b", a=2),
                   gmask[:, :].unsqueeze(1).to_broadcast([P, 2, P]), ALU.mult, after=[t, gdone.get(n - 2)])
        free[0] = t_at
        wait(PE, free[1])
        for j in range(2):
            m = PE.transpose(bank[1][:, j * P:(j + 1) * P], gk[:, n, j * P:(j + 1) * P], ident[:, :])
        t = last_pe(m)
        t_k = act(K_[:, :, :], bank[1][:, 0:S].rearrange("p (a b) -> p a b", a=2), ACT.Copy, after=[t, gdone.get(n - 2)])
        free[1] = t_k
        g_head[n] = (t_at, t_k)

    def g_states(n):
        K_ = ktT[n % 2]
        wait(PE, g_head[n][1], free[2], free[3])
        for c in range(3):
            r, j = (c % 2) * 64, c // 2
            m = PE.matmul(bank[2 + c % 2][:, j * 256:j * 256 + 256], K_[r:r + 64, j, :],
                          gv[r:r + 64, j, n * 256:(n + 1) * 256], start=True, stop=True, skip_group_check=True)
        t_u = last_pe(m)
        t = dve(DVE.tensor_copy, st[0][:, :], bank[2][:, 0:256], after=[t_u, gdone.get(n - 1)])
        t = dve(DVE.scalar_tensor_tensor, out=st[1][:, :], in0=st[0][:, :], scalar=dec[:, n, 1:2], in1=bank[3][:, 0:256],
                op0=ALU.mult, op1=ALU.add, after=[t])
        free[3] = t
        t = dve(DVE.scalar_tensor_tensor, out=st[2][:, :], in0=st[1][:, :], scalar=dec[:, n, 2:3], in1=bank[2][:, 256:512],
                op0=ALU.mult, op1=ALU.add, after=[t])
        free[2] = t
        g_head[n] += (t,)

    def g_second(n):
        A_ = at[n % 2]
        t_at, _, t_st = g_head[n]
        wait(PE, t_at, t_st)
        ts = []
        for m_ in range(2):
            b = m_
            wait(PE, free[b])
            c0 = n * 256 + m_ * P
            for j in range(2):
                PE.matmul(bank[b][:, j * P:(j + 1) * P], gv[:, j, c0:c0 + P], A_[:, j, :], start=j == 0, stop=False,
                          skip_group_check=True)
            for c in range(1, 4):
                m = PE.matmul(bank[b][:, c * 64:c * 64 + 64], st[c - 1][:, m_ * P:(m_ + 1) * P], gq[:, n, c * 64:c * 64 + 64],
                              start=False, stop=True, skip_group_check=True)
            gdone[n] = last_pe(m)
            free[b] = act(og[:, 2 * n + m_, :], bank[b][:, 0:S], ACT.Copy, after=[gdone[n]])
            ts.append(act(sq[m_][:, :], og[:, 2 * n + m_, :], ACT.Square, after=[free[b], sq_read[m_]]))
        t = pool(POOL.tensor_tensor, sq[2][:, :], sq[0][:, :], sq[1][:, :], ALU.add, after=[*ts, sq_read[2]])
        sq_read[0] = sq_read[1] = t
        return t

    def g_third(n, t):
        wait(PE, t, free[2])
        sq_read[2] = last_pe(PE.matmul(bank[2][:, 0:S], ones[:, :], sq[2][:, :], start=True, stop=True))
        free[2] = ms_t[n] = act(gms[:, n, :], bank[2][:, 0:S], ACT.Copy, after=[sq_read[2]])

    m_tok = {}

    def to_g(n, ps, t):
        tok["g", n] = act(tmp[3 + n % 2][:, :], ps, ACT.Sigmoid, after=[t, m_tok.get(n - 2), m_tok.get(n + 6)])
        return tok["g", n]

    def to_m(first):
        def evac(n, ps, t):
            if first:
                m_tok[n] = dve(DVE.tensor_tensor, merged[:, n, :], ps, tmp[3 + n % 2][:, :], ALU.mult, after=[t, tok["g", n]])
                return m_tok[n]
            t = dve(DVE.tensor_tensor, tmp[n % 2][:, :], ps, tmp[3 + n % 2][:, :], ALU.mult, after=[t, tok["g", n], m_tok.get(n - 2)])
            m_tok[n] = dve(DVE.tensor_tensor, merged[:, n, :], merged[:, n, :], tmp[n % 2][:, :], ALU.add, after=[t])
            return t
        return evac

    Y = (yh, yl)
    wait(PE, y["d", 7], tok["gv", 3, 1])
    for n in range(4):
        g_first(n)
        cols("ta", n, x, (4, 5), to_g)
        g_states(n)
        cols("wd", n, Y, (6, 7), to_m(True))
        g_third(n, g_second(n))
    dsa_done = w_tok[used[0] - 1]

    zx = slot("zx", 13)
    ox = slot("ox", 9)
    xh2, xl2 = slot("xh2", 12, dt=F32R), slot("xl2", 14, dt=F32R)
    logs()
    t_gr = act(gms[:, :, :], gms[:, :, :], ACT.Ln, scale=1.0 / 256, bias=epsc[:, 0:1], after=[ms_t[3]])
    t_gr = act(gms[:, :, :], gms[:, :, :], ACT.Exp, scale=-0.5, after=[t_gr])

    def g_out(i):
        w = tmp[i % 2]
        t = dve(DVE.scalar_tensor_tensor, out=w[:, :], in0=og[:, i, :], scalar=gain("g_gla_2", i % 2), in1=gms[:, i // 2, :],
                op0=ALU.mult, op1=ALU.mult, after=[t_gr, y.get(("g", i - 2))])
        t = dve(DVE.tensor_tensor, w[:, :], w[:, :], sz[:, i, :], ALU.mult, after=[t, tok["gz", i]])
        t1 = act(yh[:, i, :], w[:, :], ACT.Copy, after=[t, dsa_done])
        y["g", i] = dve(DVE.tensor_tensor, yl[:, i, :], w[:, :], yh[:, i, :].bitcast(F32), ALU.subtract,
                        after=[t1, dsa_done])

    def x_start(i):
        wait(PE, free[4], tok["xq", 2 * i + 1])
        for j, c in ((1, 0), (0, 256)):
            for k_ in range(2):
                m = PE.matmul(bank[4][:, c:c + 256], xq[:, 2 * i + k_, j * P:(j + 1) * P], mk[:, 2 * i + k_, :],
                              start=k_ == 0, stop=k_ == 1, skip_group_check=True)
        t = last_pe(m)
        n = head_n[0]
        head_n[0] += 1
        Lb, s_ = L[n % 2], stat[:, n % 16, :]
        t = dve(DVE.tensor_scalar, Lb[:, :], bank[4][:, :], -1.0, None, ALU.mult, after=[t, L_free[n % 2]])
        free[4] = t
        t = dve(DVE.tensor_reduce, s_[:, 0:2], Lb[:, :].rearrange("p (a b) -> p a b", a=2), AX, ALU.min, after=[t])
        return n, softmax_tail(Lb, [(0, 256), (256, 512)], None, t, None, s_)

    def x_middle(i, s):
        return s[0], turn(s[0], s[1], 5, [(256, 0), (0, 128), (384, 256), (128, 384)], 512)

    def x_end(i, s):
        n, t_t = s
        wait(PE, t_t)
        for m_ in range(2):
            b = 6 + m_
            wait(PE, free[b])
            c = i * 256 + m_ * P
            PE.matmul(bank[b][:, 0:S], mv[:, 0, c:c + P], PT[n % 2][:, 0:256], start=True, stop=False)
            t = last_pe(PE.matmul(bank[b][:, 0:S], mv[:, 1, c:c + P], PT[n % 2][:, 256:512], start=False, stop=True))
            PT_free[n % 2] = t
            free[b] = y["x", 2 * i + m_] = act(ox[:, 2 * i + m_, :], bank[b][:, 0:S], ACT.Copy, after=[t])
        g_out(2 * i)
        g_out(2 * i + 1)

    def to_zx(n, ps, t):
        tok["zx", n] = dve(DVE.tensor_copy, zx[:, n, :], ps, after=[t])
        return tok["zx", n]

    wait(PE, mk_tok[3], mv_tok[3])
    wait(DVE, gdone[3])
    pipeline(4, x_start, x_middle, x_end, {i: lambda i=i: cols("xz", i, x, (2, 3), to_zx) for i in range(4)})
    t_zx = act(zx[:, :, :], zx[:, :, :], ACT.Silu, after=[tok["zx", 7], y["x", 7]])

    def x_out(a):
        b = a + 2
        t = dve(DVE.tensor_tensor, ox[:, a:b, :], ox[:, a:b, :], zx[:, a:b, :], ALU.mult, after=[t_zx, y["x", 7]])
        t1 = act(xh2[:, a:b, :], ox[:, a:b, :], ACT.Copy, after=[t])
        y["x2"] = dve(DVE.tensor_tensor, xl2[:, a:b, :], ox[:, a:b, :], xh2[:, a:b, :].bitcast(F32), ALU.subtract,
                      after=[t1, y["g", 7]])

    wait(PE, y["g", 7])
    for n in range(4):
        cols("tg", n, x, (4, 5), to_g)
        cols("wg", n, Y, (6, 7), to_m(False))
        x_out(2 * n)

    fh, fl = slot("fh", 6, dt=F32R), slot("fl", 7, dt=F32R)
    f_tok = {}
    wait(PE, y["x2"])

    def last_in(n):
        t1 = act(fh[:, n, :], merged[:, n, :], ACT.Copy, after=[m_tok[n]])
        f_tok[n] = dve(DVE.tensor_tensor, fl[:, n, :], merged[:, n, :], fh[:, n, :].bitcast(F32), ALU.subtract, after=[t1])

    def last_rows(i):
        wait(PE, f_tok[2 * i + 1])
        return rows("wf", i, 4, fh[:, 2 * i:2 * i + 2, :], fl[:, 2 * i:2 * i + 2, :])

    for n in range(4):
        cols("tx", n, x, (4, 5), to_g)
        if n:
            last_rows(n - 1)
        cols("wx", n, (xh2, xl2), (6, 7), to_m(False))
        last_in(2 * n)
        last_in(2 * n + 1)
    done = last_rows(3)
    res = slot("res", 9)
    t_cp = []
    for j in range(NC):
        t_cp.append(dve(DVE.tensor_copy, res[:, j, :], bank[j // 2][:, (j % 2) * S:(j % 2 + 1) * S], after=[done[j // 2]]))
    t_r, _ = mean_square(res, ready=t_cp)
    outT = out.rearrange("(j p) s -> p j s", p=P)
    t_g = gained(res, "g_post_2", 0, res, t_cp, after=[t_r])
    for a in range(0, NC, 2):
        b = a + 2
        t = dve(DVE.tensor_tensor, res[:, a:b, :], res[:, a:b, :], rstd[:, :].unsqueeze(1).to_broadcast([P, 2, S]), ALU.mult,
                after=[t_r, *t_g[a:b]])
        t = dve(DVE.tensor_tensor, res[:, a:b, :], res[:, a:b, :], h[:, a:b, :], ALU.add, after=[t])
        wait(SP, t)
        t_out = inc(SP.dma_start(outT[:, a:b, :], res[:, a:b, :]), c_out, 16)
    assert used[0] == len(PLAN)
    wait(SP, t_out)
    ctx.close()


def bucket(d):
    if d < 16:
        return d
    return min(31, 16 + int(log(d / 16) / log(8) * 16))


def constants():
    f = np.float32
    selA = np.zeros((P, 2, 384), f)
    selB = np.zeros((32, 384), f)
    for i in range(383):
        n = min(max(255 - i, -128), 128) + 128 - 1
        selA[n % P, n // P, i] = 1
        selB[bucket(max(255 - i, 0)), i] = 1
    p, c = np.arange(P)[:, None], np.arange(384)[None, :]
    key = np.where(c < 256, c, c - 256)
    query = np.where(c < 256, p + P, p)
    s, t = np.arange(P)[:, None], np.arange(P)[None, :]
    return {
        "selA": selA, "selB": selB, "ones": np.ones((P, P), f), "ident": np.eye(P, dtype=f), "flip": np.eye(P, dtype=f)[::-1].copy(),
        "gmask": ((s <= t) & (s // 64 == t // 64)).astype(f),
        "reset": np.tile((np.arange(S) % 64 != 0).astype(f), (P, 1)),
        "cm": np.where(key > query, f(GONE), f(0)).astype(f),
    }


def by_cols(w):
    return np.ascontiguousarray(w.reshape(NC, P, -1, 256).transpose(2, 1, 0, 3)).reshape(-1, P, TILE)


def by_rows(w):
    return np.ascontiguousarray(w.reshape(-1, 2, P, D).transpose(0, 2, 1, 3)).reshape(-1, P, TILE)


def feature(x):
    return np.ascontiguousarray(x.T.reshape(NC, P, S).transpose(1, 0, 2))


def kernel(**inputs):
    import concourse.bacc as _bacc
    from concourse.bass_utils import run_bass_kernel_spmd as _run

    a = {k: np.asarray(v) for k, v in inputs.items()}
    qkv, win, w1, w2 = a["attn_w_qkv"][0], a["w_in_2"][0], a["mlp_w1"], a["mlp_w2"]
    cuts = np.cumsum([0, 512, 512, 1024, 16, 1024, 1024, 256, 256, 512, 64, 8, 1024, 1024, 1024, 1024, 1024, 1024])
    gq, gk, gv, ga, gz, dq, dk, dv, iq, ik, iw, dz, xq, xz, ta, tg, tx = [win[:, cuts[i]:cuts[i + 1]] for i in range(17)]
    misc = np.concatenate([ik, ik, ga, iw, np.zeros((D, 104), win.dtype)], axis=1)
    arrays = {
        "wv": by_cols(qkv[:, 2 * D:]), "wk": by_cols(qkv[:, D:2 * D]), "wq": by_cols(qkv[:, :D]),
        "wo": by_rows(a["attn_w_o"][0]), "w1_0": by_cols(w1[0]), "w2_0": by_rows(w2[0]), "w1_1": by_cols(w1[1]),
        "w2_1": by_rows(w2[1]), "rin": by_cols(a["rec_w_in"][0]), "rout": by_rows(a["rec_w_o"][0]),
        "misc": by_cols(misc), "iq": by_cols(iq), "dk": by_cols(dk), "dv": by_cols(dv), "dq": by_cols(dq),
        "gq": by_cols(gq), "gk": by_cols(gk), "gv": by_cols(gv), "dz": by_cols(dz), "ta": by_cols(tg), "wd": by_cols(a["w_dsa_out_2"][0]),
        "xq": by_cols(xq), "gz": by_cols(gz), "tg": by_cols(ta), "wg": by_cols(a["w_gla_out_2"][0]),
        "mk": by_cols(a["w_mem_kv_2"][0][:, :D]), "mv": by_cols(a["w_mem_kv_2"][0][:, D:]), "xz": by_cols(xz),
        "tx": by_cols(tx), "wx": by_cols(a["w_x_out_2"][0]), "wf": by_rows(a["w_o_2"][0]),
        "xT": feature(a["x"][0]), "memT": feature(a["mem_2"][0]),
        "gatew": np.ascontiguousarray(np.stack([a["rec_w_ga"][0], a["rec_w_gx"][0]]).transpose(2, 0, 1, 3)),
        "vec": np.ascontiguousarray(np.concatenate([a[n].reshape(-1, P) for n, _ in VEC]).T),
        "relT": np.ascontiguousarray(a["attn_rel_bias"][0][:, 1:].T.reshape(2, P, 16).transpose(1, 0, 2)),
        "rel_bias_2": a["rel_bias_2"], "w_gla_a_up_2": a["w_gla_a_up_2"], **constants(),
    }
    nc = _bacc.Bacc("TRN2", target_bir_lowering=False, num_devices=1)
    A = {n: nc.dram_tensor(f"in_{n}", v.shape, F32, kind="ExternalInput").ap() for n, v in arrays.items()}
    A["scratch"] = nc.dram_tensor("scratch", (24, 384), F32).ap()
    out = nc.dram_tensor("out_0", (D, S), F32, kind="ExternalOutput").ap()
    build(nc, A, out)
    r = _run(nc, [{f"in_{n}": v for n, v in arrays.items()}], core_ids=[0])
    return np.ascontiguousarray(r.results[0]["out_0"].T).reshape(1, S, D)
```

```python
from contextlib import ExitStack
from math import log

import numpy as np

import concourse.bass as bass
from concourse import mybir

P = 128
S = 256
D = 1024
NC = D // P
F32 = mybir.dt.float32
F32R = mybir.dt.float32r
ALU = mybir.AluOpType
ACT = mybir.ActivationFunctionType
AX = mybir.AxisListType.X

RAW, HIS = 5, 3
PITCH, COPIES = 383, 32
TILE = 2048
NEG = -1e30
GONE = -3e38
TAKEN = -3.4e38

VEC = [("norm_mix", 16), ("norm_mlp", 16), ("norm_final", 8), ("rec_b_in", 16), ("rec_conv_w", 32),
       ("rec_conv_b", 8), ("rec_b_ga", 8), ("rec_b_gx", 8), ("rec_a_param", 8), ("rec_b_o", 8),
       ("g_pre_2", 8), ("g_post_2", 8), ("g_mem_2", 8), ("b_gla_a_2", 4), ("g_gla_2", 2)]
VCOL = {}
for _name, _n in VEC:
    VCOL[_name] = sum(n for _, n in VEC[:len(VCOL)])
NV = sum(n for _, n in VEC)



def mlp_plan(n):
    out = [(f"w1_{n}", 0)]
    for i in range(1, 16):
        out += [(f"w1_{n}", i), (f"w2_{n}", i - 1)]
    return out + [(f"w2_{n}", 15)]


def plan():
    out = [("wv", i) for i in range(4)] + [("wk", 0), ("wq", 0)]
    for i in range(1, 4):
        out += [("wk", i), ("wq", i)]
    out += [("wo", i) for i in range(4)] + [("mk", 0)] + mlp_plan(0) + [("mk", 1)]
    out += [("rin", i) for i in range(8)] + [("mk", 2)] + [("rout", i) for i in range(4)]
    out += [("mk", 3)] + mlp_plan(1) + [("mv", 0), ("mv", 1)]
    out += [("iq", 0), ("misc", 0), ("iq", 1), ("dk", 0), ("dv", 0)] + [("dq", i) for i in range(4)] + [("mv", 2), ("mv", 3)]
    out += [("gq", 0), ("gq", 1), ("gk", 0), ("gk", 1)] + [("gv", i) for i in range(3)]
    out += [("dz", i) for i in range(4)] + [("gv", 3)] + [("xq", i) for i in range(4)] + [("gz", i) for i in range(4)]
    for i in range(4):
        out += [("ta", i), ("wd", i)]
    out += [("xz", i) for i in range(4)]
    for i in range(4):
        out += [("tg", i), ("wg", i)]
    out += [("tx", 0), ("wx", 0)]
    for i in range(1, 4):
        out += [("tx", i), ("wf", i - 1), ("wx", i)]
    return out + [("wf", 3)]


PLAN = plan()


class Count:

    def __init__(self, sem):
        self.sem, self.n = sem, 0


def build(nc, A, out):
    ctx = ExitStack()
    PE, ACTE, DVE, POOL, SP = nc.tensor, nc.scalar, nc.vector, nc.gpsimd, nc.sync

    def sem(name):
        return Count(ctx.enter_context(nc.semaphore(name)))

    c_hi, c_lo, c_w = sem("hi"), sem("lo"), sem("wdone")
    c_pe, c_act, c_dve, c_pool = sem("pe"), sem("act"), sem("dve"), sem("pool")
    c_raw = [sem(f"raw{i}") for i in range(RAW)]
    c_in = sem("inputs")
    c_tab, c_tab2, c_toep, c_toep2, c_out = sem("tab"), sem("tab2"), sem("toep"), sem("toep2"), sem("out")
    c_gw, c_late, c_mem, c_one, c_vec = sem("gatew"), sem("late"), sem("mem"), sem("one"), sem("vec")
    c_x0, c_x1, c_x2, c_x3 = sem("x0"), sem("x1"), sem("x2"), sem("x3")

    waited = {}

    def wait(eng, *toks):
        for tok in toks:
            if tok is None:
                continue
            c, n = tok
            if waited.get((id(eng), id(c)), 0) < n:
                waited[(id(eng), id(c))] = n
                eng.wait_ge(c.sem, n)

    def inc(ins, c, k=1):
        c.n += k
        ins.then_inc(c.sem, k)
        return (c, c.n)

    def act(o, i, f, after=(), **k):
        wait(ACTE, *after)
        return inc(ACTE.activation(o, i, f, **k), c_act)

    def dve(op, *a, after=(), **k):
        wait(DVE, *after)
        return inc(op(*a, **k), c_dve)

    def pool(op, *a, after=(), **k):
        wait(POOL, *after)
        return inc(op(*a, **k), c_pool)

    def last_pe(ins):
        return inc(ins, c_pe)

    base = (nc.sbuf_base + 63) // 64 * 64
    top = [base]

    def region(n):
        at = top[0]
        top[0] += n
        assert top[0] <= nc.sbuf_usable_end, top[0]
        return at

    def place(name, off, free, dt=F32):
        return nc.alloc_sbuf_tensor_at(name, [P] + list(free), dt, offset=off)

    o_raw = region(RAW * 4 * TILE)
    o_hi = region(HIS * 4 * TILE)
    o_slot = [region(8192) for _ in range(15)]
    raw = [place(f"raw_{i}", o_raw + i * 8192, [TILE]) for i in range(RAW)]
    lo = [place(f"lo_{i}", o_raw + i * 8192, [TILE], F32R) for i in range(RAW)]
    hi = [place(f"hi_{i}", o_hi + i * 8192, [TILE], F32R) for i in range(HIS)]

    def slot(name, i, free=(NC, S), dt=F32, off=0):
        return place(name, o_slot[i] + off, free, dt)

    def small(name, free, dt=F32):
        n = 4
        for f in free:
            n *= f
        return place(name, region((n + 31) // 32 * 32), free, dt)

    vec = small("vec", [NV])
    ones = small("ones", [P])
    ident = small("ident", [P])
    gmask = small("gmask", [P])
    reset = small("reset", [S])
    o_sq = region(4 * 1024)
    sq = [place(f"sq{i}", o_sq + 1024 * i, [S]) for i in range(4)]
    rms_t = small("rms_t", [S])
    rstd = small("rstd", [S])
    L = [small(f"L{i}", [512]) for i in range(2)]
    PT = [small(f"PT{i}", [512]) for i in range(2)]
    stat = small("stat", [16, 8])
    o_tmp = region(5 * 1024)
    tmp = [place(f"tmp{i}", o_tmp + 1024 * i, [S]) for i in range(5)]
    epsc = small("epsc", [1])
    dec = small("dec", [4, 4])

    bank = [ctx.enter_context(nc.psum_tensor(f"bank{i}", [P, 512], F32)) for i in range(8)]

    def gain(name, j):
        return vec[:, VCOL[name] + j:VCOL[name] + j + 1]

    issued, used = [0], [0]
    hi_tok, lo_tok, raw_tok, w_tok = {}, {}, {}, {}

    def issue_dma(u):
        name, i = PLAN[u]
        if u >= RAW:
            wait(SP, w_tok[u - RAW])
        raw_tok[u] = inc(SP.dma_start(raw[u % RAW][:, :], A[name][i]), c_raw[u % RAW], 16)

    def piece(x, g):
        return x[:, (g % 2) * (TILE // 2):(g % 2 + 1) * (TILE // 2)]

    def cut_hi():
        g = len(hi_tok)
        u = g // 2
        if issued[0] == u:
            issue_dma(u)
            issued[0] += 1
        if u >= HIS:
            wait(ACTE, w_tok[u - HIS])
        wait(ACTE, raw_tok[u])
        hi_tok[g] = inc(ACTE.activation(piece(hi[u % HIS], g), piece(raw[u % RAW], g), ACT.Copy), c_hi)

    def cut_lo():
        g = len(lo_tok)
        u = g // 2
        wait(DVE, hi_tok[g])
        lo_tok[g] = inc(DVE.tensor_tensor(piece(lo[u % RAW], g), piece(raw[u % RAW], g), piece(hi[u % HIS], g).bitcast(F32),
                                          ALU.subtract), c_lo)

    def flush():
        while len(lo_tok) < len(hi_tok):
            cut_lo()

    def more():
        while len(hi_tok) < 2 * min(used[0] + HIS, len(PLAN)):
            cut_hi()

    def ahead(n):
        while len(hi_tok) < n:
            cut_hi()
        flush()

    def advance():
        while issued[0] < min(used[0] + RAW, len(PLAN)):
            issue_dma(issued[0])
            issued[0] += 1
        flush()
        more()

    def advance_half():
        while issued[0] < min(used[0] + RAW, len(PLAN)):
            issue_dma(issued[0])
            issued[0] += 1
        if len(lo_tok) < len(hi_tok):
            cut_lo()
        if len(hi_tok) < 2 * min(used[0] + HIS, len(PLAN)):
            cut_hi()

    def take(name, i, run=True):
        t = used[0]
        assert PLAN[t] == (name, i), (PLAN[t], name, i)
        if run:
            advance()
        while len(hi_tok) < 2 * t + 2:
            cut_hi()
        while len(lo_tok) < 2 * t + 2:
            cut_lo()
        wait(PE, lo_tok[2 * t])
        return hi[t % HIS], lo[t % RAW]

    def give(ins):
        w_tok[used[0]] = inc(ins, c_w)
        used[0] += 1
        return w_tok[used[0] - 1]

    def mm3(o, ah, al, bh, bl, start, stop, skip=False):
        PE.matmul(o, ah, bh, start=start, stop=False, skip_group_check=skip)
        PE.matmul(o, ah, bl, start=False, stop=False, skip_group_check=skip)
        return PE.matmul(o, al, bh, start=False, stop=stop, skip_group_check=skip)

    free = [None] * 8

    def block(tile, x, j, b, by_tokens, k):
        wh, wl = tile
        xh, xl = x
        o = bank[b][:, 0:S]
        if k == NC // 2:
            wait(PE, lo_tok[2 * used[0] + 1])
        if by_tokens:
            r = slice(j * P, (j + 1) * P)
            return mm3(o, xh[:, k, r], xl[:, k, r], wh[:, k * 256:(k + 1) * 256], wl[:, k * 256:(k + 1) * 256],
                       k == 0, k == NC - 1)
        c = k * 256 + j * 128
        return mm3(o, wh[:, c:c + P], wl[:, c:c + P], xh[:, k, :], xl[:, k, :], k == 0, k == NC - 1)

    def halves(name, i, x, banks, by_tokens):
        tile = []

        def half(j):
            if j == 0:
                tile.append(take(name, i, False))
            wait(PE, free[banks[j]])
            for k in range(NC):
                m = block(tile[0], x, j, banks[j], by_tokens, k)
            return last_pe(m) if j == 0 else give(m)

        return half

    def both(name, i, x, banks, evac, by_tokens, ready):
        tile = take(name, i)
        t = [None, None]
        if ready is None:
            for j in range(2):
                b = banks[j]
                wait(PE, free[b])
                for k in range(NC):
                    m = block(tile, x, j, b, by_tokens, k)
                t = last_pe(m) if j == 0 else give(m)
                free[b] = evac(j, bank[b][:, 0:S], t)
        else:
            wait(PE, free[banks[0]], free[banks[1]])
            for k in range(NC):
                wait(PE, ready[k])
                for j in range(2):
                    m = block(tile, x, j, banks[j], by_tokens, k)
                    if j == 0 and k == NC - 1:
                        t0 = last_pe(m)
            t1 = give(m)
            free[banks[0]] = evac(0, bank[banks[0]][:, 0:S], t0)
            free[banks[1]] = evac(1, bank[banks[1]][:, 0:S], t1)

    def cols(name, i, x, banks, evac, ready=None):
        both(name, i, x, banks, lambda j, ps, t: evac(2 * i + j, ps, t), False, ready)

    def toks(name, i, x, banks, evac, ready=None):
        both(name, i, x, banks, lambda j, ps, t: evac(i, j, ps, t), True, ready)

    def rows(name, i, n, xh, xl, part=None, done=None, ready=(None, None)):
        if part is not None:
            advance_half()
        wh, wl = take(name, i, part is None)
        done = done or []
        for k in range(2):
            wait(PE, lo_tok[2 * used[0] + k], ready[k])
            for j in range(NC) if part is None else range(4 * part, 4 * part + 4):
                if i == 0 and k == 0:
                    wait(PE, free[j // 2])
                c = k * 1024 + j * 128
                m = mm3(bank[j // 2][:, (j % 2) * S:(j % 2 + 1) * S], wh[:, c:c + P], wl[:, c:c + P], xh[:, k, :], xl[:, k, :],
                        i == 0 and k == 0 and j % 2 == 0, i == n - 1 and k == 1, skip=True)
                if i == n - 1 and k == 1 and j % 2:
                    done.append(last_pe(m) if j < NC - 1 else give(m))
        if i < n - 1 and part != 0:
            give(m)
        return done

    def in_steps(name, i, x, banks, evac, by_tokens=False):
        half = halves(name, i, x, banks, by_tokens)

        def step(j):
            advance_half()
            t = half(j)
            b = banks[j]
            ps = bank[b][:, 0:S]
            free[b] = evac(i, j, ps, t) if by_tokens else evac(2 * i + j, ps, t)

        return [lambda: step(0), lambda: step(1)]

    def load(dst, src):
        return inc(SP.dma_start(dst, src), c_in, 16)

    h = slot("h", 0)
    t_eps = dve(DVE.memset, epsc[:, :], 1e-6)
    t_h = [inc(SP.dma_start(h[:, 2 * j:2 * j + 2, :], A["xT"][:, 2 * j:2 * j + 2, :]), c, 16)
           for j, c in enumerate([c_x0, c_x1, c_x2, c_x3])]
    t_one = inc(SP.dma_start(ones[:, :], A["ones"]), c_one, 16)
    t_vec = inc(SP.dma_start(vec[:, :], A["vec"]), c_vec, 16)
    issue_dma(0)
    issued[0] = 1
    load(ident[:, :], A["ident"])
    relT = slot("relT", 14, [2, 16])
    selA = slot("selA", 14, [2, 384], off=256)
    selB = slot("selB", 14, [384], off=3584)
    relB = slot("relB", 14, [8], off=5120)
    load(relT[:, :, :], A["relT"])
    load(selA[:, :, :], A["selA"])
    load(selB[0:32, :], A["selB"])
    load(relB[0:32, :], A["rel_bias_2"])
    load(gmask[:, :], A["gmask"])
    t_in = load(reset[:, :], A["reset"])
    mem = slot("mem", 6)
    mh, ml = slot("mh", 12, dt=F32R), slot("ml", 13, dt=F32R)
    issue_dma(1)
    issued[0] = 2
    t_mem = inc(SP.dma_start(mem[:, :, :], A["memT"]), c_mem, 16)
    while issued[0] < RAW - 1:
        issue_dma(issued[0])
        issued[0] += 1

    sq_read = [None] * 4

    def logs():
        ACTE.preload_act_table_set("natural_log_exp_and_others")

    def mean_square(src, add=None, ready=None, after=(), hooks=()):
        acc, t_src, ts = sq[3], [], {}
        t_acc = None
        alone = 6 if hooks else 4

        def total(j):
            if j == alone:
                wait(PE, free[6])
            wait(PE, ts[j])
            sq_read[j % 3] = last_pe(PE.matmul(bank[6][:, 0:S], ones[:, :], sq[j % 3][:, :], start=j == alone, stop=j == NC - 1))
            if j == 6:
                wait(PE, t_acc)
                sq_read[3] = last_pe(PE.matmul(bank[6][:, 0:S], ones[:, :], acc[:, :], start=False, stop=False))

        for j in range(NC):
            t = ready[j] if ready else None
            if add is not None:
                done, bias = add
                i1 = bank[j // 2][:, (j % 2) * S:(j % 2 + 1) * S]
                if bias is None:
                    t = dve(DVE.tensor_tensor, src[:, j, :], i1, src[:, j, :], ALU.add, after=[done[j // 2]])
                else:
                    t = dve(DVE.scalar_tensor_tensor, out=src[:, j, :], in0=i1, scalar=gain(bias, j),
                            in1=src[:, j, :], op0=ALU.add, op1=ALU.add, after=[done[j // 2]])
                free[j // 2] = t
            t_src.append(t)
            if j == 0:
                t_acc = act(acc[:, :], src[:, j, :], ACT.Square, after=[t, sq_read[3], *after])
                continue
            t = act(sq[j % 3][:, :], src[:, j, :], ACT.Square, after=[t, sq_read[j % 3], *after])
            if j < alone:
                t_acc = pool(POOL.tensor_tensor, acc[:, :], acc[:, :], sq[j % 3][:, :], ALU.add, after=[t, t_acc])
                sq_read[j % 3] = t_acc
            else:
                ts[j] = t
                if not hooks:
                    total(j)
        if hooks:
            hooks[0]()
            total(6)
            total(7)
        t_ms = sq_read[1]
        if hooks:
            hooks[1]()
        else:
            more()
        t = act(rms_t[:, :], bank[6][:, 0:S], ACT.Ln, scale=1.0 / D, bias=epsc[:, 0:1], after=[t_ms, t_eps])
        free[6] = t
        t_r = act(rstd[:, :], rms_t[:, :], ACT.Exp, scale=-0.5, after=[t])
        return t_r, t_src

    def gained(src, name, g0, dst, t_src, after=()):
        return [dve(DVE.tensor_scalar, dst[:, j, :], src[:, j, :], gain(name, g0 + j), None, ALU.mult,
                    after=[t_src[j], *after]) for j in range(NC)]

    GROUPS = [(0, 1), (1, 2), (2, 4), (4, 6), (6, 8)]

    def spread(hg, t_g, x, t_r, after=(), mid=None):
        xh, xl = x
        ready, t_m = {}, {}

        def product(g):
            a, b = GROUPS[g]
            t_m[g] = dve(DVE.tensor_tensor, hg[:, a:b, :], hg[:, a:b, :], rstd[:, :].unsqueeze(1).to_broadcast([P, b - a, S]),
                         ALU.mult, after=[t_r, *t_g[a:b]])

        product(0)
        for g, (a, b) in enumerate(GROUPS):
            t = act(xh[:, a:b, :], hg[:, a:b, :], ACT.Copy, after=[t_m[g], *after])
            if g + 1 < len(GROUPS):
                product(g + 1)
            t = dve(DVE.tensor_tensor, xl[:, a:b, :], hg[:, a:b, :], xh[:, a:b, :].bitcast(F32), ALU.subtract, after=[t])
            for j in range(a, b):
                ready[j] = t
            if g == 1 and mid:
                mid()
        return ready

    def norm(src, name, g0, x, hg, add=None, ready=None, fill=None, after=(), hooks=(), preload=True, mid=None):
        if fill:
            half, banks, evac = fill
            f0 = half(0)
        if preload:
            logs()
        t_g = []
        if not hooks:
            flush()
        if ready and src is not hg and hooks:
            t_g = gained(src, name, g0, hg, [ready[j] for j in range(NC)], after)
        t_r, t_src = mean_square(src, add, ready, after, hooks)
        if fill:
            f1 = half(1)
        t_g = t_g or gained(src, name, g0, hg, t_src, after)
        out = spread(hg, t_g, x, t_r, after, mid)
        flush()
        if fill:
            free[banks[0]] = evac(0, bank[banks[0]][:, 0:S], f0)
            free[banks[1]] = evac(1, bank[banks[1]][:, 0:S], f1)
            more()
        return out

    def norm_late(src, name, g0, x, hg, add, fill):
        half, banks, evac = fill
        (done, bias), (xh, xl) = add, x
        f0, f1 = half(0), half(1)
        flush()
        logs()
        ready, t_sq, t_acc, low = {}, {}, None, None

        def sub(a, b, t):
            t = dve(DVE.tensor_tensor, xl[:, a:b, :], hg[:, a:b, :], xh[:, a:b, :].bitcast(F32), ALU.subtract, after=[t])
            for j in range(a, b):
                ready[j] = t

        for a, b in GROUPS:
            if a == 4:
                while len(hi_tok) < 2 * (used[0] + HIS - 1):
                    cut_hi()
            t_src = {}
            for j in range(a, b):
                i1 = bank[j // 2][:, (j % 2) * S:(j % 2 + 1) * S]
                if bias is None:
                    t = dve(DVE.tensor_tensor, src[:, j, :], i1, src[:, j, :], ALU.add, after=[done[j // 2]])
                else:
                    t = dve(DVE.scalar_tensor_tensor, out=src[:, j, :], in0=i1, scalar=gain(bias, j),
                            in1=src[:, j, :], op0=ALU.add, op1=ALU.add, after=[done[j // 2]])
                free[j // 2] = t_src[j] = t
                t = dve(DVE.tensor_scalar, hg[:, j, :], src[:, j, :], gain(name, g0 + j), None, ALU.mult, after=[t])
            if low:
                sub(*low)
            low = (a, b, act(xh[:, a:b, :], hg[:, a:b, :], ACT.Copy, after=[t]))
            for j in range(a, b):
                s = sq[3] if j == 0 else sq[j % 3]
                r = 3 if j == 0 else j % 3
                t_sq[j] = act(s[:, :], src[:, j, :], ACT.Square, after=[t_src[j], sq_read[r]])
                if 0 < j < 6:
                    t_acc = sq_read[r] = pool(POOL.tensor_tensor, sq[3][:, :], sq[3][:, :], s[:, :], ALU.add,
                                              after=[t_sq[0], t_sq[j], t_acc])
        sub(*low)
        flush()
        free[banks[0]] = evac(0, bank[banks[0]][:, 0:S], f0)
        free[banks[1]] = evac(1, bank[banks[1]][:, 0:S], f1)
        more()

        def finish():
            wait(PE, free[6])
            for n, (s, t) in enumerate([(3, t_acc), (0, t_sq[6]), (1, t_sq[7])]):
                wait(PE, t)
                sq_read[s] = t = last_pe(PE.matmul(bank[6][:, 0:S], ones[:, :], sq[s][:, :], start=n == 0, stop=n == 2))
            free[6] = act(rms_t[:, :], bank[6][:, 0:S], ACT.Ln, scale=1.0 / D, bias=epsc[:, 0:1], after=[t])
            return act(rstd[:, :], rms_t[:, :], ACT.Exp, scale=-0.5, after=[free[6]])

        return ready, finish

    x = (slot("xh", 1, dt=F32R), slot("xl", 2, dt=F32R))
    hg = slot("hg", 2)

    wait(PE, t_one)
    wait(DVE, t_vec)
    tab_dram = A["scratch"]

    def tables():
        wait(PE, t_in)
        PE.matmul(bank[7][0:16, 0:384], relT[:, 0, :], selA[:, 0, :], start=True, stop=False)
        PE.matmul(bank[7][0:16, 0:384], relT[:, 1, :], selA[:, 1, :], start=False, stop=True)
        return last_pe(PE.matmul(bank[3][0:8, 0:384], relB[0:32, :], selB[0:32, :], start=True, stop=True))

    t_tm = []
    ready = norm(h, "norm_mix", 0, x, hg, ready=[t_h[j // 2] for j in range(NC)],
                 hooks=[lambda: None, lambda: (t_tm.append(tables()), ahead(1))], mid=lambda: ahead(2))

    def softmax_tail(Lb, tiles, mx, t_max, src_neg, st):
        t = t_max
        for n, (a, b) in enumerate(tiles):
            t = act(Lb[:, a:b], Lb[:, a:b], ACT.Exp, scale=-1.0, bias=st[:, n:n + 1], accum_out=st[:, 2 + n:3 + n],
                    after=[t_max])
        t = dve(DVE.reciprocal, st[:, 4:6], st[:, 2:4], after=[t])
        for n, (a, b) in enumerate(tiles):
            t2 = dve(DVE.tensor_scalar, Lb[:, a:b], Lb[:, a:b], st[:, 4 + n:5 + n], None, ALU.mult, after=[t])
        return t2

    TT = [(0, 256), (256, 384)]
    head_n = [0]
    L_free, PT_free = [None, None], [None, None]

    def scores(qT, kT, sb_):
        wait(PE, free[sb_])
        PE.matmul(bank[sb_][:, 0:256], qT[:, P:S], kT, start=True, stop=True)
        return last_pe(PE.matmul(bank[sb_][:, 256:384], qT[:, 0:P], kT[:, 0:P], start=True, stop=True, skip_group_check=True))

    both_ = [place(f"both{i}", o_tmp + 2048 + 1536 * i, [384]) for i in range(2)]
    L_read = {}

    def soft(t_s, sb_, bias, mask, t_b):
        n = head_n[0]
        head_n[0] += 1
        Lb, st = L[n % 2], stat[:, n % 16, :]
        if mask is None:
            for a, (o, e, c) in enumerate([(0, 256, 0), (256, 384, 128)]):
                t = dve(DVE.tensor_tensor_reduce, out=Lb[:, o:e], in0=bank[sb_][:, o:e], in1=bias[:, c:256], scale=-1.0,
                        scalar=3.4e38, op0=ALU.add, op1=ALU.min, accum_out=st[:, a:a + 1], after=[t_s, t_b, L_free[n % 2]])
            free[sb_] = t
        else:
            for o, e, c in [(0, 256, 0), (256, 384, 128)]:
                t = pool(POOL.tensor_tensor, both_[n % 2][:, o:e], bias[:, c:256], mask[:, o:e], ALU.add, after=[t_b, L_read.get(n - 2)])
            for a, (o, e) in enumerate(TT):
                t = dve(DVE.tensor_tensor_reduce, out=Lb[:, o:e], in0=bank[sb_][:, o:e], in1=both_[n % 2][:, o:e], scale=-1.0,
                        scalar=3.4e38, op0=ALU.add, op1=ALU.min, accum_out=st[:, a:a + 1], after=[t_s, t, L_free[n % 2]])
            free[sb_] = L_read[n] = t
        return n, softmax_tail(Lb, TT, None, t, None, st)

    def turn(n, t_p, pb, blocks, width):
        wait(PE, t_p, free[pb])
        for src, dst in blocks:
            m = PE.transpose(bank[pb][:, dst:dst + P], L[n % 2][:, src:src + P], ident[:, :])
        t = last_pe(m)
        L_free[n % 2] = t
        t2 = act(PT[n % 2][:, 0:width], bank[pb][:, 0:width], ACT.Copy, after=[t, PT_free[n % 2]])
        free[pb] = t2
        return t2

    CAUSAL = [(256, 0), (0, 128), (128, 256)]

    def weigh(n, t_t, o, V, lo_, hi_):
        wait(PE, t_t)
        PE.matmul(o, V[:, 0, lo_:hi_], PT[n % 2][:, 0:256], start=True, stop=False)
        t = last_pe(PE.matmul(o[:, P:S], V[:, 1, lo_:hi_], PT[n % 2][:, 256:384], start=False, stop=True))
        PT_free[n % 2] = t
        return t

    q, k = slot("q", 5), slot("k", 6)
    v = slot("v", 7, [2, D])
    oh, ol = slot("oh", 10, dt=F32R), slot("ol", 11, dt=F32R)

    def to_v(i, j, ps, t):
        return dve(DVE.tensor_copy, v[:, j, i * 256:(i + 1) * 256], ps, after=[t])

    def to_k(n, ps, t):
        return act(k[:, n, :], ps, ACT.Copy, after=[t])

    q_tok = {}

    def to_q(n, ps, t):
        q_tok[n] = act(q[:, n, :], ps, ACT.Copy, scale=0.125, after=[t])
        return q_tok[n]

    tabA = slot("tabA", 11, [384])
    tabB = slot("tabB", 11, [384], off=2048)
    t1 = dve(DVE.tensor_copy, tabA[0:16, :], bank[7][0:16, 0:384], after=t_tm)
    t2 = dve(DVE.tensor_copy, tabB[0:8, :], bank[3][0:8, 0:384], after=t_tm)
    free[7], free[3] = t1, t2
    t_tab = []
    for n0, n, tab, c in ((0, 16, tabA, c_tab), (16, 8, tabB, c_tab2)):
        wait(POOL, t2)
        t_tab.append(inc(POOL.dma_start(bass.AP(tab_dram.tensor, n0 * COPIES * PITCH,
                                                [[COPIES * PITCH, n], [PITCH, COPIES], [1, PITCH]]),
                                        tab[0:n, 0:PITCH].unsqueeze(1).to_broadcast([n, COPIES, PITCH])), c, 16))

    def toeplitz(dst, row, n, c, t):
        wait(POOL, t)
        for p in range(0, P, COPIES):
            t = inc(POOL.dma_start(dst[p:p + COPIES, :, :],
                                   bass.AP(tab_dram.tensor, row * COPIES * PITCH + P - 1 - p,
                                           [[PITCH - 1, COPIES], [COPIES * PITCH, n], [1, 256]])), c, 16)
        return t

    sp_ = small("sp_", [16])
    ap_ = vec[:, VCOL["rec_a_param"]:VCOL["rec_a_param"] + 8]
    z8 = tmp[3]
    t = act(z8[:, 0:8], ap_, ACT.Abs)
    t1 = dve(DVE.tensor_scalar, z8[:, 8:16], ap_, -1.0, 0.0, ALU.mult, ALU.max)
    t = act(z8[:, 16:24], z8[:, 0:8], ACT.Exp, scale=-1.0, after=[t])
    t = act(z8[:, 24:32], z8[:, 16:24], ACT.Ln, bias=1.0, after=[t])
    t = dve(DVE.tensor_tensor, z8[:, 32:40], z8[:, 8:16], z8[:, 24:32], ALU.add, after=[t, t1])
    t = dve(DVE.tensor_scalar, sp_[:, 0:8], z8[:, 32:40], 8.0, None, ALU.mult, after=[t])
    t_sp = dve(DVE.tensor_scalar, sp_[:, 8:16], z8[:, 32:40], -8.0, None, ALU.mult)
    ahead(4)
    toks("wv", 0, x, (4, 5), to_v, ready)
    T = place("T", o_slot[8], [16, 256])
    mg = place("mg", o_slot[13], [NC, S])
    m_ready = norm(mem, "g_mem_2", 0, (mh, ml), mg, ready=[t_mem] * NC, preload=False,
                   hooks=[lambda: toks("wv", 1, x, (0, 1), to_v), lambda: (toks("wv", 2, x, (4, 5), to_v), flush())])
    wait(POOL, t_tab[1], toeplitz(T[:, :, :], 0, 16, c_toep, t_tab[0]))
    t_T = inc(POOL.memset(T[0:64, :, 192:256], NEG), c_pool)
    gw = slot("gw", 14, [2, NC, P])
    toks("wv", 3, x, (0, 1), to_v)
    cols("wk", 0, x, (4, 5), to_k)
    cols("wq", 0, x, (0, 1), to_q)
    wait(PE, free[4], free[0], (c_dve, c_dve.n))

    def pipeline(n_heads, start, middle, end, fills):
        st1, st2 = {}, {}
        for i in range(n_heads + 2):
            if i in fills:
                fills[i]()
            if i < n_heads:
                st1[i] = start(i)
            if 2 <= i:
                end(i - 2, st2[i - 2])
            if 1 <= i <= n_heads:
                st2[i - 1] = middle(i - 1, st1[i - 1])

    o_tok = {}

    def a_start(i):
        j, r = i // 2, (i % 2) * 64
        wait(PE, q_tok[j])
        t = scores(q[r:r + 64, j, :], k[r:r + 64, j, :], 4)
        return soft(t, 4, T[:, i, :], None, t_T)

    def a_middle(i, s):
        return s[0], turn(s[0], s[1], 5, CAUSAL, 384)

    def a_end(i, s):
        r = (i % 2) * 64
        if i % 2 == 0:
            wait(PE, free[7])
        t = weigh(s[0], s[1], bank[7][r:r + 64, 0:S], v, i * 64, i * 64 + 64)
        if i % 2:
            j = i // 2
            t1 = act(oh[:, j, :], bank[7][:, 0:S], ACT.Copy, after=[t])
            o_tok[j] = dve(DVE.tensor_tensor, ol[:, j, :], bank[7][:, 0:S], oh[:, j, :].bitcast(F32), ALU.subtract, after=[t1])
            free[7] = o_tok[j]

    def wo_part(i, part=None, done=None):
        return rows("wo", i, 4, oh[:, 2 * i:2 * i + 2, :], ol[:, 2 * i:2 * i + 2, :], part, done,
                    (o_tok[2 * i], o_tok[2 * i + 1]))

    steps = []
    for i in range(1, 4):
        steps += in_steps("wk", i, x, (6, 3), to_k) + in_steps("wq", i, x, (6, 3), to_q)
    for i in range(3):
        steps += [lambda i=i: wo_part(i, 0), lambda i=i: wo_part(i, 1)]
    pipeline(16, a_start, a_middle, a_end, dict(enumerate(steps)))
    done = wo_part(3)
    t_gw = inc(POOL.dma_start(gw[:, :, :, :], A["gatew"]), c_gw, 16)

    mk, mv = slot("mk", 3), slot("mv", 4, [2, D])
    mk_tok, mv_tok = {}, {}
    wait(PE, m_ready[7])

    def mem_fill(name, i, banks=(7, 0)):
        def evac(j, ps, t):
            if name == "mk":
                mk_tok[i] = act(mk[:, 2 * i + j, :], ps, ACT.Copy, after=[t])
                return mk_tok[i]
            mv_tok[i] = act(mv[:, j, i * 256:(i + 1) * 256], ps, ACT.Copy, after=[t])
            return mv_tok[i]

        return halves(name, i, (mh, ml), banks, name == "mv"), banks, evac

    zf = [slot(f"zf{i}", 5, [S], off=1024 * i) for i in range(4)]
    zr = [slot(f"zr{i}", 6, [S], off=1024 * i) for i in range(4)]
    zh = [slot(f"zh{i}", 7, [2, S], F32R, off=2048 * i) for i in range(3)]
    zl = [slot(f"zl{i}", 10, [2, S], F32R, off=2048 * i) for i in range(3)]

    def mlp(layer, done, bias, fill):
        ready, finish = norm_late(h, "norm_mlp", 8 * layer, x, hg, (done, bias), fill)
        z_tok, z_free, t_r = {}, {}, []

        def to_z(n, ps, t):
            i, j = n // 2, n % 2
            t0 = act(zr[n % 4][:, :], ps, ACT.Relu, after=[t, z_tok.get(i - 2)])
            if n == 1:
                t_r.append(finish())
            late.append((n, t0))
            return t0

        late = []

        def scaled(n, t):
            i, j = n // 2, n % 2
            t1 = dve(DVE.tensor_tensor, zr[n % 4][:, :], zr[n % 4][:, :], rstd[:, :], ALU.mult, after=[t, *t_r])
            t2 = act(zh[i % 3][:, j, :], zr[n % 4][:, :], ACT.Square, after=[t1, z_free.get(i - 3)])
            t3 = dve(DVE.tensor_tensor, zf[n % 4][:, :], zr[n % 4][:, :], zr[n % 4][:, :], ALU.mult, after=[t1])
            z_tok[i] = dve(DVE.tensor_tensor, zl[i % 3][:, j, :], zf[n % 4][:, :], zh[i % 3][:, j, :].bitcast(F32),
                           ALU.subtract, after=[t2, t3, z_free.get(i - 3)])

        def down(i):
            wait(PE, z_tok[i])
            d = rows(f"w2_{layer}", i, 16, zh[i % 3], zl[i % 3])
            z_free[i] = w_tok[used[0] - 1]
            return d

        for i in range(17):
            if i < 16:
                cols(f"w1_{layer}", i, x, (4, 5), to_z, ready if i == 0 else None)
                while late:
                    scaled(*late.pop(0))
            if i > 0:
                d = down(i - 1)
        return d

    done = mlp(0, done, None, mem_fill("mk", 0, (7, 6)))

    ready = norm(h, "norm_mix", 8, x, hg, add=(done, None), fill=mem_fill("mk", 1))
    XW = S + 3
    xbr = place("xbr", o_slot[5], [NC, XW])
    xc, rg, ig, tt, yb = slot("xc", 7), slot("rg", 8), slot("ig", 9), slot("tt", 10), slot("yb", 11)
    gh, gl = slot("gh", 5, dt=F32R), slot("gl", 8, dt=F32R)
    t_pad = dve(DVE.memset, xbr[:, :, 0:3], 0.0)
    xc_tok = {}
    g_tok = {}
    t_t, t_a, t_m, t_gi, t_s, gh_tok = {}, {}, {}, {}, {}, {}

    y_tok = {}

    def to_y(n, ps, t):
        n -= 8
        bias = gain("rec_b_in", 8 + n)
        if n < 4:
            y_tok[n] = dve(DVE.tensor_scalar, yb[:, n, :], ps, bias, None, ALU.add, after=[t])
        else:
            y_tok[n] = act(yb[:, n, :], ps, ACT.Gelu_apprx_tanh, bias=bias, after=[t, t_m[7]])
        return y_tok[n]

    def to_x(n, ps, t):
        t1 = act(xbr[:, n, 3:XW], ps, ACT.Identity, bias=gain("rec_b_in", n), after=[t])
        t = dve(DVE.tensor_scalar, xc[:, n, :], xbr[:, n, 0:S], gain("rec_conv_w", n), gain("rec_conv_b", n),
                ALU.mult, ALU.add, after=[t1, t_pad])
        for w in range(1, 4):
            t = dve(DVE.scalar_tensor_tensor, out=xc[:, n, :], in0=xbr[:, n, w:w + S], scalar=gain("rec_conv_w", 8 * w + n),
                    in1=xc[:, n, :], op0=ALU.mult, op1=ALU.add, after=[t])
        xc_tok[n] = t
        return t1

    def gates(n):
        wait(PE, xc_tok[n], t_gw)
        for m, (dst, name, b) in enumerate([(rg, "rec_b_ga", 6 * (1 - n % 2)), (ig, "rec_b_gx", 7 - 6 * (n % 2))]):
            wait(PE, free[b])
            t = last_pe(PE.matmul(bank[b][:, 0:S], gw[:, m, n, :], xc[:, n, :], start=True, stop=True))
            free[b] = act(dst[:, n, :], bank[b][:, 0:S], ACT.Sigmoid, bias=gain(name, n), after=[t])
            g_tok[n, m] = free[b]
        t_t[n] = act(tt[:, n, :], rg[:, n, :], ACT.Tanh, scale=sp_[:, n:n + 1], after=[t_sp, g_tok[n, 0]])
        t_gi[n] = pool(POOL.tensor_tensor, ig[:, n, :], ig[:, n, :], xc[:, n, :], ALU.mult, after=[g_tok[n, 1], xc_tok[n]])

    sqs = [place("sqs", o_tmp, [4, S]), yb[:, 4:8, :]]

    def decays():
        for n in range(NC):
            t_a[n] = act(rg[:, n, :], rg[:, n, :], ACT.Exp, scale=sp_[:, 8 + n:9 + n], after=[t_t[n]])
            t_m[n] = pool(POOL.tensor_tensor, sqs[n // 4][:, n % 4, :], rg[:, n, :], rg[:, n, :], ALU.mult, after=[t_a[n]])

    def masses():
        for n in range(0, NC, 2):
            t_m[n + 1] = dve(DVE.scalar_tensor_tensor, out=tt[:, n:n + 2, :], in0=sqs[n // 4][:, n % 4:n % 4 + 2, :], scalar=1.0,
                             in1=tt[:, n:n + 2, :], op0=ALU.add, op1=ALU.mult, after=[t_m[n + 1]])

    def roots():
        for n in range(0, NC, 2):
            t = act(tt[:, n:n + 2, :], tt[:, n:n + 2, :], ACT.Sqrt, after=[t_m[n + 1]])
            for m in (n, n + 1):
                t_s[m] = pool(POOL.tensor_tensor, ig[:, m, :], tt[:, m, :], ig[:, m, :], ALU.mult, after=[t, t_gi[m]])

    def recur(n0):
        for n in (n0, n0 + 1):
            t = dve(DVE.tensor_tensor_scan, tt[:, n, :], rg[:, n, :], ig[:, n, :], 0.0, ALU.mult, ALU.add, after=[t_s[n]])
            t = dve(DVE.tensor_tensor, tt[:, n, :], tt[:, n, :], yb[:, n, :], ALU.mult, after=[t, y_tok[n]])
            gh_tok[n] = (act(gh[:, n, :], tt[:, n, :], ACT.Copy, after=[t]),)
        for n in (n0, n0 + 1):
            gh_tok[n] = dve(DVE.tensor_tensor, gl[:, n, :], tt[:, n, :], gh[:, n, :].bitcast(F32), ALU.subtract,
                            after=gh_tok[n])

    def rin(i, evac):
        cols("rin", i, x, (4, 5) if i % 2 else (2, 3), evac, ready if i == 0 else None)

    for i in range(4):
        rin(i, to_x)
        if i:
            gates(2 * i - 2)
            gates(2 * i - 1)
    rin(4, to_y)
    gates(6)
    gates(7)
    advance()
    decays()
    rin(5, to_y)
    masses()
    advance()
    roots()
    y_tok[0] = y_tok[1] = y_tok[2] = y_tok[3] = act(yb[:, 0:4, :], yb[:, 0:4, :], ACT.Gelu_apprx_tanh, after=[y_tok[3]])
    rin(6, to_y)
    recur(0)
    rin(7, to_y)
    recur(2)
    fill, banks, evac = mem_fill("mk", 2, (6, 7))
    advance()
    free[6] = evac(0, bank[6][:, 0:S], fill(0))
    recur(4)
    free[7] = evac(1, bank[7][:, 0:S], fill(1))
    flush()
    recur(6)
    for i in range(4):
        done = rows("rout", i, 4, gh[:, 2 * i:2 * i + 2, :], gl[:, 2 * i:2 * i + 2, :],
                    ready=(gh_tok[2 * i], gh_tok[2 * i + 1]))

    done = mlp(1, done, "rec_b_o", mem_fill("mk", 3, (7, 6)))

    half, (b0, b1), evac = mem_fill("mv", 0)
    f0 = half(0)
    logs()
    t_r, t_src = mean_square(h, (done, None))
    t_g = gained(h, "norm_final", 0, hg, t_src)
    f1 = half(1)
    t_res = {}
    flush()
    for a, b in GROUPS:
        t = dve(DVE.tensor_tensor, h[:, a:b, :], hg[:, a:b, :], rstd[:, :].unsqueeze(1).to_broadcast([P, b - a, S]), ALU.mult,
                after=[t_r, *t_g[a:b]])
        for j in range(a, b):
            t_res[j] = t
    free[b0] = evac(0, bank[b0][:, 0:S], f0)
    free[b1] = evac(1, bank[b1][:, 0:S], f1)
    ready = norm(h, "g_pre_2", 0, x, hg, ready=t_res, fill=mem_fill("mv", 1), preload=False)

    merged = slot("merged", 5)
    ik, low = slot("ik", 5, [S]), slot("low", 5, [S], off=1024)
    sc, wk_, cm = [slot(f"sc{n}", 5, [384], off=2048 + 1536 * n) for n in range(3)]
    rl = [slot(f"rl{n}", 10, [384], off=1536 * n) for n in range(2)]
    iw, mx8 = slot("iw", 10, [2, 32], off=3072), slot("mx8", 10, [2, 8], off=3328)
    up = slot("up", 10, [512], off=4096)
    dq = slot("dq", 6)
    iq = slot("iq", 7, [4, S])
    dk = slot("dk", 7, [2, S], off=4096)
    dv = slot("dv", 7, [2, S], off=6144)
    sz = slot("sz", 8)
    T2 = slot("T2", 9, [8, 256])
    yh, yl = slot("yh", 10, dt=F32R), slot("yl", 11, dt=F32R)
    gq, gk = slot("gq", 12, [4, S]), slot("gk", 12, [4, S], off=4096)
    gv = slot("gv", 13, [2, D])
    gb, kd = slot("gb", 14, [4, S]), slot("kd", 14, [4, S], off=4096)

    wait(ACTE, ready[0])
    t_late = inc(ACTE.dma_start(cm[:, :], A["cm"]), c_late, 16)
    t_late = inc(ACTE.dma_start(up[0:16, :], A["w_gla_a_up_2"][0]), c_late, 16)

    tok = {}

    def keep(name, dst, scale=1.0, base=0):
        def evac(n, ps, t):
            tok[name, n] = act(dst[:, n - base, :], ps, ACT.Copy, scale=scale, after=[t])
            return tok[name, n]
        return evac

    def keep_tokens(name, dst):
        def evac(i, j, ps, t):
            tok[name, i, j] = act(dst[:, j, i * 256:(i + 1) * 256], ps, ACT.Copy, after=[t])
            return tok[name, i, j]
        return evac

    cols("iq", 0, x, (4, 5), keep("iq", iq), ready)
    tile = take("misc", 0)
    wait(PE, free[0])
    for k_ in range(NC):
        m = block(tile, x, 0, 0, False, k_)
    t = give(m)
    act(ik[0:64, :], bank[0][0:64, 0:S], ACT.Copy, after=[t])
    tok["misc", 0] = act(ik[64:128, :], bank[0][0:64, 0:S], ACT.Copy)
    tok["misc", 1] = free[0] = act(low[0:32, :], bank[0][64:96, 0:S], ACT.Copy)
    t_T2 = toeplitz(T2[:, :, :], 16, 8, c_toep2, t_tab[1])
    cols("iq", 1, x, (4, 5), keep("iq", iq))
    wait(PE, tok["misc", 1], free[6])
    for j in range(2):
        m = PE.transpose(bank[6][:, 32 * j:32 * j + 32], low[0:32, j * P:(j + 1) * P], ident[0:32, 0:32])
    t = last_pe(m)
    t_iw = dve(DVE.tensor_scalar, iw[:, :, :].rearrange("p a b -> p (a b)"), bank[6][:, 0:64], 8 ** -0.5, 64 ** -0.5,
               ALU.mult, ALU.mult, after=[t])
    free[6] = t_iw

    score = {"t": None}
    rl_free = [None, None]

    def index_head(i):
        r = (i % 2) * 64
        b = 6 + i % 2
        wait(PE, tok["iq", i // 2], tok["misc", 0], free[b])
        PE.matmul(bank[b][:, 0:256], iq[r:r + 64, i // 2, P:S], ik[r:r + 64, :], start=True, stop=True)
        t = last_pe(PE.matmul(bank[b][:, 256:384], iq[r:r + 64, i // 2, 0:P], ik[r:r + 64, 0:P], start=True, stop=True,
                              skip_group_check=True))
        t = act(rl[i % 2][:, :], bank[b][:, 0:384], ACT.Relu, after=[t, rl_free[i % 2]])
        free[b] = t
        ts = []
        for j, (a, e) in ((1, TT[0]), (0, TT[1])):
            w = iw[:, j, 16 + i:17 + i]
            if i == 0:
                ts.append(dve(DVE.tensor_scalar, sc[:, a:e], rl[0][:, a:e], w, None, ALU.mult, after=[t, t_iw]))
            else:
                ts.append(dve(DVE.scalar_tensor_tensor, out=sc[:, a:e], in0=rl[i % 2][:, a:e], scalar=w, in1=sc[:, a:e],
                              op0=ALU.mult, op1=ALU.add, after=[t, score["t"]]))
        score["t"] = rl_free[i % 2] = ts[-1]

    def top8(r):
        t = score["t"]
        src = sc if r == 0 else wk_
        ts = [dve(DVE.max, mx8[:, j, :], src[:, a:e], after=[t]) for j, (a, e) in enumerate(TT)]
        for j, (a, e) in enumerate(TT):
            t = dve(DVE.match_replace, wk_[:, a:e], mx8[:, j, :], src[:, a:e], TAKEN, after=[ts[j]])
        score["t"] = t

    for i in range(4):
        index_head(i)
    cols("dk", 0, x, (4, 5), keep("dk", dk))
    for i in range(4, 8):
        index_head(i)
    score["t"] = dve(DVE.tensor_tensor, sc[:, :], sc[:, :], cm[:, :], ALU.add, after=[score["t"], t_late])
    toks("dv", 0, x, (4, 5), keep_tokens("dv", dv))
    top8(0)
    for i in range(4):
        cols("dq", i, x, (4, 5), keep("dq", dq, scale=128 ** -0.5))
        top8(1 + i)
    for i in (2, 3):
        m2 = mem_fill("mv", i)
        toks("mv", i, (mh, ml), (4, 5), lambda i_, j, ps, t: m2[2](j, ps, t))
        top8(3 + i)
    for i in range(2):
        cols("gq", i, x, (4, 5), keep("gq", gq))
        if i == 0:
            top8(7)
    mask = sc
    t = dve(DVE.tensor_scalar, sc[:, :], wk_[:, :], -3.2e38, NEG, ALU.is_gt, ALU.mult, after=[score["t"]])
    t_mask = dve(DVE.tensor_tensor, sc[:, :], sc[:, :], cm[:, :], ALU.min, after=[t])

    wait(PE, t_late)
    g_t, e_t = {}, {}

    def decay_sum(n):
        b = 6 + n % 2
        u, w = tmp[n % 2], tmp[2 + n % 2]
        wait(PE, free[b])
        t = last_pe(PE.matmul(bank[b][:, 0:S], up[0:16, n * P:(n + 1) * P], low[0:16, :], start=True, stop=True))
        t = act(u[:, :], bank[b][:, 0:S], ACT.Identity, bias=gain("b_gla_a_2", n), after=[t, e_t.get(n - 2)])
        free[b] = t
        t = act(w[:, :], u[:, :], ACT.Abs, after=[t])
        t = act(w[:, :], w[:, :], ACT.Exp, scale=-1.0, after=[t])
        t = act(w[:, :], w[:, :], ACT.Ln, bias=1.0, after=[t])
        t = dve(DVE.scalar_tensor_tensor, out=u[:, :], in0=u[:, :], scalar=0.0, in1=w[:, :], op0=ALU.min, op1=ALU.subtract,
                after=[t])
        g_t[n] = dve(DVE.tensor_tensor_scan, gb[:, n, :], reset[:, :], u[:, :], 0.0, ALU.mult, ALU.add, after=[t])

    def decayed(n):
        ep, en = tmp[n % 2], tmp[2 + n % 2]
        t = act(ep[:, :], gb[:, n, :], ACT.Exp, scale=1.0 / 16, after=[g_t[n]])
        t1 = act(en[:, :], gb[:, n, :], ACT.Exp, scale=-1.0 / 16)
        t2 = dve(DVE.tensor_copy, dec[:, n, :], ep[:, 63:S:64], after=[t])
        dve(DVE.scalar_tensor_tensor, out=gq[:, n, :], in0=gq[:, n, :], scalar=128 ** -0.5, in1=ep[:, :], op0=ALU.mult,
            op1=ALU.mult, after=[tok["gq", n]])
        t = dve(DVE.tensor_tensor, kd[:, n, :], gk[:, n, :], en[:, :], ALU.mult, after=[t1, tok["gk", n]])
        e_t[n] = dve(DVE.tensor_tensor, gk[:, n, :].rearrange("p (c t) -> p c t", c=4),
                     kd[:, n, :].rearrange("p (c t) -> p c t", c=4), dec[:, n, :].unsqueeze(2).to_broadcast([P, 4, 64]),
                     ALU.mult, after=[t, t2])

    cols("gk", 0, x, (4, 5), keep("gk", gk))
    logs()
    cols("gk", 1, x, (0, 1), keep("gk", gk))
    decay_sum(0)
    for i in range(3):
        toks("gv", i, x, (0, 1) if i % 2 else (4, 5), keep_tokens("gv", gv))
        decay_sum(i + 1)
        decayed(i)

    def to_sz(name):
        def evac(n, ps, t):
            tok[name, n] = act(sz[:, n, :], ps, ACT.Silu, after=[t, tok.get(("sz free", n))])
            return tok[name, n]
        return evac

    advance()
    decayed(3)
    for i in range(4):
        cols("dz", i, x, (4, 5) if i % 2 else (0, 1), to_sz("dz"))

    xq = slot("xq", 6)

    def d_start(i):
        wait(PE, tok["dq", i], tok["dk", i // 4])
        return soft(scores(dq[:, i, :], dk[:, i // 4, :], 4), 4, T2[:, i, :], mask, t_T2)

    y = {}

    def d_low(i):
        y["d", i] = dve(DVE.tensor_tensor, yl[:, i, :], tmp[i % 2][:, :], yh[:, i, :].bitcast(F32), ALU.subtract,
                        after=[y["dh", i]])

    def d_end(i, s):
        wait(PE, free[7])
        c = (i // 4) * 128
        t = weigh(s[0], s[1], bank[7][:, 0:S], dv, c, c + 128)
        o = tmp[i % 2]
        if i:
            d_low(i - 1)
        t = dve(DVE.tensor_tensor, o[:, :], bank[7][:, 0:S], sz[:, i, :], ALU.mult, after=[t, tok["dz", i], y.get(("d", i - 2))])
        free[7] = tok["sz free", i] = t
        y["dh", i] = act(yh[:, i, :], o[:, :], ACT.Copy, after=[t])

    wait(POOL, t_mask, e_t[3])
    wait(PE, tok["dv", 0, 0], tok["dv", 0, 1])
    logs()
    steps = in_steps("gv", 3, x, (6, 3), keep_tokens("gv", gv), True)
    for i in range(4):
        steps += in_steps("xq", i, x, (6, 3), keep("xq", xq, scale=1.0 / 16))
    pipeline(8, d_start, a_middle, d_end, dict(enumerate(steps)))
    d_low(7)
    for i in range(4):
        cols("gz", i, x, (4, 5), to_sz("gz"))

    og = slot("og", 7)
    at = [slot(f"at{i}", 9, [2, P], off=1024 * i) for i in range(2)]
    ktT = [slot(f"ktT{i}", 9, [2, P], off=2048 + 1024 * i) for i in range(2)]
    st = [slot(f"st{i}", 9, [256], off=4096 + 1024 * i) for i in range(3)]
    gms = slot("gms", 14, [4, S])
    gdone, g_head, ms_t = {}, {}, {}

    def g_first(n):
        A_, K_ = at[n % 2], ktT[n % 2]
        wait(PE, e_t[n], free[0])
        for j in range(2):
            m = PE.matmul(bank[0][:, j * P:(j + 1) * P], kd[:, n, j * P:(j + 1) * P], gq[:, n, j * P:(j + 1) * P],
                          start=True, stop=True, skip_group_check=True)
        t = last_pe(m)
        t_at = dve(DVE.tensor_tensor, A_[:, :, :], bank[0][:, 0:S].rearrange("p (a b) -> p a b", a=2),
                   gmask[:, :].unsqueeze(1).to_broadcast([P, 2, P]), ALU.mult, after=[t, gdone.get(n - 2)])
        free[0] = t_at
        wait(PE, free[1])
        for j in range(2):
            m = PE.transpose(bank[1][:, j * P:(j + 1) * P], gk[:, n, j * P:(j + 1) * P], ident[:, :])
        t = last_pe(m)
        t_k = act(K_[:, :, :], bank[1][:, 0:S].rearrange("p (a b) -> p a b", a=2), ACT.Copy, after=[t, gdone.get(n - 2)])
        free[1] = t_k
        g_head[n] = (t_at, t_k)

    def g_states(n):
        K_ = ktT[n % 2]
        wait(PE, g_head[n][1], free[2], free[3])
        for c in range(3):
            r, j = (c % 2) * 64, c // 2
            m = PE.matmul(bank[2 + c % 2][:, j * 256:j * 256 + 256], K_[r:r + 64, j, :],
                          gv[r:r + 64, j, n * 256:(n + 1) * 256], start=True, stop=True, skip_group_check=True)
        t_u = last_pe(m)
        t = dve(DVE.tensor_copy, st[0][:, :], bank[2][:, 0:256], after=[t_u, gdone.get(n - 1)])
        t = dve(DVE.scalar_tensor_tensor, out=st[1][:, :], in0=st[0][:, :], scalar=dec[:, n, 1:2], in1=bank[3][:, 0:256],
                op0=ALU.mult, op1=ALU.add, after=[t])
        free[3] = t
        t = dve(DVE.scalar_tensor_tensor, out=st[2][:, :], in0=st[1][:, :], scalar=dec[:, n, 2:3], in1=bank[2][:, 256:512],
                op0=ALU.mult, op1=ALU.add, after=[t])
        free[2] = t
        g_head[n] += (t,)

    def g_second(n):
        A_ = at[n % 2]
        t_at, _, t_st = g_head[n]
        wait(PE, t_at, t_st)
        ts = []
        for m_ in range(2):
            b = m_
            wait(PE, free[b])
            c0 = n * 256 + m_ * P
            for j in range(2):
                PE.matmul(bank[b][:, j * P:(j + 1) * P], gv[:, j, c0:c0 + P], A_[:, j, :], start=j == 0, stop=False,
                          skip_group_check=True)
            for c in range(1, 4):
                m = PE.matmul(bank[b][:, c * 64:c * 64 + 64], st[c - 1][:, m_ * P:(m_ + 1) * P], gq[:, n, c * 64:c * 64 + 64],
                              start=False, stop=True, skip_group_check=True)
            gdone[n] = last_pe(m)
            free[b] = act(og[:, 2 * n + m_, :], bank[b][:, 0:S], ACT.Copy, after=[gdone[n]])
            ts.append(act(sq[m_][:, :], og[:, 2 * n + m_, :], ACT.Square, after=[free[b], sq_read[m_]]))
        t = pool(POOL.tensor_tensor, sq[2][:, :], sq[0][:, :], sq[1][:, :], ALU.add, after=[*ts, sq_read[2]])
        sq_read[0] = sq_read[1] = t
        return t

    def g_third(n, t):
        wait(PE, t, free[1])
        sq_read[2] = last_pe(PE.matmul(bank[1][:, 0:S], ones[:, :], sq[2][:, :], start=True, stop=True))
        free[1] = ms_t[n] = act(gms[:, n, :], bank[1][:, 0:S], ACT.Copy, after=[sq_read[2]])

    m_tok = {}

    def to_g(n, ps, t):
        tok["g", n] = act(tmp[3 + n % 2][:, :], ps, ACT.Sigmoid, after=[t, m_tok.get(n - 2), m_tok.get(n + 6)])
        return tok["g", n]

    def to_m(first):
        def evac(n, ps, t):
            if first:
                m_tok[n] = dve(DVE.tensor_tensor, merged[:, n, :], ps, tmp[3 + n % 2][:, :], ALU.mult, after=[t, tok["g", n]])
                return m_tok[n]
            t = dve(DVE.tensor_tensor, tmp[n % 2][:, :], ps, tmp[3 + n % 2][:, :], ALU.mult, after=[t, tok["g", n], m_tok.get(n - 2)])
            m_tok[n] = dve(DVE.tensor_tensor, merged[:, n, :], merged[:, n, :], tmp[n % 2][:, :], ALU.add, after=[t])
            return t
        return evac

    Y = (yh, yl)
    wait(PE, y["d", 7], tok["gv", 3, 1])
    for n in range(4):
        g_first(n)
        cols("ta", n, x, (4, 5), to_g)
        if n:
            g_third(n - 1, t_sq)
        g_states(n)
        cols("wd", n, Y, (6, 7), to_m(True))
        t_sq = g_second(n)
    zx = slot("zx", 13)

    def to_zx(n, ps, t):
        tok["zx", n] = dve(DVE.tensor_copy, zx[:, n, :], ps, after=[t, gdone[3]])
        return tok["zx", n]

    dsa_done = w_tok[used[0] - 1]

    cols("xz", 0, x, (4, 5), to_zx)
    g_third(3, t_sq)
    ox = slot("ox", 9)
    xh2, xl2 = slot("xh2", 12, dt=F32R), slot("xl2", 14, dt=F32R)
    logs()
    t_gr = act(gms[:, :, :], gms[:, :, :], ACT.Ln, scale=1.0 / 256, bias=epsc[:, 0:1], after=[ms_t[3]])
    t_gr = act(gms[:, :, :], gms[:, :, :], ACT.Exp, scale=-0.5, after=[t_gr])

    pairs = [place("pair0", o_tmp, [2, S]), place("pair1", o_sq, [2, S])]

    def g_out(i):
        a, b = 2 * i, 2 * i + 2
        pair = pairs[i % 2]
        for j in range(2):
            t = dve(DVE.scalar_tensor_tensor, out=pair[:, j, :], in0=og[:, a + j, :], scalar=gain("g_gla_2", j),
                    in1=gms[:, i, :], op0=ALU.mult, op1=ALU.mult, after=[t_gr, y.get(("g", a - 3)), sq_read[0]])
        t = dve(DVE.tensor_tensor, pair[:, :, :], pair[:, :, :], sz[:, a:b, :], ALU.mult, after=[t, tok["gz", a + 1]])
        y["gh", i] = act(yh[:, a:b, :], pair[:, :, :], ACT.Copy, after=[t, dsa_done])

    def g_low(i):
        y["g", 2 * i + 1] = dve(DVE.tensor_tensor, yl[:, 2 * i:2 * i + 2, :], pairs[i % 2][:, :, :],
                                yh[:, 2 * i:2 * i + 2, :].bitcast(F32), ALU.subtract, after=[y["gh", i], dsa_done])

    def x_start(i):
        wait(PE, free[4], tok["xq", 2 * i + 1])
        for j, c in ((1, 0), (0, 256)):
            for k_ in range(2):
                m = PE.matmul(bank[4][:, c:c + 256], xq[:, 2 * i + k_, j * P:(j + 1) * P], mk[:, 2 * i + k_, :],
                              start=k_ == 0, stop=k_ == 1, skip_group_check=True)
        t = last_pe(m)
        n = head_n[0]
        head_n[0] += 1
        Lb, s_ = L[n % 2], stat[:, n % 16, :]
        t = dve(DVE.tensor_scalar, Lb[:, :], bank[4][:, :], -1.0, None, ALU.mult, after=[t, L_free[n % 2]])
        free[4] = t
        t = dve(DVE.tensor_reduce, s_[:, 0:2], Lb[:, :].rearrange("p (a b) -> p a b", a=2), AX, ALU.min, after=[t])
        return n, softmax_tail(Lb, [(0, 256), (256, 512)], None, t, None, s_)

    def x_middle(i, s):
        t = turn(s[0], s[1], 5, [(256, 0), (0, 128), (384, 256), (128, 384)], 512)
        if i:
            g_low(i - 1)
        g_out(i)
        return s[0], t

    def x_end(i, s):
        n, t_t = s
        wait(PE, t_t)
        for m_ in range(2):
            b = 6 + m_
            wait(PE, free[b])
            c = i * 256 + m_ * P
            PE.matmul(bank[b][:, 0:S], mv[:, 0, c:c + P], PT[n % 2][:, 0:256], start=True, stop=False)
            t = last_pe(PE.matmul(bank[b][:, 0:S], mv[:, 1, c:c + P], PT[n % 2][:, 256:512], start=False, stop=True))
            PT_free[n % 2] = t
            free[b] = y["x", 2 * i + m_] = act(ox[:, 2 * i + m_, :], bank[b][:, 0:S], ACT.Copy, after=[t])

    wait(PE, mk_tok[3], mv_tok[3])
    wait(DVE, gdone[3])
    steps = []
    for i in range(1, 4):
        steps += in_steps("xz", i, x, (2, 3), to_zx)

    def to_g_later(n, ps, t):
        return act(tmp[3 + n % 2][:, :], ps, ACT.Copy, after=[t, m_tok.get(n + 6)])

    steps += in_steps("tg", 0, x, (2, 3), to_g_later)
    steps[2:4] = [lambda f=steps[2], g=steps[3]: (f(), g())]
    steps[3:5] = [lambda f=steps[3], g=steps[4]: (f(), g())]
    pipeline(4, x_start, x_middle, x_end, dict(enumerate(steps)))
    g_low(3)
    t_zx = act(zx[:, :, :], zx[:, :, :], ACT.Silu, after=[tok["zx", 7], y["x", 7]])

    def x_out(a):
        b = a + 2
        t = dve(DVE.tensor_tensor, ox[:, a:b, :], ox[:, a:b, :], zx[:, a:b, :], ALU.mult, after=[t_zx, y["x", 7]])
        t1 = act(xh2[:, a:b, :], ox[:, a:b, :], ACT.Copy, after=[t])
        y["x2"] = dve(DVE.tensor_tensor, xl2[:, a:b, :], ox[:, a:b, :], xh2[:, a:b, :].bitcast(F32), ALU.subtract,
                      after=[t1, y["g", 7]])

    for n in range(2):
        tok["g", n] = act(tmp[3 + n][:, :], tmp[3 + n][:, :], ACT.Sigmoid)
    for n in range(4):
        if n:
            cols("tg", n, x, (4, 5), to_g)
        wait(PE, y["g", 7])
        cols("wg", n, Y, (6, 7), to_m(False))
        x_out(2 * n)

    fh, fl = slot("fh", 6, dt=F32R), slot("fl", 7, dt=F32R)
    f_tok = {}

    def last_in(n):
        t1 = act(fh[:, n, :], merged[:, n, :], ACT.Copy, after=[m_tok[n]])
        f_tok[n] = dve(DVE.tensor_tensor, fl[:, n, :], merged[:, n, :], fh[:, n, :].bitcast(F32), ALU.subtract, after=[t1])

    def to_last(n, ps, t):
        t = to_m(False)(n, ps, t)
        last_in(n)
        return t

    def last_rows(i):
        return rows("wf", i, 4, fh[:, 2 * i:2 * i + 2, :], fl[:, 2 * i:2 * i + 2, :],
                    ready=(f_tok[2 * i], f_tok[2 * i + 1]))

    for n in range(4):
        cols("tx", n, x, (4, 5), to_g)
        if n:
            last_rows(n - 1)
        wait(PE, y["x2"])
        cols("wx", n, (xh2, xl2), (6, 7), to_last)
    done = last_rows(3)
    res = slot("res", 9)
    part = [bank[j // 2][:, (j % 2) * S:(j % 2 + 1) * S] for j in range(NC)]
    ts, t_g, t_acc, ALONE = [], [], None, 3
    slot_of = [0] + [1 + j % 3 for j in range(NC - 1)]
    logs()
    for j in range(NC):
        ts.append(act(sq[slot_of[j]][:, :], part[j], ACT.Square, after=[done[j // 2], sq_read[slot_of[j]]]))
        if j % 2:
            t_g += [dve(DVE.tensor_scalar, res[:, i, :], part[i], gain("g_post_2", i), None, ALU.mult, after=[ts[j]])
                    for i in (j - 1, j)]
        if 0 < j < ALONE:
            t_acc = sq_read[slot_of[j]] = pool(POOL.tensor_tensor, sq[0][:, :], sq[0][:, :], sq[slot_of[j]][:, :], ALU.add,
                                               after=[t_acc, ts[j]])
        if j < ALONE:
            t_acc = t_acc or ts[0]
            continue
        wait(PE, free[6] if j == ALONE else None, ts[j])
        sq_read[slot_of[j]] = last_pe(PE.matmul(bank[6][:, 0:S], ones[:, :], sq[slot_of[j]][:, :], start=j == ALONE,
                                                stop=j == NC - 1))
        if j == NC - 3:
            wait(PE, t_acc)
            PE.matmul(bank[6][:, 0:S], ones[:, :], sq[0][:, :], start=False, stop=False)
    t = sq_read[slot_of[NC - 1]]
    t = act(rms_t[:, :], bank[6][:, 0:S], ACT.Ln, scale=1.0 / D, bias=epsc[:, 0:1], after=[t])
    t_r = act(rstd[:, :], rms_t[:, :], ACT.Exp, scale=-0.5, after=[t])
    outT = out.rearrange("(j p) s -> p j s", p=P)
    for a, b, op, eng in ((0, 2, dve, DVE), (6, 7, pool, POOL), (2, 4, dve, DVE), (4, 6, dve, DVE), (7, 8, pool, POOL)):
        t = op(eng.tensor_tensor, res[:, a:b, :], res[:, a:b, :], rstd[:, :].unsqueeze(1).to_broadcast([P, b - a, S]), ALU.mult,
               after=[t_r, *t_g[a:b]])
        t = op(eng.tensor_tensor, res[:, a:b, :], res[:, a:b, :], h[:, a:b, :], ALU.add, after=[t])
        wait(SP, t)
        t_out = inc(SP.dma_start(outT[:, a:b, :], res[:, a:b, :]), c_out, 16)
    assert used[0] == len(PLAN)
    wait(SP, t_out)
    ctx.close()


def bucket(d):
    if d < 16:
        return d
    return min(31, 16 + int(log(d / 16) / log(8) * 16))


def constants():
    f = np.float32
    selA = np.zeros((P, 2, 384), f)
    selB = np.zeros((32, 384), f)
    for i in range(383):
        n = min(max(255 - i, -128), 128) + 128 - 1
        selA[n % P, n // P, i] = 1
        selB[bucket(max(255 - i, 0)), i] = 1
    p, c = np.arange(P)[:, None], np.arange(384)[None, :]
    key = np.where(c < 256, c, c - 256)
    query = np.where(c < 256, p + P, p)
    s, t = np.arange(P)[:, None], np.arange(P)[None, :]
    return {
        "selA": selA, "selB": selB, "ones": np.ones((P, P), f), "ident": np.eye(P, dtype=f), 
        "gmask": ((s <= t) & (s // 64 == t // 64)).astype(f),
        "reset": np.tile((np.arange(S) % 64 != 0).astype(f), (P, 1)),
        "cm": np.where(key > query, f(GONE), f(0)).astype(f),
    }


def by_cols(w):
    return np.ascontiguousarray(w.reshape(NC, P, -1, 256).transpose(2, 1, 0, 3)).reshape(-1, P, TILE)


def by_rows(w):
    return np.ascontiguousarray(w.reshape(-1, 2, P, D).transpose(0, 2, 1, 3)).reshape(-1, P, TILE)


def feature(x):
    return np.ascontiguousarray(x.T.reshape(NC, P, S).transpose(1, 0, 2))


def kernel(**inputs):
    import concourse.bacc as _bacc
    from concourse.bass_utils import run_bass_kernel_spmd as _run

    a = {k: np.asarray(v) for k, v in inputs.items()}
    qkv, win, w1, w2 = a["attn_w_qkv"][0], a["w_in_2"][0], a["mlp_w1"], a["mlp_w2"]
    cuts = np.cumsum([0, 512, 512, 1024, 16, 1024, 1024, 256, 256, 512, 64, 8, 1024, 1024, 1024, 1024, 1024, 1024])
    gq, gk, gv, ga, gz, dq, dk, dv, iq, ik, iw, dz, xq, xz, ta, tg, tx = [win[:, cuts[i]:cuts[i + 1]] for i in range(17)]
    misc = np.concatenate([ik, ga, iw, np.zeros((D, 168), win.dtype)], axis=1)
    arrays = {
        "wv": by_cols(qkv[:, 2 * D:]), "wk": by_cols(qkv[:, D:2 * D]), "wq": by_cols(qkv[:, :D]),
        "wo": by_rows(a["attn_w_o"][0]), "w1_0": by_cols(w1[0]), "w2_0": by_rows(w2[0]), "w1_1": by_cols(w1[1]),
        "w2_1": by_rows(w2[1]), "rin": by_cols(a["rec_w_in"][0]), "rout": by_rows(a["rec_w_o"][0]),
        "misc": by_cols(misc), "iq": by_cols(iq), "dk": by_cols(dk), "dv": by_cols(dv), "dq": by_cols(dq),
        "gq": by_cols(gq), "gk": by_cols(gk), "gv": by_cols(gv), "dz": by_cols(dz), "ta": by_cols(tg), "wd": by_cols(a["w_dsa_out_2"][0]),
        "xq": by_cols(xq), "gz": by_cols(gz), "tg": by_cols(ta), "wg": by_cols(a["w_gla_out_2"][0]),
        "mk": by_cols(a["w_mem_kv_2"][0][:, :D]), "mv": by_cols(a["w_mem_kv_2"][0][:, D:]), "xz": by_cols(xz),
        "tx": by_cols(tx), "wx": by_cols(a["w_x_out_2"][0]), "wf": by_rows(a["w_o_2"][0]),
        "xT": feature(a["x"][0]), "memT": feature(a["mem_2"][0]),
        "gatew": np.ascontiguousarray(np.stack([a["rec_w_ga"][0], a["rec_w_gx"][0]]).transpose(2, 0, 1, 3)),
        "vec": np.ascontiguousarray(np.concatenate([a[n].reshape(-1, P) for n, _ in VEC]).T),
        "relT": np.ascontiguousarray(a["attn_rel_bias"][0][:, 1:].T.reshape(2, P, 16).transpose(1, 0, 2)),
        "rel_bias_2": a["rel_bias_2"], "w_gla_a_up_2": a["w_gla_a_up_2"], **constants(),
    }
    nc = _bacc.Bacc("TRN2", target_bir_lowering=False, num_devices=1)
    A = {n: nc.dram_tensor(f"in_{n}", v.shape, F32, kind="ExternalInput").ap() for n, v in arrays.items()}
    A["scratch"] = nc.dram_tensor("scratch", (24, COPIES, PITCH), F32).ap()
    out = nc.dram_tensor("out_0", (D, S), F32, kind="ExternalOutput").ap()
    build(nc, A, out)
    r = _run(nc, [{f"in_{n}": v for n, v in arrays.items()}], core_ids=[0])
    return np.ascontiguousarray(r.results[0]["out_0"].T).reshape(1, S, D)
```
